# Optimizing a Trainium2 kernel written in Bass

```python
import math
import jax, jax.numpy as jnp
from jax import lax
import numpy as np

D_MODEL = 1024
BATCH = 1
SEQ = 1024
DEPTH = 1
DEC_BATCH = 1
DEC_SEQ = 64
PAST_LEN = 512

CHUNK = 64
Q_BLOCK = 128
D_LRU = 1024
N_LRU_HEADS = 8
LRU_HEAD = D_LRU // N_LRU_HEADS
CONV_W = 4
LRU_C = 8.0
N_HEADS = 8
N_KV_HEADS = 2
HEAD_DIM = 128
GROUP = N_HEADS // N_KV_HEADS
D_ATT = N_HEADS * HEAD_DIM
KV_DIM = N_KV_HEADS * HEAD_DIM
N_IDX_HEADS = 8
IDX_DIM = 64
TOPK_MAX = 256
D_MIX = D_LRU + D_ATT
IN_SPLITS = (D_LRU, D_LRU, D_ATT, KV_DIM, KV_DIM, D_ATT, N_IDX_HEADS * IDX_DIM, IDX_DIM, N_IDX_HEADS)
IN_OFFSETS = (1024, 2048, 3072, 3328, 3584, 4608, 5120, 5184)
D_IN = 5192
EPS = 1e-6

kernel_name = "hybrid_rglru_dsa_stream_step"

def rms_norm(x, g):
    xf = x.astype(jnp.float32)
    y = xf * lax.rsqrt(jnp.mean(xf * xf, axis=-1, keepdims=True) + EPS)
    return (y * g.astype(jnp.float32)).astype(x.dtype)

def causal_conv(u, buf, w, b):
    T = u.shape[1]
    up = jnp.concatenate([buf.astype(u.dtype), u], axis=1)
    y = b
    for j in range(CONV_W):
        y = y + up[:, j:j + T] * w[j]
    return y, up[:, -(CONV_W - 1):]

def _lru_combine(left, right):
    a1, b1 = left
    a2, b2 = right
    return a1 * a2, a2 * b1 + b2

def rg_lru(u, h0, w_r, b_r, w_i, b_i, lam, reset_first):
    B, T, _ = u.shape
    uf = u.astype(jnp.float32)
    uh = uf.reshape(B, T, N_LRU_HEADS, LRU_HEAD)
    r = jax.nn.sigmoid(jnp.einsum('bthi,hij->bthj', uh, w_r.astype(jnp.float32)) + b_r.astype(jnp.float32)).reshape(B, T, D_LRU)
    gi = jax.nn.sigmoid(jnp.einsum('bthi,hij->bthj', uh, w_i.astype(jnp.float32)) + b_i.astype(jnp.float32)).reshape(B, T, D_LRU)
    log_a = -LRU_C * r * jax.nn.softplus(-lam.astype(jnp.float32))
    a = jnp.exp(log_a)
    mult = jnp.sqrt(-jnp.expm1(2.0 * log_a))
    if reset_first:
        mult = mult.at[:, 0].set(1.0)
    bterm = mult * gi * uf
    a_cum, b_cum = lax.associative_scan(_lru_combine, (a, bterm), axis=1)
    h = b_cum + a_cum * h0.astype(jnp.float32)[:, None]
    return h, h[:, -1]

def dsa_block(q, iq, iw, q_pos, k_all, v_all, ik_all, topk):
    B, Tq = q.shape[0], q.shape[1]
    L = k_all.shape[1]
    neg = jnp.finfo(jnp.float32).min
    key_pos = jnp.arange(L)
    adm = (key_pos[None, :] // CHUNK) <= (q_pos[:, None] // CHUNK)
    s = jnp.einsum('bthd,bsd->bths', iq.astype(jnp.float32), ik_all.astype(jnp.float32))
    score = jnp.einsum('bths,bth->bts', jax.nn.relu(s), iw.astype(jnp.float32))
    score = jnp.where(adm[None], score, neg)
    _, idx = lax.top_k(score, topk)
    valid = (idx // CHUNK) <= (q_pos[None, :, None] // CHUNK)
    kg = jax.vmap(lambda kk, ii: kk[ii])(k_all, idx)
    vg = jax.vmap(lambda vv, ii: vv[ii])(v_all, idx)
    qg = q.reshape(B, Tq, N_KV_HEADS, GROUP, HEAD_DIM).astype(jnp.float32)
    logits = jnp.einsum('bthgd,btkhd->bthgk', qg, kg.astype(jnp.float32)) * (HEAD_DIM ** -0.5)
    logits = jnp.where(valid[:, :, None, None, :], logits, neg)
    p = jax.nn.softmax(logits, axis=-1)
    o = jnp.einsum('bthgk,btkhd->bthgd', p, vg.astype(jnp.float32))
    return o.reshape(B, Tq, D_ATT)

def layer(x, c, conv_buf, h0, k_past, v_past, ik_past, pos0, reset_first,
          w_mod, b_mod, g_norm, w_in, conv_w, conv_b, w_r, b_r, w_i, b_i,
          lru_lambda, g_a, g_b, w_out):
    B, T, _ = x.shape
    dt = x.dtype
    mod = jax.nn.silu(c) @ w_mod + b_mod
    shift, scale, gate = jnp.split(mod, 3, axis=-1)
    hn = rms_norm(x, g_norm) * (1.0 + scale[:, None]) + shift[:, None]
    u = hn @ w_in
    xa, za, q, k, v, zb, iq, ik, iw = jnp.split(u, IN_OFFSETS, axis=-1)
    xa_c, conv_new = causal_conv(xa, conv_buf, conv_w, conv_b)
    h, h_last = rg_lru(xa_c, h0, w_r, b_r, w_i, b_i, lru_lambda, reset_first)
    ya = rms_norm(h.astype(dt), g_a) * jax.nn.silu(za)
    q = q.reshape(B, T, N_HEADS, HEAD_DIM)
    k = k.reshape(B, T, N_KV_HEADS, HEAD_DIM)
    v = v.reshape(B, T, N_KV_HEADS, HEAD_DIM)
    iq = iq.reshape(B, T, N_IDX_HEADS, IDX_DIM)
    iw = iw * ((N_IDX_HEADS * IDX_DIM) ** -0.5)
    k_all = jnp.concatenate([k_past.astype(dt), k], axis=1)
    v_all = jnp.concatenate([v_past.astype(dt), v], axis=1)
    ik_all = jnp.concatenate([ik_past.astype(dt), ik], axis=1)
    L = k_all.shape[1]
    topk = min(TOPK_MAX, L // 4)
    q_pos = pos0 + jnp.arange(T)
    if T >= Q_BLOCK and T % Q_BLOCK == 0:
        nblk = T // Q_BLOCK
        def to_blocks(a):
            return jnp.moveaxis(a.reshape((B, nblk, Q_BLOCK) + a.shape[2:]), 1, 0)
        ob = lax.map(lambda a: dsa_block(a[0], a[1], a[2], a[3], k_all, v_all, ik_all, topk),
                     (to_blocks(q), to_blocks(iq), to_blocks(iw), q_pos.reshape(nblk, Q_BLOCK)))
        ob = jnp.moveaxis(ob, 0, 1).reshape(B, T, D_ATT)
    else:
        ob = dsa_block(q, iq, iw, q_pos, k_all, v_all, ik_all, topk)
    yb = rms_norm(ob.astype(dt), g_b) * jax.nn.silu(zb)
    y = jnp.concatenate([ya, yb], axis=-1) @ w_out
    x_out = x + gate[:, None] * y
    return x_out, k, v, ik, h_last.astype(dt), conv_new

def setup_inputs(seed: int = 0) -> dict:
    key = jax.random.key(seed)
    ks = jax.random.split(key, 24)
    f32 = jnp.float32
    nrm = lambda k, s, sc: jax.random.normal(k, s, f32) * sc
    u = jax.random.uniform(ks[20], (DEPTH, D_LRU), f32, 0.9, 0.999)
    p = u ** (1.0 / LRU_C)
    lru_lambda = jnp.log(p) - jnp.log1p(-p)
    return {
        "x_prompt": nrm(ks[0], (BATCH, SEQ, D_MODEL), 1.0),
        "x_sample": nrm(ks[1], (DEC_BATCH, DEC_SEQ, D_MODEL), 1.0),
        "c_prompt": nrm(ks[2], (BATCH, D_MODEL), 1.0),
        "c_sample": nrm(ks[3], (DEC_BATCH, D_MODEL), 1.0),
        "cache_k": nrm(ks[4], (DEPTH, DEC_BATCH, PAST_LEN, N_KV_HEADS, HEAD_DIM), 1.0),
        "cache_v": nrm(ks[5], (DEPTH, DEC_BATCH, PAST_LEN, N_KV_HEADS, HEAD_DIM), 1.0),
        "cache_idx_k": nrm(ks[6], (DEPTH, DEC_BATCH, PAST_LEN, IDX_DIM), 1.0),
        "state_lru_h": nrm(ks[7], (DEPTH, DEC_BATCH, D_LRU), 0.5),
        "state_conv": nrm(ks[8], (DEPTH, DEC_BATCH, CONV_W - 1, D_LRU), 1.0),
        "w_mod": nrm(ks[9], (DEPTH, D_MODEL, 3 * D_MODEL), 0.5 * D_MODEL ** -0.5),
        "b_mod": nrm(ks[10], (DEPTH, 3 * D_MODEL), 0.02),
        "g_norm": 1.0 + nrm(ks[11], (DEPTH, D_MODEL), 0.02),
        "w_in": nrm(ks[12], (DEPTH, D_MODEL, D_IN), D_MODEL ** -0.5),
        "conv_w": nrm(ks[13], (DEPTH, CONV_W, D_LRU), CONV_W ** -0.5),
        "conv_b": nrm(ks[14], (DEPTH, D_LRU), 0.02),
        "w_r": nrm(ks[15], (DEPTH, N_LRU_HEADS, LRU_HEAD, LRU_HEAD), LRU_HEAD ** -0.5),
        "b_r": nrm(ks[16], (DEPTH, N_LRU_HEADS, LRU_HEAD), 0.02),
        "w_i": nrm(ks[17], (DEPTH, N_LRU_HEADS, LRU_HEAD, LRU_HEAD), LRU_HEAD ** -0.5),
        "b_i": nrm(ks[18], (DEPTH, N_LRU_HEADS, LRU_HEAD), 0.02),
        "lru_lambda": lru_lambda,
        "g_a": 1.0 + nrm(ks[19], (DEPTH, D_LRU), 0.02),
        "g_b": 1.0 + nrm(ks[21], (DEPTH, D_ATT), 0.02),
        "w_out": nrm(ks[22], (DEPTH, D_MIX, D_MODEL), D_MIX ** -0.5),
        "g_final": 1.0 + nrm(ks[23], (D_MODEL,), 0.02),
    }

def reference(x_prompt, x_sample, c_prompt, c_sample, cache_k, cache_v, cache_idx_k,
              state_lru_h, state_conv, w_mod, b_mod, g_norm, w_in, conv_w, conv_b,
              w_r, b_r, w_i, b_i, lru_lambda, g_a, g_b, w_out, g_final):
    dt = x_prompt.dtype
    Bp = x_prompt.shape[0]
    past_len = cache_k.shape[2]
    xp, xs = x_prompt, x_sample
    kp_l, vp_l, ikp_l, hp_l, cp_l = [], [], [], [], []
    ks_l, vs_l, iks_l, hs_l, cs_l = [], [], [], [], []
    for l in range(DEPTH):
        w = (w_mod[l], b_mod[l], g_norm[l], w_in[l], conv_w[l], conv_b[l], w_r[l], b_r[l],
             w_i[l], b_i[l], lru_lambda[l], g_a[l], g_b[l], w_out[l])
        xp, kp, vp, ikp, hp, cp = layer(
            xp, c_prompt,
            jnp.zeros((Bp, CONV_W - 1, D_LRU), dt), jnp.zeros((Bp, D_LRU), dt),
            jnp.zeros((Bp, 0, N_KV_HEADS, HEAD_DIM), dt), jnp.zeros((Bp, 0, N_KV_HEADS, HEAD_DIM), dt),
            jnp.zeros((Bp, 0, IDX_DIM), dt), 0, True, *w)
        xs, ks_, vs, iks, hs, cs = layer(
            xs, c_sample, state_conv[l], state_lru_h[l], cache_k[l], cache_v[l], cache_idx_k[l],
            past_len, False, *w)
        kp_l.append(kp); vp_l.append(vp); ikp_l.append(ikp); hp_l.append(hp); cp_l.append(cp)
        ks_l.append(ks_); vs_l.append(vs); iks_l.append(iks); hs_l.append(hs); cs_l.append(cs)
    y_prompt = rms_norm(xp, g_final)
    y_sample = rms_norm(xs, g_final)
    return (y_prompt, y_sample,
            jnp.stack(kp_l), jnp.stack(vp_l), jnp.stack(ikp_l), jnp.stack(hp_l), jnp.stack(cp_l),
            jnp.stack(ks_l), jnp.stack(vs_l), jnp.stack(iks_l), jnp.stack(hs_l), jnp.stack(cs_l))


_drawn_inputs = setup_inputs


def setup_inputs(seed=0):
    import zlib

    import numpy as np

    out = dict(_drawn_inputs(seed))
    spreads = {}
    factors = {'g_norm': 2.771, 'b_r': 8.0, 'b_i': 7.042, 'g_a': 8.0, 'g_b': 8.0, 'g_final': 2.902}
    for name, (base, spread) in spreads.items():
        noise = np.random.default_rng([zlib.crc32(name.encode()), seed]).standard_normal(out[name].shape)
        drawn = base * np.exp(spread * noise) if base else spread * noise
        out[name] = __import__('jax').numpy.asarray(drawn.astype(out[name].dtype))
    for name, factor in factors.items():
        out[name] = (out[name] * factor).astype(out[name].dtype)
    return out
```

```python
import concourse.bass as bass
import concourse.mybir as mybir
import numpy as np
from concourse.alu_op_type import AluOpType as ALU

F32 = mybir.dt.float32
F32R = mybir.dt.float32r
BF16 = mybir.dt.bfloat16
ACT = mybir.ActivationFunctionType
AX = mybir.AxisListType

P = 128
D = 1024
KT = D // P
T_PROMPT = 1024
T_SAMPLE = 64
S0 = T_PROMPT + 4
TP = S0 + T_SAMPLE
NCH = 3
CH = TP // NCH
CHUNK = 64
PAST = 512
NKEY = T_PROMPT + PAST + T_SAMPLE
NH, NKV, GROUP = 8, 2, 4
IDX = 64
TOPK_P, TOPK_S = 256, 144
EPS = 1e-6
NEG = -3.4028234663852886e38
TAKEN = -3.0e38
BIAS = -1.0e30
SM_SCALE = P ** -0.5
IW_SCALE = (NH * IDX) ** -0.5
NT = 9
ROUND_ONE_TILES = (7, 6, 5, 4, 3, 2)

XA, ZA, QQ, KK, VV, ZB, IQ, IK = 0, 1024, 2048, 3072, 3328, 3584, 4608, 5120

V_SHIFT, V_SCALE, V_GATE, V_GN, V_CW, V_CB, V_LAM, V_BR, V_BI, V_GA, V_GB, V_H0, V_SC, V_DECAY, NVEC = (
    0, 8, 16, 24, 32, 64, 72, 80, 88, 96, 104, 112, 120, 144, 160)

J_IQ, J_Q, J_K, J_V, J_LRU, J_ZB, J_END = 1, 5, 13, 15, 17, 33, 41
S_LRU, S_ZB = 17, 49
SETS_PER_STEP = 4


def tile_at(i):
    return (i * P, P) if i < NT - 1 else (S0, T_SAMPLE)


def keys_of(i):
    return (0, P * (i + 1)) if i < NT - 1 else (T_PROMPT, PAST + T_SAMPLE)


def pieces_of(i):
    n = keys_of(i)[1]
    if n <= 512:
        return [(0, n)]
    return [(0, n // 2), (n // 2, n - n // 2)]


def score_at(i):
    if i == NT - 1:
        return sum(P * (t + 1) for t in range(2, 8))
    return sum(P * (t + 1) for t in range(2, i))


def bias_at(i):
    return sum(P * (t + 1) for t in range(min(i, NT - 1)))


SCORES = score_at(NT - 1) + PAST + T_SAMPLE
BIASES = bias_at(NT - 1) + PAST + T_SAMPLE

INDEX_TILES = (7, 6, 5, 4, 3, 2, 8)
INDEX_UNITS = [(i, h, p) for i in INDEX_TILES for h in range(NH) for p in range(len(pieces_of(i)))]

PASSES = [(i, g) for i in (0, 1, 8, 2, 3, 4, 5, 6, 7) for g in range(NKV)]


def key_tiles(i):
    k0, n = keys_of(i)
    return [(k0 + P * t, min(P, n - P * t)) for t in range((n + P - 1) // P)]


def attention_order():
    steps = [("head", u) for u in range(GROUP)] + [("turn", 0)]
    x = 0
    for a, (i, g) in enumerate(PASSES):
        kts = len(key_tiles(i))
        more = a + 1 < len(PASSES)
        heads = [("head", u) for u in range(GROUP * (a + 1), GROUP * (a + 2))] if more else []
        at_once = -(-GROUP // max(1, kts - 3))
        for t in range(kts):
            last = t == kts - 1
            if last:
                steps += heads
                heads = []
            if more or not last:
                steps.append(("turn", x + 1))
            steps.append(("mix", x))
            x += 1
            steps += heads[:at_once]
            heads = heads[at_once:]
        steps.append(("out", a))
    return steps


TURNS = [(a, t) for a, (i, g) in enumerate(PASSES) for t in range(len(key_tiles(i)))]

SHARED_ROUNDS = TOPK_S // 8
Q_ROUNDS = 13
TOPK_ROUNDS = TOPK_P // 8
EARLY = (5, 4, 3, 2)
LATE = ((7, 6), (7, 6))
PER_STEP = 2 * (len(EARLY) + sum(len(tiles) for tiles in LATE))


def build(nc, a):
    def sem(name):
        return nc.alloc_semaphore(name)

    base = (nc.sbuf_base + 31) // 32 * 32

    def at(name, shape, dt, off):
        return nc.alloc_sbuf_tensor_at(name, shape, dt, offset=off)

    def nbytes(shape, dt):
        n = 2 if dt == BF16 else 4
        for s in shape[1:]:
            n *= s
        return (n + 31) // 32 * 32

    class Zone:

        def __init__(self, start):
            self.start = self.end = start

        def take(self, name, shape, dt):
            t = at(name, shape, dt, self.end)
            self.end += nbytes(shape, dt)
            assert self.end <= nc.sbuf_usable_end, (name, self.end)
            return t

    keep = Zone(base)
    ident = keep.take("ident", [P, P], F32)
    ones = keep.take("ones", [P, P], F32)
    vec = keep.take("vec", [P, NVEC], F32)
    mod = keep.take("mod", [P, 16, 2], F32)
    shiftscale = keep.take("shiftscale", [P, KT, 2], F32)
    gate_cols = keep.take("gate_cols", [P, KT, 2], F32)
    silc = keep.take("silc", [P, KT, 2], F32)
    craw = keep.take("craw", [P, 2, KT], F32)
    conv_cols = keep.take("conv_cols", [P, NVEC // 8], F32)
    gate_cols_now = keep.take("gate_cols_now", [P, NVEC // 8], F32)
    soft = keep.take("soft", [P, 4, KT], F32)
    ssq = keep.take("ssq", [P, 3, NT], F32)
    norm_v = keep.take("norm_v", [P, NT], F32)
    norm_q = keep.take("norm_q", [P, NT], F32)
    norm_t = keep.take("norm_t", [P, NT], F32)
    rstd = keep.take("rstd", [P, 3, NT], F32)
    iw = keep.take("iw", [P, NT, NH], F32)
    best = keep.take("best", [P, 7, 8], F32)
    held = soft[:, 0, 0:1]
    lasts = keep.take("lasts", [P, 8, 8], F32)
    lasts_t = keep.take("lasts_t", [64, P], F32)
    hsq = keep.take("hsq", [P, TP], F32)
    zone_scores = keep.end
    scores = keep.take("scores", [P, SCORES], F32)

    zone_h = keep.end
    zh = Zone(zone_h)
    h_hi = zh.take("h_hi", [P, KT, TP], F32R)
    h_lo = zh.take("h_lo", [P, KT, TP], F32R)
    w_mod_raw = at("w_mod_raw", [P, KT, 2 * D], F32, zone_h)

    zone_w = zh.end
    zw = Zone(zone_w)
    w_raw = zw.take("w_raw", [P, 2, KT, P], F32)
    zone_wsplit = zw.end
    w_hi = zw.take("w_hi", [P, 2, KT, P], F32R)
    w_lo = zw.take("w_lo", [P, 2, KT, P], F32R)

    zone_s = zw.end
    zs = Zone(zone_s)
    stage = zs.take("stage", [P, 2, TP], F32)

    zone_x = zs.end
    z = Zone(zone_x)
    x_in = z.take("x_in", [P, NT, D], F32)
    x_t = z.take("x_t", [P, KT, TP], F32)
    vrows = z.take("vrows", [P, 2, P], F32)

    z = Zone(zone_x)
    iq_parts = z.take("iq_parts", [P, NH, TP], F32R)
    ik_hi = z.take("ik_hi", [P, NKEY], F32R)
    ik_lo = z.take("ik_lo", [P, NKEY], F32R)
    relu = z.take("relu", [P, 3, 512], F32)
    ikw_rows = z.take("ikw_rows", [P, NT, 72], F32)
    cache_ik = z.take("cache_ik", [P, 4, IDX], F32)

    z = Zone(zone_x)
    padded = z.take("padded", [P, TP + 4], F32)
    conv = z.take("conv", [P, TP], F32)
    conv_hi = z.take("conv_hi", [P, TP], F32R)
    conv_lo = z.take("conv_lo", [P, TP], F32R)
    gate_r = z.take("gate_r", [P, TP], F32)
    gate_i = z.take("gate_i", [P, TP], F32)
    decay_t = z.take("decay_t", [P, TP], F32)
    tanh_t = z.take("tanh_t", [P, TP], F32)
    mult = z.take("mult", [P, TP], F32)
    hidden = z.take("hidden", [P, TP], F32)
    silu_z = z.take("silu_z", [P, TP], F32)
    y_a = z.take("y_a", [P, TP], F32)
    gw_raw = z.take("gw_raw", [P, 2, P], F32)
    gw_hi = z.take("gw_hi", [P, 2, P], F32R)
    gw_lo = z.take("gw_lo", [P, 2, P], F32R)
    kv_rows = z.take("kv_rows", [P, 2, NT, P], F32)
    wg_raw = z.take("wg_raw", [P, KT, P], F32)

    zx = Zone(zone_x)
    k_hi = zx.take("k_hi", [P, NKV, NKEY], F32R)
    k_lo = zx.take("k_lo", [P, NKV, NKEY], F32R)
    v_hi = zx.take("v_hi", [P, 13, NKV * P], F32R)
    v_lo = zx.take("v_lo", [P, 13, NKV * P], F32R)
    bias = zx.take("bias", [P, BIASES], BF16)
    zone_kv = zx.end
    z = Zone(zone_kv)
    k_raw = z.take("k_raw", [P, NKV, NKEY], F32)
    v_raw = at("v_raw", [P, 13, NKV * P], F32, zone_kv)
    z = Zone(max(z.end, zone_kv + nbytes([P, 13, 256], F32)))
    cache_k_rows = z.take("cache_k_rows", [P, 4, NKV * P], F32)
    z = Zone(zone_kv)
    q_raw = z.take("q_raw", [P, NH, P], F32)
    pt_lo = z.take("pt_lo", [P, 2, 512], F32R)
    q_hi = z.take("q_hi", [P, NH, P], F32R)
    q_lo = z.take("q_lo", [P, NH, P], F32R)
    diag_b = z.take("diag_b", [P, 4, P], F32)
    z = Zone(zone_s)
    silu_zb = z.take("silu_zb", [P, NH, P], F32)
    y_b = z.take("y_b", [P, 512], F32)
    o_sq = z.take("o_sq", [P, 512], F32)
    z = Zone(zone_scores)
    probs_a = z.take("probs_a", [P, 4, D], F32)
    diag_a = z.take("diag_a", [P, 4, P], F32)
    probs_b = at("probs_b", [P, 4, D], F32, zone_wsplit)
    z = Zone(zone_h)
    woa_hi = z.take("woa_hi", [P, KT, D], F32R)
    woa_lo = z.take("woa_lo", [P, KT, D], F32R)
    pt_hi = z.take("pt_hi", [P, 2, 512], F32R)
    small = z.take("small", [P, 4, 8], F32)
    wo_raw = at("wo_raw", [P, 2, D], F32, zone_w)

    z = Zone(zone_x)
    wob_hi = z.take("wob_hi", [P, KT, D], F32R)
    wob_lo = z.take("wob_lo", [P, KT, D], F32R)
    x_res = z.take("x_res", [P, 2, D], F32)
    y_fin = z.take("y_fin", [P, 2, D], F32)
    z = Zone(zone_s)
    y_raw = z.take("y_raw", [P, 2, KT, P], F32)
    z = Zone(zone_wsplit)
    y_hi = z.take("y_hi", [P, 2, KT, P], F32R)
    y_lo = z.take("y_lo", [P, 2, KT, P], F32R)
    z = Zone(zone_scores)
    gate_rows = z.take("gate_rows", [P, 2, D], F32)
    gf_rows = z.take("gf_rows", [P, D], F32)
    acc = z.take("acc", [P, D], F32)

    ps = nc.alloc_psum_tensor("ps", [P, 8, 512], F32)

    q_s = nc.dram_tensor("q_scratch", [NH, P, TP], F32, kind="Internal").ap()
    k_s = nc.dram_tensor("k_scratch", [NKV, P, TP], F32, kind="Internal").ap()
    zb_s = nc.dram_tensor("zb_scratch", [NH, P, TP], F32, kind="Internal").ap()
    y_s = nc.dram_tensor("y_scratch", [2, KT, P, TP], F32, kind="Internal").ap()

    w_in = a["w_in"].rearrange("l (k p) n -> p (l k) n", p=P)
    w_mod = a["w_mod"].rearrange("l (p k) n -> p (l k) n", k=KT)
    w_out = a["w_out"].rearrange("l (k p) n -> (l k) p n", p=P)

    def f32(ap):
        return ap.bitcast(F32)

    def row_slice(ap, i):
        p, s = ap
        return p[i * P:(i + 1) * P] if i < NT - 1 else s

    x_rows = (a["x_prompt"].rearrange("b t d -> (b t) d"), a["x_sample"].rearrange("b t d -> (b t) d"))
    y_rows = (a["y_prompt"].rearrange("b t d -> (b t) d"), a["y_sample"].rearrange("b t d -> (b t) d"))

    vec_in = sem("vec_in")
    c_in = sem("c_in")
    x_in_s = [sem(f"x_in{i}") for i in range(NT)]
    wmod_in = [sem(f"wmod_in{i}") for i in range(4)]
    w_landed = [sem(f"w_landed{i}") for i in range(2)]
    w_hi_done = sem("w_hi_done")
    w_lo_done = sem("w_lo_done")
    set_ready = sem("set_ready")
    set_read = sem("set_read")
    const_done = sem("const_done")
    const_zero = sem("const_zero")
    vec_t = sem("vec_t")
    vec_done = sem("vec_done")
    init_done = sem("init_done")
    silc_done = sem("silc_done")
    sq_done = sem("sq_done")
    rs_step = sem("rs_step")
    rs_sqrt = sem("rs_sqrt")
    xn_done = sem("xn_done")
    xt_ready = sem("xt_ready")
    xt_read = sem("xt_read")
    mod_ready = sem("mod_ready")
    mod_step = sem("mod_step")
    h_full = sem("h_full")
    h_hi_done = sem("h_hi_done")
    h_lo_done = sem("h_lo_done")
    soft_act = sem("soft_act")
    soft_step = sem("soft_step")
    cik_in = sem("cik_in")
    cik_t = sem("cik_t")
    ik_t = sem("ik_t")
    ik_read = sem("ik_read")
    ik_parts = sem("ik_parts")
    iq_done = sem("iq_done")
    iw_done = sem("iw_done")
    ik_out = sem("ik_out")
    index_ready = sem("index_ready")
    relu_done = sem("relu_done")
    index_added = sem("index_added")
    masked = sem("masked")
    select = sem("select")
    staged = [sem(f"staged_out{i}") for i in range(2)]
    kv_t = sem("kv_t")
    kv_read = sem("kv_read")
    kv_out = [sem(f"kv_out{i}") for i in range(2)]
    conv_cols_done = sem("conv_cols_done")
    gate_cols_done = sem("gate_cols_done")
    wg_in = sem("wg_in")
    pad_edge = sem("pad_edge")
    tap0 = sem("tap0")
    taps = sem("taps")
    gw_in = sem("gw_in")
    gw_hi_done = sem("gw_hi_done")
    gw_lo_done = sem("gw_lo_done")
    conv_hi_done = sem("conv_hi_done")
    conv_lo_done = sem("conv_lo_done")
    gated_u = sem("gated_u")
    decays = sem("decays")
    mult_sq = sem("mult_sq")
    mult_done = sem("mult_done")
    lru = sem("lru")
    hsq_step = sem("hsq_step")
    ya_out = sem("ya_out")
    zb_scaled = sem("zb_scaled")
    lasts_ready = sem("lasts_ready")
    lasts_read = sem("lasts_read")
    lasts_out = sem("lasts_out")
    ssa_ready = sem("ssa_ready")
    ssa_read = sem("ssa_read")
    gate_ready = sem("gate_ready")
    gate_read = sem("gate_read")
    ck_in = sem("ck_in")
    k_in = sem("k_in")
    ck_t = sem("ck_t")
    ck_read = sem("ck_read")
    k_hi_done = sem("k_hi_done")
    k_lo_done = sem("k_lo_done")
    v_in = sem("v_in")
    v_hi_done = sem("v_hi_done")
    v_lo_done = sem("v_lo_done")
    bias_done = sem("bias_done")
    q_in = [sem(f"q_in{i}") for i in range(2)]
    q_hi_done = sem("q_hi_done")
    q_lo_done = sem("q_lo_done")
    zb_in = [sem(f"zb_in{i}") for i in range(2)]
    qk_ready = sem("qk_ready")
    logits = sem("logits")
    max_neg = sem("max_neg")
    exp_done = sem("exp_done")
    inv_done = sem("inv_done")
    diag_ready = sem("diag_ready")
    turned = sem("turned")
    pt_hi_done = sem("pt_hi_done")
    pt_lo_done = sem("pt_lo_done")
    mixed = sem("mixed")
    o_ready = sem("o_ready")
    o_sq_done = sem("o_sq_done")
    yb_done = sem("yb_done")
    yb_out = sem("yb_out")
    osum = sem("osum")
    ssb_ready = sem("ssb_ready")
    ssb_read = sem("ssb_read")
    wo_in = [sem(f"wo_in{i}") for i in range(2)]
    wo_hi_done = sem("wo_hi_done")
    wo_lo_done = sem("wo_lo_done")
    wob_lo_done = sem("wob_lo_done")
    diag_done = sem("diag_done")
    out_small = sem("out_small")
    grow_ready = sem("grow_ready")
    grow_read = sem("grow_read")
    gf_in = sem("gf_in")
    y_in = [sem(f"y_in{i}") for i in range(2)]
    y_hi_done = sem("y_hi_done")
    y_lo_done = sem("y_lo_done")
    xres_in = [sem(f"xres_in{i}") for i in range(2)]
    proj_ready = sem("proj_ready")
    out_step = sem("out_step")
    fin_sq = sem("fin_sq")
    fin_done = sem("fin_done")
    y_out = [sem(f"y_out{i}") for i in range(2)]

    def split3(k, w_part_hi, w_part_lo, x_hi, x_lo, out, first, last):
        nc.tensor.matmul(out, w_part_hi, x_hi, start=first, stop=False)
        nc.tensor.matmul(out, w_part_hi, x_lo, start=False, stop=False)
        return nc.tensor.matmul(out, w_part_lo, x_hi, start=False, stop=last)

    block = nc.Block()
    with block:
        @block.sync
        def _(sp):
            def load_w(j, col, width=P):
                if not isinstance(j, int) or j >= 2:
                    sp.wait_ge(w_lo_done, j - 1)
                slot = load_w.slot
                load_w.slot = 1 - slot
                sp.dma_start(w_raw[:, slot, :, 0:width], w_in[:, :, bass.ds(col, width)]).then_inc(w_landed[slot], 16)
            load_w.slot = 0

            def rows(r0, n, ap, tile=0):
                sp.dma_start(vrows[r0:r0 + n, tile, :], ap).then_inc(vec_in, 16)

            sp.dma_start(craw[:, 0, :], a["c_prompt"].rearrange("b (p k) -> p (b k)", k=KT)).then_inc(c_in, 16)
            sp.dma_start(craw[:, 1, :], a["c_sample"].rearrange("b (p k) -> p (b k)", k=KT)).then_inc(c_in, 16)
            rows(V_SHIFT, 24, a["b_mod"].rearrange("l (r c) -> (l r) c", c=P))
            rows(V_GN, 8, a["g_norm"].rearrange("l (r c) -> (l r) c", c=P))
            rows(V_CW, 32, a["conv_w"].rearrange("l j (r c) -> (l j r) c", c=P))
            rows(V_CB, 8, a["conv_b"].rearrange("l (r c) -> (l r) c", c=P))
            rows(V_LAM, 8, a["lru_lambda"].rearrange("l (r c) -> (l r) c", c=P))
            rows(V_BR, 8, a["b_r"].rearrange("l h c -> (l h) c"))
            rows(V_BI, 8, a["b_i"].rearrange("l h c -> (l h) c"))
            rows(V_GA, 8, a["g_a"].rearrange("l (r c) -> (l r) c", c=P))
            rows(V_GB, 8, a["g_b"].rearrange("l (r c) -> (l r) c", c=P))
            rows(V_H0, 8, a["state_lru_h"].rearrange("l b (r c) -> (l b r) c", c=P))
            rows(0, 24, a["state_conv"].rearrange("l b j (r c) -> (l b j r) c", c=P), 1)
            for i in range(NT):
                n = tile_at(i)[1]
                sp.dma_start(x_in[0:n, i, :], row_slice(x_rows, i)).then_inc(x_in_s[i], 16)
                if i % 2 == 1:
                    m = i // 2
                    sp.dma_start(w_mod_raw[:, :, 512 * m:512 * (m + 1)],
                                 w_mod[:, :, 512 * m:512 * (m + 1)]).then_inc(wmod_in[m], 16)
            load_w(0, IK, 72)
            for m in range(4):
                load_w(J_IQ + m, IQ + P * m)
                if m == 0:
                    sp.wait_ge(h_lo_done, KT)
                    sp.dma_start(cache_ik[:, :, :], a["cache_idx_k"].rearrange(
                        "l b (s p) d -> p (l b s) d", p=P)).then_inc(cik_in, 16)
            sp.wait_ge(ik_read, 2)
            sp.dma_start(a["ik_prompt"].rearrange("l b (s p) d -> p (l b s) d", p=P),
                         ikw_rows[:, 0:8, 0:IDX]).then_inc(ik_out, 16)
            sp.dma_start(a["ik_sample"].rearrange("l b t d -> (l b t) d"),
                         ikw_rows[0:T_SAMPLE, 8, 0:IDX]).then_inc(ik_out, 16)

            load_w(J_Q, QQ)
            load_w(J_Q + 1, QQ + P)

            def store_q(j, head, slot):
                sp.wait_ge(set_read, 3 * j + 3)
                sp.dma_start(q_s[bass.ds(head, 1)].rearrange("h p t -> (h p) t"), stage[:, slot, :]).then_inc(staged[slot], 16)

            with sp.Fori(0, 4) as i:
                for u in range(2):
                    load_w(i * 2 + (J_Q + 2 + u), i * (2 * P) + (QQ + P * (2 + u)))
                    store_q(i * 2 + (J_Q + u), i * 2 + u, (J_Q + u) % 2)
            kv_dst = []
            for n, which in ((0, "k"), (0, "v")):
                for g in range(NKV):
                    kv_dst.append((a[which + "_prompt"].rearrange("l b (s p) g d -> p (l b s) g d", p=P)[:, :, g, :],
                                   a[which + "_sample"].rearrange("l b t g d -> (l b t) g d")[:, g, :]))
            for m in range(4):
                j = J_K + m
                if m < 2:
                    load_w(j + 2, KK + P * (m + 2))
                    sp.wait_ge(set_read, 3 * j + 3)
                    sp.dma_start(k_s[m], stage[:, j % 2, :]).then_inc(staged[j % 2], 16)
                else:
                    load_w(j + 2, XA if m == 2 else ZA)
                if m >= 1:
                    sp.wait_ge(kv_read, 3 * m)
                    sp.dma_start(kv_dst[m - 1][0], kv_rows[:, (m - 1) % 2, 0:8, :]).then_inc(kv_out[(m - 1) % 2], 16)
                    sp.dma_start(kv_dst[m - 1][1], kv_rows[0:T_SAMPLE, (m - 1) % 2, 8, :]).then_inc(kv_out[(m - 1) % 2], 16)

            def load_gates(i):
                sp.dma_start(gw_raw[:, 0, :], a["w_r"][0, bass.ds(i, 1)].rearrange("h i j -> (h i) j")).then_inc(gw_in, 16)
                sp.dma_start(gw_raw[:, 1, :], a["w_i"][0, bass.ds(i, 1)].rearrange("h i j -> (h i) j")).then_inc(gw_in, 16)

            sp.wait_ge(index_added, len(INDEX_UNITS))
            sp.wait_ge(ik_out, 32)
            load_gates(0)
            sp.wait_ge(kv_read, 12)
            sp.dma_start(kv_dst[3][0], kv_rows[:, 1, 0:8, :]).then_inc(kv_out[1], 16)
            sp.dma_start(kv_dst[3][1], kv_rows[0:T_SAMPLE, 1, 8, :]).then_inc(kv_out[1], 16)

            def load_gate_block(i):
                if not isinstance(i, int) or i > 0:
                    sp.wait_ge(gate_ready, i)
                sp.dma_start(wg_raw[:, :, :], w_mod[:, :, bass.ds(i * P + 2 * D, P)]).then_inc(wg_in, 16)

            def store_ya(i):
                sp.wait_ge(lru, i * 7 + 8)
                sp.dma_start(y_s[0, bass.ds(i, 1)].rearrange("h p t -> (h p) t"), y_a[:, :]).then_inc(ya_out, 16)

            load_gate_block(0)
            load_w(J_LRU + 2, XA + P)
            load_w(J_LRU + 3, ZA + P)

            def lru_step(i, col_xa, col_za):
                load_w(i * 2 + (J_LRU + 4), col_xa)
                load_w(i * 2 + (J_LRU + 5), col_za)
                sp.wait_ge(gw_lo_done, i + 1)
                load_gates(i + 1)
                load_gate_block(i + 1)
                store_ya(i)

            with sp.Fori(0, 6) as i:
                lru_step(i, i * P + (XA + 2 * P), i * P + (ZA + 2 * P))
            lru_step(6, ZB, ZB + P)
            load_w(J_ZB + 2, ZB + 2 * P)
            load_w(J_ZB + 3, ZB + 3 * P)

            def store_zb(m):
                slot = (J_ZB + m) % 2
                sp.wait_ge(zb_scaled, m + 1)
                sp.dma_start(zb_s[m], stage[:, slot, :]).then_inc(staged[slot], 16)

            def load_keys():
                sp.wait_ge(v_lo_done, 2)
                for g in range(NKV):
                    sp.dma_start(k_raw[:, g, 0:T_PROMPT], k_s[g, :, 0:T_PROMPT]).then_inc(k_in, 16)
                    sp.dma_start(k_raw[:, g, T_PROMPT + PAST:], k_s[g, :, S0:]).then_inc(k_in, 16)

            def load_values():
                sp.wait_ge(ya_out, 129)
                sp.wait_ge(hsq_step, 17)
                sp.wait_ge(lru, 57)
                sp.wait_ge(gate_ready, KT)
                sp.wait_ge(kv_out[0], 64)
                sp.wait_ge(kv_out[1], 64)
                sp.dma_start(v_raw[:, 0:8, :], a["v_prompt"].rearrange(
                    "l b (s p) g d -> p (l b s) (g d)", p=P)).then_inc(v_in, 16)
                sp.dma_start(v_raw[:, 8:12, :], a["cache_v"].rearrange(
                    "l b (s p) g d -> p (l b s) (g d)", p=P)).then_inc(v_in, 16)
                sp.dma_start(v_raw[0:T_SAMPLE, 12, :], a["v_sample"].rearrange(
                    "l b t g d -> (l b t) (g d)")).then_inc(v_in, 16)
                sp.dma_start(cache_k_rows[:, :, :], a["cache_k"].rearrange(
                    "l b (s p) g d -> p (l b s) (g d)", p=P)).then_inc(ck_in, 16)

            load_w(J_ZB + 4, ZB + 4 * P)
            store_zb(0)
            store_ya(7)
            load_values()
            for m in range(1, 4):
                load_w(J_ZB + 4 + m, ZB + (4 + m) * P)
                store_zb(m)
            load_keys()
            for m in range(4, 6):
                store_zb(m)
            sp.wait_ge(lasts_read, 1)
            sp.dma_start(a["conv_prompt"].rearrange("l b j (r c) -> (l b j r) c", c=P), lasts_t[0:24, :]).then_inc(lasts_out, 16)
            sp.dma_start(a["conv_sample"].rearrange("l b j (r c) -> (l b j r) c", c=P), lasts_t[24:48, :]).then_inc(lasts_out, 16)
            sp.dma_start(a["h_prompt"].rearrange("l b (r c) -> (l b r) c", c=P), lasts_t[48:56, :]).then_inc(lasts_out, 16)
            sp.dma_start(a["h_sample"].rearrange("l b (r c) -> (l b r) c", c=P), lasts_t[56:64, :]).then_inc(lasts_out, 16)

            def load_wo(k):
                if k < 2:
                    sp.wait_ge(w_lo_done, J_END)
                elif k < KT + 2:
                    sp.wait_ge(wo_lo_done, k - 1)
                else:
                    sp.wait_ge(wob_lo_done, k - KT - 1)
                sp.dma_start(wo_raw[:, k % 2, :], w_out[k]).then_inc(wo_in[k % 2], 16)

            def load_q(p_):
                i, g = PASSES[p_]
                t0, rows_ = tile_at(i)
                if p_ == 0:
                    sp.wait_ge(k_lo_done, 1)
                    for s in range(2):
                        sp.wait_ge(staged[s], 16 * 4)
                if p_ >= 2:
                    sp.wait_ge(q_lo_done, p_ - 1)
                heads = slice(GROUP * g, GROUP * (g + 1))
                sp.dma_start(q_raw[:, heads, 0:rows_],
                             q_s[heads, :, t0:t0 + rows_].rearrange("h p t -> p h t")).then_inc(q_in[g], 16)

            def load_zb(p_):
                i, g = PASSES[p_]
                t0, rows_ = tile_at(i)
                if p_ == 0:
                    for s in range(2):
                        sp.wait_ge(staged[s], 16 * 9)
                if p_ >= 2:
                    sp.wait_ge(yb_done, p_ - 1)
                heads = slice(GROUP * g, GROUP * (g + 1))
                sp.dma_start(silu_zb[:, heads, 0:rows_],
                             zb_s[heads, :, t0:t0 + rows_].rearrange("h p t -> p h t")).then_inc(zb_in[g], 16)

            load_q(0)
            load_q(1)
            for m in range(6, KT):
                store_zb(m)
            load_wo(0)
            load_wo(1)
            load_zb(0)
            load_zb(1)
            for p_, (i, g) in enumerate(PASSES):
                t0, rows_ = tile_at(i)
                if p_ + 2 < len(PASSES):
                    load_q(p_ + 2)
                if p_ + 2 < KT:
                    load_wo(p_ + 2)
                sp.wait_ge(yb_done, p_ + 1)
                sp.dma_start(y_s[1, GROUP * g:GROUP * (g + 1), :, t0:t0 + rows_].rearrange("h p t -> p h t"),
                             y_b[:, 0:GROUP * rows_].rearrange("p (h t) -> p h t", h=GROUP)).then_inc(yb_out, 16)
                if p_ + 2 < len(PASSES):
                    load_zb(p_ + 2)
            for k in range(KT, 2 * KT):
                load_wo(k)
            sp.dma_start(gf_rows[:, :], a["g_final"].rearrange("(b d) -> b d", b=1).broadcast_to([P, D])).then_inc(gf_in, 16)

            def load_y(e):
                t, half = e // 2, e % 2
                t0, rows_ = tile_at(t)
                if e >= 2:
                    sp.wait_ge(y_lo_done, e - 1)
                sp.dma_start(y_raw[:, e % 2, :, 0:rows_], y_s[half, :, :, t0:t0 + rows_].rearrange("k p t -> p k t")).then_inc(y_in[e % 2], 16)

            def load_x(t):
                rows_ = tile_at(t)[1]
                if t >= 2:
                    sp.wait_ge(out_step, 4 * (t - 1))
                sp.dma_start(x_res[0:rows_, t % 2, :], row_slice(x_rows, t)).then_inc(xres_in[t % 2], 16)

            def store_y(t):
                rows_ = tile_at(t)[1]
                sp.wait_ge(fin_done, t + 1)
                sp.dma_start(row_slice(y_rows, t), y_fin[0:rows_, t % 2, :]).then_inc(y_out[t % 2], 16)

            sp.wait_ge(ya_out, 129)
            sp.wait_ge(yb_out, 16 * len(PASSES))
            sp.wait_ge(osum, 3 * len(PASSES) + 1)
            sp.wait_ge(mixed, len(TURNS))
            for e in range(2):
                load_y(e)
            load_x(0)
            load_x(1)
            for t in range(NT):
                if t + 1 < NT:
                    load_y(2 * t + 2)
                    load_y(2 * t + 3)
                if 2 <= t + 1 < NT:
                    load_x(t + 1)
                store_y(t)
            sp.wait_ge(ik_out, 32)
            sp.wait_ge(kv_out[0], 64)
            sp.wait_ge(kv_out[1], 64)
            sp.wait_ge(lasts_out, 64)
            sp.wait_ge(y_out[0], 16 * 5)
            sp.wait_ge(y_out[1], 16 * 4)

        @block.gpsimd
        def _(pool):
            pool.memset(ident[:, :], 0.0).then_inc(const_zero, 1)
            pool.wait_ge(const_zero, 1)
            pool.affine_select(out=ident[:, :], in_=ident[:, :], compare_op=ALU.not_equal, fill=1.0, base=0,
                               pattern=[[-1, P]], channel_multiplier=1).then_inc(const_done, 1)
            pool.memset(ones[:, :], 1.0).then_inc(const_done, 1)
            pool.memset(x_t[:, :, T_PROMPT:S0], 0.0).then_inc(const_done, 1)
            pool.memset(hsq[:, :], 0.0).then_inc(hsq_step, 1)

            def split_w(j, slot, width=P):
                pool.wait_ge(w_hi_done, j + 1)
                pool.tensor_tensor(w_lo[:, slot, :, 0:width], w_raw[:, slot, :, 0:width],
                                   f32(w_hi[:, slot, :, 0:width]), ALU.subtract).then_inc(w_lo_done, 1)

            split_w(0, 0, 72)
            for j in range(1, J_Q + 2):
                split_w(j, j % 2)
            with pool.Fori(0, 4) as i:
                for u in range(2):
                    split_w(i * 2 + (J_Q + 2 + u), (J_Q + u) % 2)
            for j in range(J_K + 2, J_LRU + 2):
                split_w(j, j % 2)

            def split_gates(i):
                pool.wait_ge(gw_hi_done, i + 1)
                pool.tensor_tensor(gw_lo[:, :, :], gw_raw[:, :, :], f32(gw_hi[:, :, :]), ALU.subtract).then_inc(gw_lo_done, 1)

            def split_conv(i):
                pool.wait_ge(conv_hi_done, i + 1)
                pool.tensor_tensor(conv_lo[:, :], conv[:, :], f32(conv_hi[:, :]), ALU.subtract).then_inc(conv_lo_done, 1)

            def gate_conv(i):
                pool.wait_ge(set_read, i * 12 + (3 * S_LRU + 15))
                pool.tensor_tensor(gate_i[:, :], gate_i[:, :], conv[:, :], ALU.mult).then_inc(gated_u, 1)

            def square_hidden(i):
                pool.wait_ge(lru, i * 7 + 6)
                pool.tensor_tensor(mult[:, :], hidden[:, :], hidden[:, :], ALU.mult).then_inc(hsq_step, 1)
                pool.wait_ge(hsq_step, i * 2 + 2)
                pool.tensor_tensor(hsq[:, :], hsq[:, :], mult[:, :], ALU.add).then_inc(hsq_step, 1)

            split_gates(0)
            split_w(J_LRU + 2, J_LRU % 2)
            split_conv(0)
            split_w(J_LRU + 3, (J_LRU + 1) % 2)
            split_w(J_LRU + 4, J_LRU % 2)
            with pool.Fori(0, 7) as i:
                gate_conv(i)
                split_gates(i + 1)
                split_w(i * 2 + (J_LRU + 5), (J_LRU + 1) % 2)
                split_conv(i + 1)
                square_hidden(i)
                split_w(i * 2 + (J_LRU + 6), J_LRU % 2)

            def scale_zb(m):
                slot = (J_ZB + m) % 2
                pool.wait_ge(set_read, 3 * (S_ZB + m) + 3 if m else 3 * (S_ZB - 2) + 3)
                pool.tensor_tensor(stage[:, slot, :], stage[:, slot, :],
                                   vec[:, V_GB + m:V_GB + m + 1].broadcast_to([P, TP]), ALU.mult).then_inc(zb_scaled, 1)

            gate_conv(7)
            scale_zb(0)
            split_w(J_ZB + 3, (J_ZB + 3) % 2)
            square_hidden(7)
            for m in range(1, KT):
                scale_zb(m)
                if J_ZB + 3 + m < J_END:
                    split_w(J_ZB + 3 + m, (J_ZB + 3 + m) % 2)
                if m == 3:
                    pool.wait_ge(v_hi_done, 2)
                    pool.tensor_tensor(v_lo[:, 0:12, :], v_raw[:, 0:12, :], f32(v_hi[:, 0:12, :]),
                                       ALU.subtract).then_inc(v_lo_done, 1)
                    pool.tensor_tensor(v_lo[0:T_SAMPLE, 12, :], v_raw[0:T_SAMPLE, 12, :],
                                       f32(v_hi[0:T_SAMPLE, 12, :]), ALU.subtract).then_inc(v_lo_done, 1)
                if m == 5:
                    pool.wait_ge(k_hi_done, 1)
                    pool.tensor_tensor(k_lo[:, :, :], k_raw[:, :, :], f32(k_hi[:, :, :]), ALU.subtract).then_inc(k_lo_done, 1)

            def split_q(p_):
                i, g = PASSES[p_]
                rows_ = tile_at(i)[1]
                heads = slice(GROUP * g, GROUP * (g + 1))
                pool.wait_ge(q_hi_done, p_ + 1)
                pool.tensor_tensor(q_lo[:, heads, 0:rows_], q_raw[:, heads, 0:rows_], f32(q_hi[:, heads, 0:rows_]),
                                   ALU.subtract).then_inc(q_lo_done, 1)

            split_q(0)
            pool.wait_ge(ssa_ready, 1)
            pool.memset(hsq[:, :], 0.0).then_inc(osum, 1)
            for kind, n in attention_order():
                if kind == "head":
                    p_ = n // GROUP
                    if n % GROUP == 0 and p_ + 1 < len(PASSES):
                        split_q(p_ + 1)
                    if n % GROUP == GROUP - 1 and p_ < KT:
                        pool.wait_ge(wo_hi_done, p_ + 1)
                        pool.tensor_tensor(woa_lo[:, p_, :], wo_raw[:, p_ % 2, :], f32(woa_hi[:, p_, :]),
                                           ALU.subtract).then_inc(wo_lo_done, 1)
                elif kind == "out":
                    t0, r = tile_at(PASSES[n][0])
                    pool.wait_ge(o_sq_done, n + 1)
                    pool.tensor_tensor(o_sq[:, 0:2 * r], o_sq[:, 0:2 * r], o_sq[:, 2 * r:4 * r], ALU.add).then_inc(osum, 1)
                    pool.wait_ge(osum, 3 * n + 2)
                    pool.tensor_tensor(o_sq[:, 0:r], o_sq[:, 0:r], o_sq[:, r:2 * r], ALU.add).then_inc(osum, 1)
                    pool.wait_ge(osum, 3 * n + 3)
                    pool.tensor_tensor(hsq[:, t0:t0 + r], hsq[:, t0:t0 + r], o_sq[:, 0:r], ALU.add).then_inc(osum, 1)
            for e in range(2 * NT):
                rows_ = tile_at(e // 2)[1]
                pool.wait_ge(y_hi_done, e + 1)
                pool.tensor_tensor(y_lo[:, e % 2, :, 0:rows_], y_raw[:, e % 2, :, 0:rows_],
                                   f32(y_hi[:, e % 2, :, 0:rows_]), ALU.subtract).then_inc(y_lo_done, 1)

        @block.scalar
        def _(act):
            act.wait_ge(c_in, 32)
            nc.scalar.activation(silc[:, :, :], craw[:, :, :].rearrange("p b k -> p k b"), ACT.Silu).then_inc(silc_done, 1)
            act.wait_ge(init_done, 1)
            for i in range(NT):
                n = tile_at(i)[1]
                act.wait_ge(x_in_s[i], 16)
                if i >= 2:
                    act.wait_ge(sq_done, i - 1)
                nc.scalar.activation(stage[0:n, i % 2, 0:D], x_in[0:n, i, :], ACT.Square,
                                     accum_out=ssq[0:n, 0, i:i + 1]).then_inc(sq_done, 1)

            def root(n):
                act.wait_ge(rs_step, 6 * n + 1)
                nc.scalar.activation(norm_q[:, :], norm_v[:, :], ACT.Sqrt).then_inc(rs_sqrt, 1)

            root(0)
            act.wait_ge(vec_done, 1)
            nc.scalar.activation(soft[:, 0, :], vec[:, V_LAM:V_LAM + 8], ACT.Abs).then_inc(soft_act, 1)
            act.wait_ge(soft_act, 1)
            nc.scalar.activation(soft[:, 0, :], soft[:, 0, :], ACT.Exp, scale=-1.0).then_inc(soft_act, 1)
            for i in range(NT):
                t0, n = tile_at(i)
                act.wait_ge(xt_ready, i + 1)
                b = 2 * (i % 3)
                nc.scalar.activation(x_t[:, :, t0:t0 + n],
                                     ps[:, b:b + 2, :].rearrange("p b (k t) -> p (b k) t", t=P)[:, :, 0:n],
                                     ACT.Copy).then_inc(xt_read, 1)

            def split_w(slot, loads, s_before=None, width=P):
                act.wait_ge(w_landed[slot], loads * 16)
                if s_before is not None:
                    act.wait_ge(set_ready, s_before)
                nc.scalar.activation(w_hi[:, slot, :, 0:width], w_raw[:, slot, :, 0:width], ACT.Copy).then_inc(w_hi_done, 1)

            split_w(0, 1, None, 72)
            split_w(1, 1)
            for k in range(KT):
                act.wait_ge(h_full, 2 * k + 2)
                nc.scalar.activation(h_hi[:, k, :], x_t[:, k, :], ACT.Copy).then_inc(h_hi_done, 1)

            def read_set(s, dst, func, m=P, bias=None):
                for c in range(NCH):
                    act.wait_ge(set_ready, s * 3 + (c + 1))
                    b = 3 * (read_set.parity) + c
                    d = dst[0:m, CH * c:CH * (c + 1)]
                    if bias is None:
                        x = nc.scalar.activation(d, ps[0:m, b, 0:CH], func)
                    else:
                        x = nc.scalar.activation(d, ps[0:m, b, 0:CH], func, bias=bias)
                    x.then_inc(set_read, 1)
                read_set.parity = 1 - read_set.parity
            read_set.parity = 0

            read_set(0, stage[:, 0, :], ACT.Copy, 72)
            split_w(0, 2, 3)
            act.wait_ge(ik_t, 1)
            nc.scalar.activation(ikw_rows[:, 0:5, :], ps[:, 7, 0:360].rearrange("p (t w) -> p t w", w=72),
                                 ACT.Copy).then_inc(ik_read, 1)
            act.wait_ge(ik_t, 2)
            nc.scalar.activation(ikw_rows[:, 5:8, :], ps[:, 7, 0:216].rearrange("p (t w) -> p t w", w=72), ACT.Copy)
            nc.scalar.activation(ikw_rows[0:T_SAMPLE, 8, :], ps[0:T_SAMPLE, 7, 216:288], ACT.Copy).then_inc(ik_read, 1)
            for m in range(4):
                j = J_IQ + m
                if m == 1:
                    act.wait_ge(ik_parts, 12)
                if m >= 2:
                    act.wait_ge(iq_done, 4 * (m - 1))
                read_set(j, stage[:, j % 2, :], ACT.Copy)
                split_w(j % 2, (j + 2) // 2 + 1, 3 * j + 3)
            for u, (i, h, p_) in enumerate(INDEX_UNITS):
                rows_ = tile_at(i)[1]
                n = pieces_of(i)[p_][1]
                act.wait_ge(index_ready, u + 1)
                if u >= 3:
                    act.wait_ge(index_added, u - 2)
                nc.scalar.activation(relu[0:rows_, u % 3, 0:n], ps[0:rows_, 6 + u % 2, 0:n], ACT.Relu).then_inc(relu_done, 1)

            act.wait_ge(iq_done, 16)

            def read_q(i, u):
                slot = (J_Q + u) % 2
                if not isinstance(i, int):
                    act.wait_ge(staged[slot], i * 16)
                read_set(i * 2 + (J_Q + u), stage[:, slot, :], ACT.Copy)
                split_w(slot, i + ((J_Q + 2 + u) // 2 + 1), i * 6 + (3 * (J_Q + u) + 3))

            for u in range(2):
                read_q(0, u)
            with act.Fori(1, 4) as i:
                for u in range(2):
                    read_q(i, u)

            def read_rows(m):
                slot = m % 2
                if m == 0:
                    act.wait_ge(ik_out, 32)
                    act.wait_ge(index_added, len(INDEX_UNITS))
                if m >= 2:
                    act.wait_ge(kv_out[slot], 32)
                act.wait_ge(kv_t, 3 * m + 1)
                nc.scalar.activation(kv_rows[:, slot, 0:4, :], ps[:, 6, :].rearrange("p (t w) -> p t w", w=P),
                                     ACT.Copy).then_inc(kv_read, 1)
                act.wait_ge(kv_t, 3 * m + 2)
                nc.scalar.activation(kv_rows[:, slot, 4:8, :], ps[:, 7, :].rearrange("p (t w) -> p t w", w=P),
                                     ACT.Copy).then_inc(kv_read, 1)
                act.wait_ge(kv_t, 3 * m + 3)
                nc.scalar.activation(kv_rows[0:T_SAMPLE, slot, 8, :], ps[0:T_SAMPLE, 6, 0:P], ACT.Copy).then_inc(kv_read, 1)

            for m in range(4):
                j = J_K + m
                if m < 2:
                    act.wait_ge(staged[j % 2], 64)
                else:
                    act.wait_ge(staged[j % 2], 80)
                    act.wait_ge(kv_t, 3 * (m - 1))
                read_set(j, stage[:, j % 2, :], ACT.Copy)
                split_w(j % 2, (j + 2) // 2 + 1, 3 * j + 3)
                if m >= 1:
                    read_rows(m - 1)
            read_rows(3)

            def take_cols(dst, i):
                return nc.scalar.activation(dst[:, :].unsqueeze(2), vec[:, :].rearrange(
                    "p (v b) -> p v b", b=KT)[:, :, bass.ds(i, 1)], ACT.Copy)

            def ccol(v):
                return conv_cols[:, v // 8:v // 8 + 1]

            def gcol(v):
                return gate_cols_now[:, v // 8:v // 8 + 1]

            def read_xa(i, s):
                take_cols(conv_cols, i).then_inc(conv_cols_done, 1)
                act.wait_ge(taps, i * 3 + 1)
                read_set(s, padded[:, 3:3 + TP], ACT.Copy)
                act.wait_ge(set_read, s * 3 + 3)
                act.wait_ge(conv_cols_done, i + 1)
                nc.scalar.activation(padded[:, S0:S0 + 3], conv_cols[:, V_SC // 8:V_SC // 8 + 3],
                                     ACT.Copy).then_inc(pad_edge, 1)

            def first_tap(i):
                act.wait_ge(gw_in, i * 32 + 32)
                nc.scalar.activation(gw_hi[:, :, :], gw_raw[:, :, :], ACT.Copy).then_inc(gw_hi_done, 1)
                act.wait_ge(pad_edge, i + 1)
                if not isinstance(i, int) or i > 0:
                    act.wait_ge(gated_u, i)
                nc.scalar.activation(conv[:, :], padded[:, 0:TP], ACT.Identity, bias=ccol(V_CB),
                                     scale=ccol(V_CW)).then_inc(tap0, 1)

            def round_conv(i):
                act.wait_ge(taps, i * 3 + 4)
                nc.scalar.activation(conv_hi[:, :], conv[:, :], ACT.Copy).then_inc(conv_hi_done, 1)

            read_set.parity = S_LRU % 2
            split_w(J_LRU % 2, (J_LRU + 2) // 2 + 1, S_LRU * 3 + 3)
            read_xa(0, S_LRU)
            first_tap(0)
            round_conv(0)

            def lru_step(i, last):
                s0 = i * SETS_PER_STEP + (S_LRU + 1)
                read_set.parity = (S_LRU + 1) % 2
                split_w((J_LRU + 1) % 2, i + ((J_LRU + 3) // 2 + 1), s0 * 3 + 3)
                take_cols(gate_cols_now, i).then_inc(gate_cols_done, 1)
                act.wait_ge(lru, i * 7 + 1)
                read_set(s0, silu_z[:, :], ACT.Silu)
                if last:
                    read_zb(0, s0 + 1)
                    split_w(J_ZB % 2, (J_ZB + 2) // 2 + 1, s0 * 3 + 6)
                else:
                    split_w(J_LRU % 2, i + ((J_LRU + 4) // 2 + 1), s0 * 3 + 6)
                    read_xa(i + 1, s0 + 1)
                act.wait_ge(gate_cols_done, i + 1)
                read_set(s0 + 2, gate_r[:, :], ACT.Sigmoid, bias=gcol(V_BR))
                read_set(s0 + 3, gate_i[:, :], ACT.Sigmoid, bias=gcol(V_BI))
                act.wait_ge(set_read, s0 * 3 + 9)
                nc.scalar.activation(tanh_t[:, :], gate_r[:, :], ACT.Tanh, scale=gcol(V_DECAY))
                nc.scalar.activation(decay_t[:, :], gate_r[:, :], ACT.Exp, scale=gcol(V_DECAY + 8)).then_inc(decays, 1)
                act.wait_ge(decays, i * 2 + 1)
                act.wait_ge(hsq_step, i * 2 + 1)
                nc.scalar.activation(mult[:, :], decay_t[:, :], ACT.Square).then_inc(decays, 1)
                if not last:
                    first_tap(i + 1)
                act.wait_ge(mult_sq, i + 1)
                nc.scalar.activation(mult[:, :], mult[:, :], ACT.Sqrt).then_inc(mult_done, 1)
                if not last:
                    round_conv(i + 1)

            def read_zb(m, s):
                slot = (J_ZB + m) % 2
                act.wait_ge(staged[slot], 16 * (m // 2) + 80)
                read_set(s, stage[:, slot, :], ACT.Silu)

            with act.Fori(0, 7) as i:
                lru_step(i, False)
            lru_step(7, True)

            read_set.parity = (S_ZB + 1) % 2
            for m in range(1, KT):
                if J_ZB + 2 + m < J_END:
                    split_w((J_ZB + m) % 2, (J_ZB + 2 + m) // 2 + 1, 3 * (S_ZB + m) + 3)
                read_zb(m, S_ZB + m)
                if m == 3:
                    act.wait_ge(v_in, 48)
                    nc.scalar.activation(v_hi[:, 0:12, :], v_raw[:, 0:12, :], ACT.Copy).then_inc(v_hi_done, 1)
                    nc.scalar.activation(v_hi[0:T_SAMPLE, 12, :], v_raw[0:T_SAMPLE, 12, :], ACT.Copy).then_inc(v_hi_done, 1)
                if m == 5:
                    act.wait_ge(ssa_ready, 1)
                    nc.scalar.activation(ssq[:, 1, 0:8], ps[:, 6, 0:16:2], ACT.Copy).then_inc(ssa_read, 1)
                    nc.scalar.activation(ssq[0:T_SAMPLE, 1, 8:9], ps[0:T_SAMPLE, 6, 16:17], ACT.Copy).then_inc(ssa_read, 1)
                    act.wait_ge(lasts_ready, 1)
                    nc.scalar.activation(lasts_t[:, :], ps[0:64, 7, 0:P], ACT.Copy).then_inc(lasts_read, 1)
                    act.wait_ge(k_in, 64)
                    for g in range(NKV):
                        act.wait_ge(ck_t, g + 1)
                        nc.scalar.activation(k_raw[:, g, T_PROMPT:T_PROMPT + PAST], ps[:, 6 + g, :], ACT.Copy).then_inc(ck_read, 1)
                    act.wait_ge(ck_read, 2)
                    nc.scalar.activation(k_hi[:, :, :], k_raw[:, :, :], ACT.Copy).then_inc(k_hi_done, 1)

            def split_q(p_):
                i, g = PASSES[p_]
                rows_ = tile_at(i)[1]
                heads = slice(GROUP * g, GROUP * (g + 1))
                act.wait_ge(q_in[g], 16 * (p_ // 2 + 1))
                if p_ >= 2:
                    act.wait_ge(qk_ready, GROUP * (p_ - 1))
                nc.scalar.activation(q_hi[:, heads, 0:rows_], q_raw[:, heads, 0:rows_], ACT.Copy).then_inc(q_hi_done, 1)

            def probs_of(u):
                return probs_a[:, u % 8, :] if u % 8 < 4 else probs_b[:, u % 8 - 4, :]

            split_q(0)
            root(1)
            for kind, n in attention_order():
                if kind == "head":
                    i, g = PASSES[n // GROUP]
                    rows_, keys = tile_at(i)[1], keys_of(i)[1]
                    w = probs_of(n)[0:rows_, 0:keys]
                    act.wait_ge(max_neg, n + 1)
                    nc.scalar.activation(w, w, ACT.Exp, bias=small[0:rows_, 1, n % 8:n % 8 + 1], scale=SM_SCALE,
                                         accum_out=small[0:rows_, 2, n % 8:n % 8 + 1]).then_inc(exp_done, 1)
                    p_ = n // GROUP
                    if n % GROUP == 0 and p_ + 1 < len(PASSES):
                        split_q(p_ + 1)
                    if n % GROUP == GROUP - 1 and p_ < KT:
                        act.wait_ge(wo_in[p_ % 2], 16 * (p_ // 2 + 1))
                        nc.scalar.activation(woa_hi[:, p_, :], wo_raw[:, p_ % 2, :], ACT.Copy).then_inc(wo_hi_done, 1)
                elif kind == "turn":
                    p_, t = TURNS[n]
                    i = PASSES[p_][0]
                    rows_, kr = tile_at(i)[1], key_tiles(i)[t][1]
                    act.wait_ge(turned, n + 1)
                    if n >= 2:
                        act.wait_ge(mixed, n - 1)
                    nc.scalar.activation(pt_hi[0:kr, n % 2, 0:GROUP * rows_], ps[0:kr, 4 + n % 2, 0:GROUP * rows_],
                                         ACT.Copy).then_inc(pt_hi_done, 1)
                elif kind == "out":
                    rows_ = tile_at(PASSES[n][0])[1]
                    act.wait_ge(mixed, TURNS_UPTO[n])
                    if n >= 1:
                        act.wait_ge(osum, 3 * n + 1)
                    nc.scalar.activation(o_sq[:, 0:GROUP * rows_], ps[:, 6 + n % 2, 0:GROUP * rows_], ACT.Square).then_inc(o_sq_done, 1)
            root(2)
            act.wait_ge(pt_lo_done, len(TURNS))
            act.wait_ge(q_lo_done, len(PASSES))
            for k in range(KT, 2 * KT):
                act.wait_ge(wo_in[k % 2], 16 * (k // 2 + 1))
                nc.scalar.activation(wob_hi[:, k - KT, :], wo_raw[:, k % 2, :], ACT.Copy).then_inc(wo_hi_done, 1)
            for b in range(2):
                act.wait_ge(grow_ready, b + 1)
                nc.scalar.activation(gate_rows[:, b, :].rearrange("p (c n) -> p c n", c=2), ps[:, 4 + 2 * b:6 + 2 * b, :],
                                     ACT.Copy).then_inc(grow_read, 1)

            def split_y(e):
                rows_ = tile_at(e // 2)[1]
                act.wait_ge(y_in[e % 2], 16 * (e // 2 + 1))
                if e >= 2:
                    act.wait_ge(proj_ready, e - 1)
                nc.scalar.activation(y_hi[:, e % 2, :, 0:rows_], y_raw[:, e % 2, :, 0:rows_], ACT.Copy).then_inc(y_hi_done, 1)

            split_y(0)
            split_y(1)
            for t in range(NT):
                rows_ = tile_at(t)[1]
                if t + 1 < NT:
                    split_y(2 * t + 2)
                    split_y(2 * t + 3)
                act.wait_ge(out_step, 4 * t + 4)
                nc.scalar.activation(acc[0:rows_, :], y_fin[0:rows_, t % 2, :], ACT.Square,
                                     accum_out=ssq[0:rows_, 0, t:t + 1]).then_inc(fin_sq, 1)
                act.wait_ge(rs_step, 6 * (3 + t) + 1)
                nc.scalar.activation(norm_q[0:rows_, t:t + 1], norm_v[0:rows_, t:t + 1], ACT.Sqrt).then_inc(rs_sqrt, 1)

        @block.tensor
        def _(pe):
            pe.wait_ge(const_done, 3)
            pe.wait_ge(vec_in, 16 * 11)
            nc.tensor.transpose(ps[:, 7, 0:120], vrows[0:120, 0, :], ident[0:120, 0:120])
            nc.tensor.transpose(ps[:, 7, 120:144], vrows[0:24, 1, :], ident[0:24, 0:24]).then_inc(vec_t, 1)
            pe.wait_ge(silc_done, 1)

            def mod_cols(m):
                for k in range(KT):
                    x = nc.tensor.matmul(ps[:, 6, 2 * m:2 * m + 2], w_mod_raw[:, k, P * m:P * (m + 1)], silc[:, k, :],
                                         start=(k == 0), stop=(k == KT - 1))
                return x

            def turn_x(i):
                n = tile_at(i)[1]
                pe.wait_ge(xn_done, i + 1)
                if i >= 3:
                    pe.wait_ge(xt_read, i - 2)
                for k in range(KT):
                    b = 2 * (i % 3) + k // 4
                    x = nc.tensor.transpose(ps[:, b, P * (k % 4):P * (k % 4) + n], x_in[0:n, i, P * k:P * (k + 1)],
                                            ident[0:n, 0:n])
                x.then_inc(xt_ready, 1)

            for m in range(8):
                if m % 4 == 0:
                    pe.wait_ge(wmod_in[m // 4], 16)
                mod_cols(m)
            for i in range(NT):
                turn_x(i)
            for m in range(8, 16):
                if m % 4 == 0:
                    pe.wait_ge(wmod_in[m // 4], 16)
                x = mod_cols(m)
            x.then_inc(mod_ready, 1)

            def project(j, s, slot, width=P, first=False):
                pe.wait_ge(w_lo_done, j + 1)
                for c in range(NCH):
                    if not first:
                        pe.wait_ge(set_read, s * 3 + (c + 1 - 6))
                    out = ps[0:width, 3 * project.parity + c, 0:CH]
                    for k in range(KT):
                        if j_is_zero(j) and c == 0:
                            pe.wait_ge(h_lo_done, k + 1)
                        cols = slice(CH * c, CH * (c + 1))
                        x = split3(k, w_hi[:, slot, k, 0:width], w_lo[:, slot, k, 0:width],
                                   h_hi[:, k, cols], h_lo[:, k, cols], out, k == 0, k == KT - 1)
                    x.then_inc(set_ready, 1)
                project.parity = 1 - project.parity
            project.parity = 0

            def j_is_zero(j):
                return isinstance(j, int) and j == 0

            pe.wait_ge(xt_read, NT)
            project(0, 0, 0, 72, True)
            project(1, 1, 1, P, True)
            pe.wait_ge(cik_in, 16)
            pe.wait_ge(mod_step, 1)
            for t in range(4):
                x = nc.tensor.transpose(ps[0:IDX, 6, P * t:P * (t + 1)], cache_ik[:, t, :], ident[:, :])
            x.then_inc(cik_t, 1)
            pe.wait_ge(set_read, 3)
            pe.wait_ge(vec_done, 1)
            for i in range(NT):
                t0, n = tile_at(i)
                if i == 5:
                    pe.wait_ge(ik_read, 1)
                c = 72 * (i if i < 5 else i - 5)
                x = nc.tensor.transpose(ps[0:n, 7, c:c + 72], stage[0:72, 0, t0:t0 + n], ident[0:72, 0:72])
                if i in (4, NT - 1):
                    x.then_inc(ik_t, 1)
            for m in range(1, 4):
                j = J_IQ + m
                project(j, j, j % 2)
            pe.wait_ge(iq_done, 16)
            pe.wait_ge(ik_parts, 12)
            pe.wait_ge(ik_read, 2)
            for u, (i, h, p_) in enumerate(INDEX_UNITS):
                t0, rows_ = tile_at(i)
                off, n = pieces_of(i)[p_]
                k0 = keys_of(i)[0] + off
                if u >= 2:
                    pe.wait_ge(relu_done, u - 1)
                out = ps[0:rows_, 6 + u % 2, 0:n]
                nc.tensor.matmul(out, iq_parts[:, h, t0:t0 + rows_], ik_hi[:, k0:k0 + n], start=True, stop=False)
                nc.tensor.matmul(out, iq_parts[:, h, t0:t0 + rows_], ik_lo[:, k0:k0 + n], start=False,
                                 stop=True).then_inc(index_ready, 1)
            with pe.Fori(0, 4) as i:
                for u in range(2):
                    project(i * 2 + (J_Q + u), i * 2 + (J_Q + u), (J_Q + u) % 2)

            def turn_rows(m):
                slot = (J_K + m) % 2
                pe.wait_ge(set_read, 3 * (J_K + m) + 3)
                for part, tiles in enumerate((range(0, 4), range(4, 8), (8,))):
                    bank = (6, 7, 6)[part]
                    if part < 2:
                        if m >= 1:
                            pe.wait_ge(kv_read, 3 * m)
                        else:
                            pe.wait_ge(relu_done, len(INDEX_UNITS))
                    else:
                        pe.wait_ge(kv_read, 3 * m + 1)
                    for q, i in enumerate(tiles):
                        t0, n = tile_at(i)
                        x = nc.tensor.transpose(ps[0:n, bank, P * q:P * (q + 1)], stage[:, slot, t0:t0 + n], ident[:, :])
                    x.then_inc(kv_t, 1)

            for m in range(4):
                project(J_K + m, J_K + m, (J_K + m) % 2)
                if m >= 1:
                    turn_rows(m - 1)
            turn_rows(3)

            project.parity = S_LRU % 2
            project(J_LRU, S_LRU, J_LRU % 2)
            pe.wait_ge(kv_read, 12)

            def lru_step(i):
                s0 = i * SETS_PER_STEP + (S_LRU + 1)
                project.parity = (S_LRU + 1) % 2
                project(i * 2 + (J_LRU + 1), s0, (J_LRU + 1) % 2)
                project(i * 2 + (J_LRU + 2), s0 + 1, J_LRU % 2)
                pe.wait_ge(conv_lo_done, i + 1)
                pe.wait_ge(gw_lo_done, i + 1)
                for q in range(2):
                    for c in range(NCH):
                        pe.wait_ge(set_read, s0 * 3 + (3 * q + c + 1))
                        cols = slice(CH * c, CH * (c + 1))
                        split3(0, gw_hi[:, q, :], gw_lo[:, q, :], conv_hi[:, cols], conv_lo[:, cols],
                               ps[:, 3 * project.parity + c, 0:CH], True, True).then_inc(set_ready, 1)
                    project.parity = 1 - project.parity
                pe.wait_ge(wg_in, i * 16 + 16)
                for k in range(KT):
                    x = nc.tensor.matmul(ps[:, 7, bass.ds(i * 2, 2)], wg_raw[:, k, :], silc[:, k, :],
                                         start=(k == 0), stop=(k == KT - 1))
                x.then_inc(gate_ready, 1)

            with pe.Fori(0, 8) as i:
                lru_step(i)
            project.parity = (S_ZB + 1) % 2
            with pe.Fori(0, 2) as i:
                for u in range(2):
                    m = 1 + u
                    project(i * 2 + (J_ZB + m), i * 2 + (S_ZB + m), (J_ZB + m) % 2)

            pe.wait_ge(hsq_step, 17)
            for i in range(NT):
                t0, n = tile_at(i)
                x = nc.tensor.matmul(ps[0:n, 6, 2 * i:2 * i + 2], hsq[:, t0:t0 + n], ones[:, 0:2], start=True, stop=True)
            x.then_inc(ssa_ready, 1)
            pe.wait_ge(lru, 57)
            pe.wait_ge(gate_read, 1)
            nc.tensor.transpose(ps[0:64, 7, 0:P], lasts[:, :, :].rearrange("p v b -> p (v b)"), ident[:, :]).then_inc(lasts_ready, 1)
            project(J_ZB + 5, S_ZB + 5, (J_ZB + 5) % 2)
            pe.wait_ge(ck_in, 16)
            for g in range(NKV):
                pe.wait_ge(ssa_read if g == 0 else lasts_read, 2 if g == 0 else 1)
                for t in range(4):
                    x = nc.tensor.transpose(ps[:, 6 + g, P * t:P * (t + 1)], cache_k_rows[:, t, P * g:P * (g + 1)], ident[:, :])
                x.then_inc(ck_t, 1)
            project(J_ZB + 6, S_ZB + 6, (J_ZB + 6) % 2)
            project(J_ZB + 7, S_ZB + 7, (J_ZB + 7) % 2)
            pe.wait_ge(ck_read, 2)

            def probs_of(u):
                return probs_a[:, u % 8, :] if u % 8 < 4 else probs_b[:, u % 8 - 4, :]

            def diag_of(u):
                return diag_a[:, u % 8, :] if u % 8 < 4 else diag_b[:, u % 8 - 4, :]

            pe.wait_ge(k_lo_done, 1)
            pe.wait_ge(set_read, 3 * (S_ZB + 7) + 3)
            for kind, n in attention_order():
                if kind == "head":
                    p_ = n // GROUP
                    i, g = PASSES[p_]
                    rows_ = tile_at(i)[1]
                    k0, keys = keys_of(i)
                    h = n % 8
                    if n % GROUP == 0:
                        pe.wait_ge(q_lo_done, p_ + 1)
                    if n >= 2:
                        pe.wait_ge(logits, n - 1)
                    for q in range((keys + 511) // 512):
                        off, w = 512 * q, min(512, keys - 512 * q)
                        cols = slice(k0 + off, k0 + off + w)
                        x = split3(0, q_hi[:, h, 0:rows_], q_lo[:, h, 0:rows_], k_hi[:, g, cols], k_lo[:, g, cols],
                                   ps[0:rows_, 2 * (n % 2) + q, 0:w], True, True)
                    x.then_inc(qk_ready, 1)
                elif kind == "turn":
                    p_, t = TURNS[n]
                    i = PASSES[p_][0]
                    rows_, kr = tile_at(i)[1], key_tiles(i)[t][1]
                    pe.wait_ge(diag_ready, GROUP * (p_ + 1))
                    if n >= 2:
                        pe.wait_ge(pt_lo_done, n - 1)
                    for h in range(GROUP):
                        u = GROUP * p_ + h
                        x = nc.tensor.matmul(ps[0:kr, 4 + n % 2, rows_ * h:rows_ * (h + 1)],
                                             probs_of(u)[0:rows_, P * t:P * t + kr], diag_of(u)[0:rows_, 0:rows_],
                                             start=True, stop=True)
                    x.then_inc(turned, 1)
                elif kind == "mix":
                    p_, t = TURNS[n]
                    i, g = PASSES[p_]
                    rows_ = tile_at(i)[1]
                    key, kr = key_tiles(i)[t]
                    if n == 0:
                        pe.wait_ge(v_lo_done, 2)
                    if t == 0 and p_ >= 2:
                        pe.wait_ge(yb_done, p_ - 1)
                    pe.wait_ge(pt_lo_done, n + 1)
                    kt, cols = key // P, slice(P * g, P * (g + 1))
                    split3(0, v_hi[0:kr, kt, cols], v_lo[0:kr, kt, cols], pt_hi[0:kr, n % 2, 0:GROUP * rows_],
                           pt_lo[0:kr, n % 2, 0:GROUP * rows_], ps[:, 6 + p_ % 2, 0:GROUP * rows_],
                           t == 0, t == len(key_tiles(i)) - 1).then_inc(mixed, 1)
            pe.wait_ge(osum, 3 * len(PASSES) + 1)
            for i in range(NT):
                t0, n = tile_at(i)
                x = nc.tensor.matmul(ps[0:n, 0, 2 * i:2 * i + 2], hsq[:, t0:t0 + n], ones[:, 0:2], start=True, stop=True)
            x.then_inc(ssb_ready, 1)

            for b in range(2):
                pe.wait_ge(diag_done, 8 * (b + 1))
                src = acc if b == 0 else y_fin[:, 0, :]
                if b == 1:
                    pe.wait_ge(yb_done, len(PASSES))
                for k in range(KT):
                    x = nc.tensor.matmul(ps[:, 4 + 2 * b + k // 4, P * (k % 4):P * (k % 4 + 1)], ones[:, :],
                                         src[:, P * k:P * (k + 1)], start=True, stop=True)
                x.then_inc(grow_ready, 1)

            for e in range(2 * NT):
                t, half = e // 2, e % 2
                rows_ = tile_at(t)[1]
                wh, wl = (woa_hi, woa_lo) if half == 0 else (wob_hi, wob_lo)
                pe.wait_ge(y_lo_done, e + 1)
                if e == 0:
                    pe.wait_ge(ssb_read, 2)
                    pe.wait_ge(wo_lo_done, KT)
                if e == 1:
                    pe.wait_ge(wob_lo_done, KT)
                if e in (2, 3):
                    pe.wait_ge(grow_read, e - 1)
                if e >= 4:
                    pe.wait_ge(out_step, 4 * (t - 1))
                for k in range(KT):
                    for q in range(2):
                        cols = slice(512 * q, 512 * (q + 1))
                        x = split3(k, y_hi[:, e % 2, k, 0:rows_], y_lo[:, e % 2, k, 0:rows_], wh[:, k, cols], wl[:, k, cols],
                                   ps[0:rows_, 2 * (e % 4) + q, :], k == 0, k == KT - 1)
                x.then_inc(proj_ready, 1)

        @block.vector
        def _(dve):
            V = nc.vector
            V.memset(ssq[:, :, :], 1.0).then_inc(init_done, 1)
            dve.wait_ge(vec_t, 1)
            V.tensor_copy(vec[:, 0:V_DECAY], ps[:, 7, 0:V_DECAY]).then_inc(vec_done, 1)
            dve.wait_ge(vec_done, 1)

            def inv_rms(n, src, dst, rows_=P, cols=slice(0, NT)):
                v, q, t = norm_v[0:rows_, cols], norm_q[0:rows_, cols], norm_t[0:rows_, cols]
                src, dst = src[0:rows_, cols], dst[0:rows_, cols]
                V.tensor_scalar(v, src, 1.0 / D, EPS, ALU.mult, ALU.add).then_inc(rs_step, 1)
                dve.wait_ge(rs_sqrt, n + 1)
                V.reciprocal(dst, q).then_inc(rs_step, 1)
                dve.wait_ge(rs_step, 6 * n + 2)
                V.tensor_tensor(t, dst, dst, ALU.mult).then_inc(rs_step, 1)
                dve.wait_ge(rs_step, 6 * n + 3)
                V.tensor_tensor(t, t, v, ALU.mult).then_inc(rs_step, 1)
                dve.wait_ge(rs_step, 6 * n + 4)
                V.tensor_scalar(t, t, -0.5, 1.5, ALU.mult, ALU.add).then_inc(rs_step, 1)
                dve.wait_ge(rs_step, 6 * n + 5)
                V.tensor_tensor(dst, dst, t, ALU.mult).then_inc(rs_step, 1)
                dve.wait_ge(rs_step, 6 * n + 6)

            dve.wait_ge(sq_done, NT)
            inv_rms(0, ssq[:, 0, :], rstd[:, 0, :])
            for i in range(NT):
                n = tile_at(i)[1]
                V.tensor_scalar(x_in[0:n, i, :], x_in[0:n, i, :], rstd[0:n, 0, i:i + 1], None, ALU.mult).then_inc(xn_done, 1)
            dve.wait_ge(soft_act, 2)
            steps = [0]

            def soft_next(ins):
                steps[0] += 1
                ins.then_inc(soft_step, 1)
                dve.wait_ge(soft_step, steps[0])

            e_, s_, q_, p_ = (soft[:, n, :] for n in range(4))
            soft_next(V.tensor_scalar(s_, e_, 2.0, None, ALU.add))
            soft_next(V.reciprocal(s_, s_))
            soft_next(V.tensor_tensor(s_, s_, e_, ALU.mult))
            soft_next(V.tensor_tensor(q_, s_, s_, ALU.mult))
            soft_next(V.tensor_scalar(p_, q_, 1.0 / 15, None, ALU.mult))
            for d in (13, 11, 9, 7, 5, 3):
                soft_next(V.scalar_tensor_tensor(p_, p_, 1.0 / d, q_, ALU.add, ALU.mult))
            soft_next(V.scalar_tensor_tensor(p_, p_, 1.0, s_, ALU.add, ALU.mult))
            soft_next(V.tensor_scalar(q_, vec[:, V_LAM:V_LAM + 8], -1.0, 0.0, ALU.mult, ALU.max))
            soft_next(V.scalar_tensor_tensor(p_, p_, 2.0, q_, ALU.mult, ALU.add))
            soft_next(V.tensor_scalar(vec[:, V_DECAY:V_DECAY + 8], p_, 8.0, None, ALU.mult))
            soft_next(V.tensor_scalar(vec[:, V_DECAY + 8:V_DECAY + 16], p_, -8.0, None, ALU.mult))

            dve.wait_ge(mod_ready, 1)
            V.tensor_tensor(mod[:, :, :], ps[:, 6, 0:32].rearrange("p (m b) -> p m b", b=2),
                            vec[:, 0:16].unsqueeze(2).broadcast_to([P, 16, 2]), ALU.add).then_inc(mod_step, 1)
            dve.wait_ge(mod_step, 1)
            V.scalar_tensor_tensor(shiftscale[:, :, :], mod[:, 8:16, :], 1.0,
                                   vec[:, V_GN:V_GN + 8].unsqueeze(2).broadcast_to([P, 8, 2]),
                                   ALU.add, ALU.mult).then_inc(mod_step, 1)
            dve.wait_ge(mod_step, 2)
            dve.wait_ge(xt_read, NT)
            dve.wait_ge(const_done, 3)

            def h_low(k):
                dve.wait_ge(h_hi_done, k + 1)
                V.tensor_tensor(h_lo[:, k, :], x_t[:, k, :], f32(h_hi[:, k, :]), ALU.subtract).then_inc(h_lo_done, 1)

            for k in range(KT):
                for b, cols in ((0, slice(0, S0)), (1, slice(S0, TP))):
                    V.tensor_scalar(x_t[:, k, cols], x_t[:, k, cols], shiftscale[:, k, b:b + 1], mod[:, k, b:b + 1],
                                    ALU.mult, ALU.add).then_inc(h_full, 1)
                if k >= 1:
                    h_low(k - 1)
            h_low(KT - 1)

            dve.wait_ge(cik_t, 1)
            dve.wait_ge(set_read, 3)
            n_ik = 0
            for src, k0, n in ((stage[0:IDX, 0, 0:T_PROMPT], 0, T_PROMPT), (ps[0:IDX, 6, :], T_PROMPT, PAST),
                               (stage[0:IDX, 0, S0:TP], T_PROMPT + PAST, T_SAMPLE)):
                cols = slice(k0, k0 + n)
                V.tensor_copy(ik_hi[0:IDX, cols], src).then_inc(ik_parts, 1)
                V.tensor_copy(ik_hi[IDX:P, cols], src).then_inc(ik_parts, 1)
                dve.wait_ge(ik_parts, n_ik + 1)
                V.tensor_tensor(ik_lo[0:IDX, cols], src, f32(ik_hi[0:IDX, cols]), ALU.subtract).then_inc(ik_parts, 1)
                V.tensor_tensor(ik_lo[IDX:P, cols], src, f32(ik_hi[0:IDX, cols]), ALU.subtract).then_inc(ik_parts, 1)
                n_ik += 4
            dve.wait_ge(ik_read, 2)
            V.tensor_scalar(iw[:, 0:8, :], ikw_rows[:, 0:8, IDX:72], IW_SCALE, None, ALU.mult).then_inc(iw_done, 1)
            V.tensor_scalar(iw[0:T_SAMPLE, 8, :], ikw_rows[0:T_SAMPLE, 8, IDX:72], IW_SCALE, None, ALU.mult).then_inc(iw_done, 1)

            lower, upper = slice(0, IDX), slice(IDX, P)
            for m in range(4):
                j = J_IQ + m
                src = stage[:, j % 2, :]
                dve.wait_ge(set_read, 3 * j + 3)
                V.tensor_copy(iq_parts[lower, 2 * m, :], src[lower]).then_inc(iq_done, 1)
                V.tensor_copy(iq_parts[upper, 2 * m + 1, :], src[upper]).then_inc(iq_done, 1)
                dve.wait_ge(iq_done, 4 * m + 2)
                V.tensor_tensor(iq_parts[upper, 2 * m, :], src[lower], f32(iq_parts[lower, 2 * m, :]),
                                ALU.subtract).then_inc(iq_done, 1)
                V.tensor_tensor(iq_parts[lower, 2 * m + 1, :], src[upper], f32(iq_parts[upper, 2 * m + 1, :]),
                                ALU.subtract).then_inc(iq_done, 1)

            dve.wait_ge(iw_done, 2)
            for u, (i, h, p_) in enumerate(INDEX_UNITS):
                rows_ = tile_at(i)[1]
                off, n = pieces_of(i)[p_]
                out = scores[0:rows_, score_at(i) + off:score_at(i) + off + n]
                dve.wait_ge(relu_done, u + 1)
                if h == 0:
                    x = V.tensor_scalar(out, relu[0:rows_, u % 3, 0:n], iw[0:rows_, i, h:h + 1], None, ALU.mult)
                else:
                    dve.wait_ge(index_added, u - len(pieces_of(i)) + 1)
                    x = V.scalar_tensor_tensor(out, relu[0:rows_, u % 3, 0:n], iw[0:rows_, i, h:h + 1], out,
                                               ALU.mult, ALU.add)
                x.then_inc(index_added, 1)
            dve.wait_ge(index_added, len(INDEX_UNITS))
            for i in ROUND_ONE_TILES:
                end = score_at(i) + P * (i + 1)
                V.memset(scores[0:CHUNK, end - CHUNK:end], NEG).then_inc(masked, 1)
            dve.wait_ge(masked, len(ROUND_ONE_TILES))

            def select_round(tiles, before):
                w = {i: (scores[0:tile_at(i)[1], score_at(i):score_at(i) + keys_of(i)[1]],
                         best[0:tile_at(i)[1], min(i, 8) - 2, :]) for i in tiles}
                dve.wait_ge(select, before)
                V.memset(held, 0.0)
                for i in tiles:
                    V.max(w[i][1], w[i][0]).then_inc(select, 1)
                dve.wait_ge(select, before + len(tiles))
                V.memset(held, 0.0)
                for i in tiles:
                    V.match_replace(w[i][0], w[i][1], w[i][0], TAKEN).then_inc(select, 1)

            V.memset(soft[:, 3, 0:1], 0.0).then_inc(select, 1)
            with dve.Fori(0, Q_ROUNDS) as i:
                select_round(INDEX_TILES, i * 14 + 1)
            with dve.Fori(0, SHARED_ROUNDS - Q_ROUNDS) as i:
                select_round((8,), i * 2 + (14 * Q_ROUNDS + 1))
            n_select = 1 + 14 * Q_ROUNDS + 2 * (SHARED_ROUNDS - Q_ROUNDS)

            V.memset(padded[:, 0:3], 0.0).then_inc(taps, 1)
            V.memset(soft[:, 1, 0:1], 0.0).then_inc(lru, 1)
            V.memset(soft[:, 2, 0:1], 0.0).then_inc(ya_out, 1)

            def col(v, i):
                return vec[:, bass.ds(i + v, 1)]

            def other_taps(i):
                dve.wait_ge(tap0, i + 1)
                V.tensor_copy(lasts[:, 0:3, bass.ds(i, 1)], padded[:, T_PROMPT:T_PROMPT + 3].unsqueeze(2))
                V.tensor_copy(lasts[:, 3:6, bass.ds(i, 1)], padded[:, TP:TP + 3].unsqueeze(2))
                for j in range(1, 4):
                    V.scalar_tensor_tensor(conv[:, :], padded[:, j:j + TP], col(V_CW + 8 * j, i), conv[:, :],
                                           ALU.mult, ALU.add).then_inc(taps, 1)
                    dve.wait_ge(taps, i * 3 + (j + 1))

            def lru_step(i, last):
                select_round(EARLY, i * PER_STEP + n_select)
                dve.wait_ge(decays, i * 2 + 2)
                V.scalar_tensor_tensor(mult[:, :], mult[:, :], 1.0, tanh_t[:, :], ALU.add, ALU.mult).then_inc(mult_sq, 1)
                if not last:
                    other_taps(i + 1)
                dve.wait_ge(mult_done, i + 1)
                V.memset(mult[:, 0:1], 1.0).then_inc(lru, 1)
                V.memset(decay_t[:, S0 - 1:S0], 0.0).then_inc(lru, 1)
                dve.wait_ge(gated_u, i + 1)
                dve.wait_ge(lru, i * 7 + 3)
                V.tensor_tensor(mult[:, :], mult[:, :], gate_i[:, :], ALU.mult).then_inc(lru, 1)
                dve.wait_ge(lru, i * 7 + 4)
                V.tensor_copy(mult[:, S0 - 1:S0], col(V_H0, i)).then_inc(lru, 1)
                dve.wait_ge(lru, i * 7 + 5)
                dve.wait_ge(hsq_step, i * 2 + 1)
                V.tensor_tensor_scan(hidden[:, :], decay_t[:, :], mult[:, :], 0.0, ALU.mult, ALU.add).then_inc(lru, 1)
                dve.wait_ge(lru, i * 7 + 6)
                V.tensor_copy(lasts[:, 6:8, bass.ds(i, 1)],
                              hidden[:, T_PROMPT - 1:TP:TP - T_PROMPT].unsqueeze(2)).then_inc(lru, 1)
                dve.wait_ge(ya_out, i * 16 + 1)
                V.scalar_tensor_tensor(y_a[:, :], hidden[:, :], col(V_GA, i), silu_z[:, :], ALU.mult, ALU.mult).then_inc(lru, 1)
                done = 2 * len(EARLY)
                for tiles in LATE:
                    select_round(tiles, i * PER_STEP + (n_select + done))
                    done += 2 * len(tiles)

            other_taps(0)
            with dve.Fori(0, 7) as i:
                lru_step(i, False)
            lru_step(7, True)
            n_select += PER_STEP * KT
            dve.wait_ge(gate_ready, KT)
            V.tensor_tensor(gate_cols[:, :, :], ps[:, 7, 0:16].rearrange("p (m b) -> p m b", b=2),
                            vec[:, V_GATE:V_GATE + 8].unsqueeze(2).broadcast_to([P, 8, 2]), ALU.add).then_inc(gate_read, 1)
            left = {i: TOPK_ROUNDS - Q_ROUNDS - KT * sum(i in tiles for tiles in (EARLY, *LATE)) for i in ROUND_ONE_TILES}
            few = min(left.values())
            with dve.Fori(0, few) as i:
                select_round(ROUND_ONE_TILES, i * 12 + n_select)
            n_select += 12 * few
            others = tuple(i for i in ROUND_ONE_TILES if left[i] > few)
            with dve.Fori(0, max(left.values()) - few) as i:
                select_round(others, i * (2 * len(others)) + n_select)
            n_select += 2 * len(others) * (max(left.values()) - few)

            dve.wait_ge(ssa_read, 2)
            inv_rms(1, ssq[:, 1, :], rstd[:, 1, :])

            dve.wait_ge(kv_out[0], 64)
            dve.wait_ge(kv_out[1], 64)
            dve.wait_ge(ya_out, 129)
            dve.wait_ge(select, n_select)
            n0 = bias_at(2)
            V.memset(bias[:, 0:n0], 0.0).then_inc(bias_done, 1)
            dve.wait_ge(bias_done, 1)
            for i in (0, 1):
                end = bias_at(i) + P * (i + 1)
                V.memset(bias[0:CHUNK, end - CHUNK:end], BIAS).then_inc(bias_done, 1)
            V.tensor_scalar(bias[:, n0:bias_at(8)], scores[:, 0:score_at(8)], TAKEN, BIAS,
                            ALU.not_equal, ALU.mult).then_inc(bias_done, 1)
            V.tensor_scalar(bias[0:T_SAMPLE, bias_at(8):], scores[0:T_SAMPLE, score_at(8):], TAKEN, BIAS,
                            ALU.not_equal, ALU.mult).then_inc(bias_done, 1)
            dve.wait_ge(bias_done, 5)
            def probs_of(u):
                return probs_a[:, u % 8, :] if u % 8 < 4 else probs_b[:, u % 8 - 4, :]

            def diag_of(u):
                return diag_a[:, u % 8, :] if u % 8 < 4 else diag_b[:, u % 8 - 4, :]

            def invert(u):
                r = tile_at(PASSES[u // GROUP][0])[1]
                dve.wait_ge(exp_done, u + 1)
                V.reciprocal(small[0:r, 3, u % 8:u % 8 + 1], small[0:r, 2, u % 8:u % 8 + 1]).then_inc(inv_done, 1)
                dve.wait_ge(inv_done, u + 1)
                V.tensor_scalar(diag_of(u)[0:r, 0:r], ident[0:r, 0:r], small[0:r, 3, u % 8:u % 8 + 1], None,
                                ALU.mult).then_inc(diag_ready, 1)

            waiting = []
            for kind, n in attention_order():
                if kind == "head":
                    p_ = n // GROUP
                    i, g = PASSES[p_]
                    rows_, keys = tile_at(i)[1], keys_of(i)[1]
                    dve.wait_ge(qk_ready, n + 1)
                    if n >= 8:
                        dve.wait_ge(turned, TURNS_UPTO[p_ - 2])
                    b = 2 * (n % 2)
                    src = ps[0:rows_, b:b + 2, :].rearrange("p b n -> p (b n)")[:, 0:keys]
                    c = n % 8
                    V.tensor_tensor_reduce(probs_of(n)[0:rows_, 0:keys], src, bias[0:rows_, bias_at(i):bias_at(i) + keys],
                                           1.0, NEG, ALU.add, ALU.max, small[0:rows_, 0, c:c + 1]).then_inc(logits, 1)
                    dve.wait_ge(logits, n + 1)
                    V.tensor_scalar(small[0:rows_, 1, c:c + 1], small[0:rows_, 0, c:c + 1], -SM_SCALE, None,
                                    ALU.mult).then_inc(max_neg, 1)
                    for u in waiting:
                        invert(u)
                    waiting = [n]
                elif kind == "turn":
                    p_, t = TURNS[n]
                    i = PASSES[p_][0]
                    rows_, kr = tile_at(i)[1], key_tiles(i)[t][1]
                    for u in waiting:
                        invert(u)
                    waiting = []
                    dve.wait_ge(pt_hi_done, n + 1)
                    V.tensor_tensor(pt_lo[0:kr, n % 2, 0:GROUP * rows_], ps[0:kr, 4 + n % 2, 0:GROUP * rows_],
                                    f32(pt_hi[0:kr, n % 2, 0:GROUP * rows_]), ALU.subtract).then_inc(pt_lo_done, 1)
                elif kind == "out":
                    i, g = PASSES[n]
                    rows_ = tile_at(i)[1]
                    dve.wait_ge(o_sq_done, n + 1)
                    dve.wait_ge(zb_in[g], 16 * (n // 2 + 1))
                    if n >= 1:
                        dve.wait_ge(yb_out, 16 * n)
                    V.tensor_tensor(y_b[:, 0:GROUP * rows_].rearrange("p (h t) -> p h t", h=GROUP),
                                    ps[:, 6 + n % 2, 0:GROUP * rows_].rearrange("p (h t) -> p h t", h=GROUP),
                                    silu_zb[:, GROUP * g:GROUP * (g + 1), 0:rows_], ALU.mult).then_inc(yb_done, 1)
            dve.wait_ge(ssb_ready, 1)
            V.tensor_copy(ssq[:, 2, 0:8], ps[:, 0, 0:16:2]).then_inc(ssb_read, 1)
            V.tensor_copy(ssq[0:T_SAMPLE, 2, 8:9], ps[0:T_SAMPLE, 0, 16:17]).then_inc(ssb_read, 1)
            dve.wait_ge(ssb_read, 2)
            inv_rms(2, ssq[:, 2, :], rstd[:, 2, :])

            dve.wait_ge(turned, len(TURNS))
            dve.wait_ge(mixed, len(TURNS))
            for b in range(2):
                dst = acc if b == 0 else y_fin[:, 0, :]
                for k in range(KT):
                    V.tensor_scalar(dst[:, P * k:P * (k + 1)], ident[:, :], gate_cols[:, k, b:b + 1], None,
                                    ALU.mult).then_inc(diag_done, 1)
            for k in range(KT):
                dve.wait_ge(wo_hi_done, KT + k + 1)
                V.tensor_tensor(wob_lo[:, k, :], wo_raw[:, k % 2, :], f32(wob_hi[:, k, :]), ALU.subtract).then_inc(wob_lo_done, 1)
            dve.wait_ge(gf_in, 16)
            dve.wait_ge(grow_read, 2)
            for t in range(NT):
                rows_ = tile_at(t)[1]
                r = slice(0, rows_)

                def banks(e):
                    return ps[r, 2 * (e % 4):2 * (e % 4) + 2, :].rearrange("p b n -> p (b n)")

                y = y_fin[r, t % 2, :]
                dve.wait_ge(proj_ready, 2 * t + 1)
                if t >= 1:
                    dve.wait_ge(fin_sq, t)
                V.tensor_scalar(acc[r, :], banks(2 * t), rstd[r, 1, t:t + 1], None, ALU.mult).then_inc(out_step, 1)
                dve.wait_ge(proj_ready, 2 * t + 2)
                dve.wait_ge(out_step, 4 * t + 1)
                V.scalar_tensor_tensor(acc[r, :], banks(2 * t + 1), rstd[r, 2, t:t + 1], acc[r, :],
                                       ALU.mult, ALU.add).then_inc(out_step, 1)
                dve.wait_ge(out_step, 4 * t + 2)
                V.tensor_tensor(acc[r, :], acc[r, :], gate_rows[r, 0 if t < NT - 1 else 1, :], ALU.mult).then_inc(out_step, 1)
                dve.wait_ge(out_step, 4 * t + 3)
                dve.wait_ge(xres_in[t % 2], 16 * (t // 2 + 1))
                if t >= 2:
                    dve.wait_ge(y_out[t % 2], 16 * (t // 2))
                V.tensor_tensor(y, acc[r, :], x_res[r, t % 2, :], ALU.add).then_inc(out_step, 1)
                dve.wait_ge(fin_sq, t + 1)
                inv_rms(3 + t, ssq[:, 0, :], rstd[:, 0, :], rows_, slice(t, t + 1))
                V.scalar_tensor_tensor(y, y, rstd[r, 0, t:t + 1], gf_rows[r, :], ALU.mult, ALU.mult).then_inc(fin_done, 1)


TURNS_UPTO = [sum(len(key_tiles(i)) for i, _ in PASSES[:p + 1]) for p in range(len(PASSES))]

_INS = ["x_prompt", "x_sample", "c_prompt", "c_sample", "cache_k", "cache_v", "cache_idx_k", "state_lru_h",
        "state_conv", "w_mod", "b_mod", "g_norm", "w_in", "conv_w", "conv_b", "w_r", "b_r", "w_i", "b_i",
        "lru_lambda", "g_a", "g_b", "w_out", "g_final"]
_OUTS = [("y_prompt", (1, T_PROMPT, D)), ("y_sample", (1, T_SAMPLE, D)),
         ("k_prompt", (1, 1, T_PROMPT, NKV, P)), ("v_prompt", (1, 1, T_PROMPT, NKV, P)),
         ("ik_prompt", (1, 1, T_PROMPT, IDX)), ("h_prompt", (1, 1, D)), ("conv_prompt", (1, 1, 3, D)),
         ("k_sample", (1, 1, T_SAMPLE, NKV, P)), ("v_sample", (1, 1, T_SAMPLE, NKV, P)),
         ("ik_sample", (1, 1, T_SAMPLE, IDX)), ("h_sample", (1, 1, D)), ("conv_sample", (1, 1, 3, D))]


def kernel(**inputs):
    import concourse.bacc as bacc
    from concourse.bass_utils import run_bass_kernel_spmd

    nc = bacc.Bacc("TRN2", target_bir_lowering=False, num_devices=1)
    arrays, aps = {}, {}
    for name in _INS:
        x = np.ascontiguousarray(inputs[name])
        arrays[f"in_{name}"] = x
        aps[name] = nc.dram_tensor(f"in_{name}", x.shape, mybir.dt.from_np(x.dtype), kind="ExternalInput").ap()
    for name, shape in _OUTS:
        aps[name] = nc.dram_tensor(f"out_{name}", shape, F32, kind="ExternalOutput").ap()
    build(nc, aps)
    r = run_bass_kernel_spmd(nc, [arrays], core_ids=[0])
    return tuple(r.results[0][f"out_{name}"] for name, _ in _OUTS)
```

```python
import concourse.bass as bass
import concourse.mybir as mybir
import numpy as np
from concourse.alu_op_type import AluOpType as ALU

F32 = mybir.dt.float32
F32R = mybir.dt.float32r
BF16 = mybir.dt.bfloat16
ACT = mybir.ActivationFunctionType

P = 128
D = 1024
KT = D // P
T_PROMPT = 1024
T_SAMPLE = 64
S0 = T_PROMPT + 4
TP = S0 + T_SAMPLE
NCH = 3
CH = TP // NCH
CHUNK = 64
PAST = 512
NKEY = T_PROMPT + PAST + T_SAMPLE
NH, NKV, GROUP = 8, 2, 4
IDX = 64
TOPK_P, TOPK_S = 256, 144
EPS = 1e-6
NEG = -3.4028234663852886e38
TAKEN = -3.0e38
BIAS = -1.0e30
SM_SCALE = P ** -0.5
IW_SCALE = (NH * IDX) ** -0.5
NT = 9
ROUND_ONE_TILES = (7, 6, 5, 4, 3, 2)

XA, ZA, QQ, KK, VV, ZB, IQ, IK = 0, 1024, 2048, 3072, 3328, 3584, 4608, 5120

V_SHIFT, V_SCALE, V_GATE, V_GN, V_CW, V_CB, V_LAM, V_BR, V_BI, V_GA, V_GB, V_H0, V_SC, V_DECAY, NVEC = (
    0, 8, 16, 24, 32, 64, 72, 80, 88, 96, 104, 112, 120, 144, 160)

J_IQ, J_Q, J_K, J_V, J_LRU, J_ZB, J_END = 1, 5, 13, 15, 17, 33, 41
S_LRU, S_ZB = 17, 49
SETS_PER_STEP = 4


def tile_at(i):
    return (i * P, P) if i < NT - 1 else (S0, T_SAMPLE)


def keys_of(i):
    return (0, P * (i + 1)) if i < NT - 1 else (T_PROMPT, PAST + T_SAMPLE)


def pieces_of(i):
    n = keys_of(i)[1]
    if n <= 512:
        return [(0, n)]
    return [(0, n // 2), (n // 2, n - n // 2)]


def score_at(i):
    if i == NT - 1:
        return sum(P * (t + 1) for t in range(2, 8))
    return sum(P * (t + 1) for t in range(2, i))


def bias_at(i):
    return sum(P * (t + 1) for t in range(min(i, NT - 1)))


SCORES = score_at(NT - 1) + PAST + T_SAMPLE
BIASES = bias_at(NT - 1) + PAST + T_SAMPLE

INDEX_TILES = (7, 6, 5, 4, 3, 2, 8)
POOL_TILES = (3, 8)


def index_units():
    parts = [[(i, h, p) for i in INDEX_TILES if (i in POOL_TILES) == pool for h in range(NH)
              for p in range(len(pieces_of(i)))] for pool in (False, True)]
    spread = [((n + 0.5) / len(part), unit) for part in parts for n, unit in enumerate(part)]
    return [unit for _, unit in sorted(spread)]


INDEX_UNITS = index_units()


def units_before(u):
    pool = INDEX_UNITS[u][0] in POOL_TILES
    return sum((i in POOL_TILES) == pool for i, _, _ in INDEX_UNITS[:u])


POOL_UNITS = sum(i in POOL_TILES for i, _, _ in INDEX_UNITS)
DVE_UNITS = len(INDEX_UNITS) - POOL_UNITS

Q_INSIDE = 2
Q_STEPS = [(b, c, k) for b in range(Q_INSIDE) for c in range(NCH) for k in range(KT)]


def q_step_after(u):
    return Q_STEPS[u // 2] if u % 2 and u // 2 < len(Q_STEPS) else None


PASSES = [(i, g) for i in (2, 8, 3, 4, 5, 6, 7, 1, 0) for g in range(NKV)]
SMALL_PASS = PASSES.index((1, 0))


def key_tiles(i):
    k0, n = keys_of(i)
    return [(k0 + P * t, min(P, n - P * t)) for t in range((n + P - 1) // P)]


OUT_ORDER = [(0, 0), (1, 0), (2, 0), (3, 0), (0, 1), (1, 1)]
for _t in range(4, NT):
    OUT_ORDER += [(_t, 0), (_t - 2, 1)]
OUT_ORDER += [(NT - 2, 1), (NT - 1, 1)]
WO_PASS = 4
INSIDE = 2
FILL_AFTER = {SMALL_PASS: 1, SMALL_PASS + 1: 2, SMALL_PASS + 2: 2, SMALL_PASS + 3: 4}
FILL_BEFORE = {SMALL_PASS + 1: 1, SMALL_PASS + 2: 3}


def attention_order():
    steps = [("head", u) for u in range(GROUP)] + [("turn", 0)]
    x = fills = 0

    def fill(n):
        nonlocal fills
        for _ in range(min(n, INSIDE * KT - fills)):
            steps.append(("fill", fills))
            fills += 1
            if fills % KT == 0:
                steps.append(("take", fills // KT - 1))
                steps.append(("prep", INSIDE + fills // KT - 1))

    for a, (i, g) in enumerate(PASSES):
        kts = len(key_tiles(i))
        more = a + 1 < len(PASSES)
        heads = [("head", u) for u in range(GROUP * (a + 1), GROUP * (a + 2))] if more else []
        at_once = -(-GROUP // max(1, kts - 2))
        for t in range(kts):
            last = t == kts - 1
            if last:
                steps += heads
                heads = []
                fill(FILL_BEFORE.get(a, 0))
            if more or not last:
                steps.append(("turn", x + 1))
                if a == SMALL_PASS - 1 and last:
                    steps.append(("prep", 0))
                if a == SMALL_PASS and last:
                    steps.append(("prep", 1))
            steps.append(("mix", x))
            x += 1
            steps += heads[:at_once]
            heads = heads[at_once:]
            fill(FILL_AFTER.get(a, 0))
        if not more:
            fill(INSIDE * KT)
        steps.append(("out", a))
    return steps


TURNS = [(a, t) for a, (i, g) in enumerate(PASSES) for t in range(len(key_tiles(i)))]

MOD_CHUNKS = 8
MOD_CH = 2 * D // MOD_CHUNKS
DVE_CHUNKS = (3, 4)
PE_CHUNKS = tuple(m for m in range(MOD_CHUNKS) if m not in DVE_CHUNKS)
DVE_COLS = slice(MOD_CH * DVE_CHUNKS[0], MOD_CH * (DVE_CHUNKS[-1] + 1))
EARLY_TILES = (0, 1, 2, 3)
LATE_TILES = (4, 5, 6, 7, 8)
POOL_LOW = (2, 5)

SHARED_ROUNDS = TOPK_S // 8
Q_ROUNDS = 12
TOPK_ROUNDS = TOPK_P // 8
LAST_ROUNDS = 3
FIRST_TILES = (7, 6)
FIRST_ROUNDS = (7, 7, 7, 6, 6, 6)
FIRST_SELECTION = 1 + max(units_before(u) for u, (i, _, _) in enumerate(INDEX_UNITS) if i in FIRST_TILES)
BEFORE_LRU = (ROUND_ONE_TILES, (5, 4, 3, 2))
EARLY = (5, 4, 3, 2)
LATE = ((7, 6), (7, 6, 3, 2))
PER_STEP = 2 * (len(EARLY) + sum(len(tiles) for tiles in LATE))


def build(nc, a):
    def sem(name):
        return nc.alloc_semaphore(name)

    base = (nc.sbuf_base + 31) // 32 * 32

    def at(name, shape, dt, off):
        return nc.alloc_sbuf_tensor_at(name, shape, dt, offset=off)

    def nbytes(shape, dt):
        n = 2 if dt == BF16 else 4
        for s in shape[1:]:
            n *= s
        return (n + 31) // 32 * 32

    class Zone:

        def __init__(self, start):
            self.start = self.end = start

        def take(self, name, shape, dt):
            t = at(name, shape, dt, self.end)
            self.end += nbytes(shape, dt)
            assert self.end <= nc.sbuf_usable_end, (name, self.end)
            return t

    keep = Zone(base)
    ident = keep.take("ident", [P, P], F32)
    ones = keep.take("ones", [P, P], F32)
    vec = keep.take("vec", [P, NVEC], F32)
    mod = keep.take("mod", [P, 16, 2], F32)
    shiftscale = keep.take("shiftscale", [P, KT, 2], F32)
    gate_cols = keep.take("gate_cols", [P, KT, 2], F32)
    silc = keep.take("silc", [P, KT, 2], F32)
    craw = keep.take("craw", [P, 2, KT], F32)
    conv_cols = keep.take("conv_cols", [P, NVEC // 8], F32)
    gate_cols_now = keep.take("gate_cols_now", [P, NVEC // 8], F32)
    soft = keep.take("soft", [P, 4, KT], F32)
    ssq = keep.take("ssq", [P, 3, NT], F32)
    norm_v = keep.take("norm_v", [P, NT], F32)
    norm_q = keep.take("norm_q", [P, NT], F32)
    norm_t = keep.take("norm_t", [P, NT], F32)
    rstd = keep.take("rstd", [P, 3, NT], F32)
    iw = keep.take("iw", [P, NT, NH], F32)
    small = keep.take("small", [P, 4, 8], F32)
    best = keep.take("best", [P, 7, 8], F32)
    held = soft[:, 0, 0:1]
    lasts = keep.take("lasts", [P, 8, 8], F32)
    lasts_t = keep.take("lasts_t", [64, P], F32)
    hsq = keep.take("hsq", [P, TP], F32)
    zone_scores = keep.end
    scores = keep.take("scores", [P, SCORES], F32)

    zone_h = keep.end
    zh = Zone(zone_h)
    h_hi = zh.take("h_hi", [P, KT, TP], F32R)
    h_lo = zh.take("h_lo", [P, KT, TP], F32R)
    z = Zone(zone_scores)
    x_diags = z.take("x_diags", [P, NT, P], F32)
    mod_rows = z.take("mod_rows", [P, 2 * D], F32)
    mod_acc = z.take("mod_acc", [P, 2, MOD_CH * len(DVE_CHUNKS)], F32)
    w_mod_raw = at("w_mod_raw", [P, KT, 2 * D], F32, zone_h)

    zone_w = zh.end
    zw = Zone(zone_w)
    w_raw = zw.take("w_raw", [P, 2, KT, P], F32)
    zone_wsplit = zw.end
    w_hi = zw.take("w_hi", [P, 2, KT, P], F32R)
    w_lo = zw.take("w_lo", [P, 2, KT, P], F32R)

    zone_s = zw.end
    zs = Zone(zone_s)
    stage = zs.take("stage", [P, 2, TP], F32)

    zone_x = zs.end
    z = Zone(zone_x)
    x_in = z.take("x_in", [P, NT, D], F32)
    x_t = z.take("x_t", [P, KT, TP], F32)
    vrows = z.take("vrows", [P, 2, P], F32)

    z = Zone(zone_x)
    iq_parts = z.take("iq_parts", [P, NH, TP], F32R)
    ik_hi = z.take("ik_hi", [P, NKEY], F32R)
    ik_lo = z.take("ik_lo", [P, NKEY], F32R)
    relu = z.take("relu", [P, 3, 512], F32)
    ikw_rows = z.take("ikw_rows", [P, NT, 72], F32)
    cache_ik = z.take("cache_ik", [P, 4, IDX], F32)
    relu_pool = z.take("relu_pool", [P, 2, 512], F32)

    z = Zone(zone_x)
    padded = z.take("padded", [P, TP + 4], F32)
    conv = z.take("conv", [P, TP], F32)
    conv_hi = z.take("conv_hi", [P, TP], F32R)
    conv_lo = z.take("conv_lo", [P, TP], F32R)
    gate_r = z.take("gate_r", [P, TP], F32)
    gate_i = z.take("gate_i", [P, TP], F32)
    decay_t = z.take("decay_t", [P, TP], F32)
    tanh_t = z.take("tanh_t", [P, TP], F32)
    mult = z.take("mult", [P, TP], F32)
    hidden = z.take("hidden", [P, TP], F32)
    silu_z = z.take("silu_z", [P, TP], F32)
    y_a = z.take("y_a", [P, TP], F32)
    gw_raw = z.take("gw_raw", [P, 2, P], F32)
    gw_hi = z.take("gw_hi", [P, 2, P], F32R)
    gw_lo = z.take("gw_lo", [P, 2, P], F32R)
    kv_rows = z.take("kv_rows", [P, 2, NT, P], F32)
    wg_raw = z.take("wg_raw", [P, KT, P], F32)

    zx = Zone(zone_x)
    k_hi = zx.take("k_hi", [P, NKV, NKEY], F32R)
    k_lo = zx.take("k_lo", [P, NKV, NKEY], F32R)
    v_hi = zx.take("v_hi", [P, 13, NKV * P], F32R)
    v_lo = zx.take("v_lo", [P, 13, NKV * P], F32R)
    zone_kv = zx.end
    z = Zone(zone_kv)
    k_raw = z.take("k_raw", [P, NKV, NKEY], F32)
    v_raw = at("v_raw", [P, 13, NKV * P], F32, zone_kv)
    z = Zone(max(z.end, zone_kv + nbytes([P, 13, 256], F32)))
    cache_k_rows = z.take("cache_k_rows", [P, 4, NKV * P], F32)
    z = Zone(zone_kv)
    q_raw = z.take("q_raw", [P, NH, P], F32)
    pt_lo = z.take("pt_lo", [P, 2, 512], F32R)
    q_hi = z.take("q_hi", [P, NH, P], F32R)
    q_lo = z.take("q_lo", [P, NH, P], F32R)
    diag_b = z.take("diag_b", [P, 4, P], F32)
    zone_bias = z.end
    bias = z.take("bias", [P, BIASES], BF16)
    z = Zone(zone_s)
    silu_zb = z.take("silu_zb", [P, NH, P], F32)
    y_b = z.take("y_b", [P, 512], F32)
    o_sq = z.take("o_sq", [P, 512], F32)
    z = Zone(zone_scores)
    probs_a = z.take("probs_a", [P, 4, D], F32)
    diag_a = z.take("diag_a", [P, 4, P], F32)
    probs_c = at("probs_c", [P, 8, 2 * P], F32, zone_scores)
    probs_b = at("probs_b", [P, 4, D], F32, zone_wsplit)
    z = Zone(zone_h)
    woa_hi = z.take("woa_hi", [P, KT, D], F32R)
    woa_lo = z.take("woa_lo", [P, KT, D], F32R)
    zone_pt = z.end
    pt_hi = z.take("pt_hi", [P, 2, 512], F32R)
    wo_raw = at("wo_raw", [P, 2, D], F32, zone_w)

    z = Zone(zone_x)
    wob_hi = z.take("wob_hi", [P, KT, D], F32R)
    wob_raw = at("wob_raw", [P, KT, D], F32, z.end)
    wob_lo = z.take("wob_lo", [P, KT, D], F32R)
    gf_rows = z.take("gf_rows", [P, D], F32)
    z = Zone(zone_bias + nbytes([P, bias_at(2)], BF16))
    acc = [z.take("acc0", [P, D], F32), z.take("acc1", [P, D], F32), at("acc2", [P, D], F32, zone_pt)]
    x_res = at("x_res", [P, 2, D], F32, zone_w)
    y_fin = at("y_fin", [P, 2, D], F32, zone_s)
    z = Zone(zone_wsplit)
    y_hi = z.take("y_hi", [P, 2, KT, P], F32R)
    y_lo = z.take("y_lo", [P, 2, KT, P], F32R)
    z = Zone(zone_scores)
    gate_rows = z.take("gate_rows", [P, 2, D], F32)
    y_raw = z.take("y_raw", [P, 2, KT, P], F32)

    ps = nc.alloc_psum_tensor("ps", [P, 8, 512], F32)

    q_s = nc.dram_tensor("q_scratch", [NH, P, TP], F32, kind="Internal").ap()
    k_s = nc.dram_tensor("k_scratch", [NKV, P, TP], F32, kind="Internal").ap()
    zb_s = nc.dram_tensor("zb_scratch", [NH, P, TP], F32, kind="Internal").ap()
    y_s = nc.dram_tensor("y_scratch", [2, KT, P, TP], F32, kind="Internal").ap()

    w_in = a["w_in"].rearrange("l (k p) n -> p (l k) n", p=P)
    w_mod = a["w_mod"].rearrange("l (p k) n -> p (l k) n", k=KT)
    w_out = a["w_out"].rearrange("l (k p) n -> (l k) p n", p=P)

    def f32(ap):
        return ap.bitcast(F32)

    def row_slice(ap, i):
        p, s = ap
        return p[i * P:(i + 1) * P] if i < NT - 1 else s

    x_rows = (a["x_prompt"].rearrange("b t d -> (b t) d"), a["x_sample"].rearrange("b t d -> (b t) d"))
    y_rows = (a["y_prompt"].rearrange("b t d -> (b t) d"), a["y_sample"].rearrange("b t d -> (b t) d"))

    vec_in = sem("vec_in")
    c_in = sem("c_in")
    x_in_s = [sem(f"x_in{i}") for i in range(NT)]
    wmod_in = [sem(f"wmod_in{i}") for i in range(MOD_CHUNKS)]
    w_landed = [sem(f"w_landed{i}") for i in range(2)]
    w_hi_done = sem("w_hi_done")
    w_lo_done = sem("w_lo_done")
    set_ready = sem("set_ready")
    set_read = sem("set_read")
    const_done = sem("const_done")
    const_zero = sem("const_zero")
    vec_t = sem("vec_t")
    vec_done = sem("vec_done")
    init_done = sem("init_done")
    silc_done = sem("silc_done")
    sq_done = sem("sq_done")
    rs_step = sem("rs_step")
    rs_sqrt = sem("rs_sqrt")
    x_diag = sem("x_diag")
    mod_chunk = sem("mod_chunk")
    mod_rows_done = sem("mod_rows_done")
    mod_acc_step = sem("mod_acc_step")
    xt_ready = sem("xt_ready")
    xt_read = sem("xt_read")
    mod_ready = sem("mod_ready")
    mod_step = sem("mod_step")
    h_full = sem("h_full")
    h_hi_done = sem("h_hi_done")
    h_lo_done = sem("h_lo_done")
    h_lo_pool = sem("h_lo_pool")
    soft_act = sem("soft_act")
    soft_step = sem("soft_step")
    cik_in = sem("cik_in")
    cik_t = sem("cik_t")
    ik_t = sem("ik_t")
    ik_read = sem("ik_read")
    ik_parts = sem("ik_parts")
    iq_done = sem("iq_done")
    iw_done = sem("iw_done")
    ik_out = sem("ik_out")
    index_ready = sem("index_ready")
    relu_done = sem("relu_done")
    index_added = sem("index_added")
    pool_added = sem("pool_added")
    masked = sem("masked")
    select = sem("select")
    staged = [sem(f"staged_out{i}") for i in range(2)]
    kv_t = sem("kv_t")
    kv_read = sem("kv_read")
    kv_out = [sem(f"kv_out{i}") for i in range(2)]
    conv_cols_done = sem("conv_cols_done")
    gate_cols_done = sem("gate_cols_done")
    wg_in = sem("wg_in")
    pad_edge = sem("pad_edge")
    tap0 = sem("tap0")
    taps = sem("taps")
    gw_in = sem("gw_in")
    gw_hi_done = sem("gw_hi_done")
    gw_lo_done = sem("gw_lo_done")
    conv_hi_done = sem("conv_hi_done")
    conv_lo_done = sem("conv_lo_done")
    gated_u = sem("gated_u")
    decays = sem("decays")
    mult_sq = sem("mult_sq")
    mult_done = sem("mult_done")
    lru = sem("lru")
    hsq_step = sem("hsq_step")
    ya_out = sem("ya_out")
    zb_scaled = sem("zb_scaled")
    lasts_ready = sem("lasts_ready")
    lasts_read = sem("lasts_read")
    lasts_out = sem("lasts_out")
    ssa_ready = sem("ssa_ready")
    ssa_read = sem("ssa_read")
    gate_ready = sem("gate_ready")
    gate_read = sem("gate_read")
    ck_in = sem("ck_in")
    k_in = sem("k_in")
    ck_t = sem("ck_t")
    ck_read = sem("ck_read")
    k_hi_done = sem("k_hi_done")
    k_lo_done = sem("k_lo_done")
    k_lo_dve = sem("k_lo_dve")
    v_in = sem("v_in")
    v_hi_done = sem("v_hi_done")
    v_lo_done = sem("v_lo_done")
    bias_done = sem("bias_done")
    q_in = [sem(f"q_in{i}") for i in range(2)]
    q_hi_done = sem("q_hi_done")
    q_lo_done = sem("q_lo_done")
    zb_in = [sem(f"zb_in{i}") for i in range(2)]
    qk_ready = sem("qk_ready")
    logits = sem("logits")
    max_neg = sem("max_neg")
    exp_done = sem("exp_done")
    inv_done = sem("inv_done")
    diag_ready = sem("diag_ready")
    turned = sem("turned")
    pt_hi_done = sem("pt_hi_done")
    pt_lo_done = sem("pt_lo_done")
    mixed = sem("mixed")
    o_sq_done = sem("o_sq_done")
    yb_done = sem("yb_done")
    yb_out = sem("yb_out")
    osum = sem("osum")
    ssb_ready = sem("ssb_ready")
    ssb_read = sem("ssb_read")
    wo_in = [sem(f"wo_in{i}") for i in range(2)]
    wob_in = [sem(f"wob_in{i}") for i in range(3)]
    wo_hi_done = sem("wo_hi_done")
    wo_lo_done = sem("wo_lo_done")
    wob_lo_done = sem("wob_lo_done")
    diag_done = sem("diag_done")
    grow_ready = sem("grow_ready")
    grow_read = sem("grow_read")
    gf_in = sem("gf_in")
    y_in = [sem(f"y_in{i}") for i in range(2)]
    y_hi_done = sem("y_hi_done")
    y_lo_done = sem("y_lo_done")
    xres_in = [sem(f"xres_in{i}") for i in range(2)]
    proj_ready = sem("proj_ready")
    a_scaled = sem("a_scaled")
    out_step = sem("out_step")
    fin_sq = sem("fin_sq")
    fin_done = sem("fin_done")
    y_out = [sem(f"y_out{i}") for i in range(2)]

    def split3(k, w_part_hi, w_part_lo, x_hi, x_lo, out, first, last):
        nc.tensor.matmul(out, w_part_hi, x_hi, start=first, stop=False)
        nc.tensor.matmul(out, w_part_hi, x_lo, start=False, stop=False)
        return nc.tensor.matmul(out, w_part_lo, x_hi, start=False, stop=last)

    block = nc.Block()
    with block:
        @block.sync
        def _(sp):
            def load_w(j, col, width=P):
                if not isinstance(j, int) or j >= 2:
                    sp.wait_ge(w_lo_done, j - 1)
                slot = load_w.slot
                load_w.slot = 1 - slot
                sp.dma_start(w_raw[:, slot, :, 0:width], w_in[:, :, bass.ds(col, width)]).then_inc(w_landed[slot], 16)
            load_w.slot = 0

            def rows(r0, n, ap, tile=0):
                sp.dma_start(vrows[r0:r0 + n, tile, :], ap).then_inc(vec_in, 16)

            sp.dma_start(craw[:, 0, :], a["c_prompt"].rearrange("b (p k) -> p (b k)", k=KT)).then_inc(c_in, 16)
            sp.dma_start(craw[:, 1, :], a["c_sample"].rearrange("b (p k) -> p (b k)", k=KT)).then_inc(c_in, 16)
            def load_mod(m):
                cols = slice(MOD_CH * m, MOD_CH * (m + 1))
                sp.dma_start(w_mod_raw[:, :, cols], w_mod[:, :, cols]).then_inc(wmod_in[m], 16)

            load_mod(0)
            load_mod(1)
            rows(V_SHIFT, 24, a["b_mod"].rearrange("l (r c) -> (l r) c", c=P))
            rows(V_GN, 8, a["g_norm"].rearrange("l (r c) -> (l r) c", c=P))
            rows(V_CW, 32, a["conv_w"].rearrange("l j (r c) -> (l j r) c", c=P))
            rows(V_CB, 8, a["conv_b"].rearrange("l (r c) -> (l r) c", c=P))
            rows(V_LAM, 8, a["lru_lambda"].rearrange("l (r c) -> (l r) c", c=P))
            rows(V_BR, 8, a["b_r"].rearrange("l h c -> (l h) c"))
            rows(V_BI, 8, a["b_i"].rearrange("l h c -> (l h) c"))
            rows(V_GA, 8, a["g_a"].rearrange("l (r c) -> (l r) c", c=P))
            rows(V_GB, 8, a["g_b"].rearrange("l (r c) -> (l r) c", c=P))
            rows(V_H0, 8, a["state_lru_h"].rearrange("l b (r c) -> (l b r) c", c=P))
            rows(0, 24, a["state_conv"].rearrange("l b j (r c) -> (l b j r) c", c=P), 1)
            for i in range(NT):
                n = tile_at(i)[1]
                sp.dma_start(x_in[0:n, i, :], row_slice(x_rows, i)).then_inc(x_in_s[i], 16)
                if i == 3:
                    load_mod(2)
            for m in range(3, MOD_CHUNKS):
                load_mod(m)
            load_w(0, IK, 72)
            for m in range(4):
                load_w(J_IQ + m, IQ + P * m)
                if m == 0:
                    sp.wait_ge(h_lo_done, KT - len(POOL_LOW))
                    sp.wait_ge(h_lo_pool, len(POOL_LOW))
                    sp.dma_start(cache_ik[:, :, :], a["cache_idx_k"].rearrange(
                        "l b (s p) d -> p (l b s) d", p=P)).then_inc(cik_in, 16)
            sp.wait_ge(ik_read, 2)
            sp.dma_start(a["ik_prompt"].rearrange("l b (s p) d -> p (l b s) d", p=P),
                         ikw_rows[:, 0:8, 0:IDX]).then_inc(ik_out, 16)
            sp.dma_start(a["ik_sample"].rearrange("l b t d -> (l b t) d"),
                         ikw_rows[0:T_SAMPLE, 8, 0:IDX]).then_inc(ik_out, 16)

            load_w(J_Q, QQ)
            load_w(J_Q + 1, QQ + P)

            def store_q(j, head, slot):
                sp.wait_ge(set_read, 3 * j + 3)
                sp.dma_start(q_s[bass.ds(head, 1)].rearrange("h p t -> (h p) t"), stage[:, slot, :]).then_inc(staged[slot], 16)

            with sp.Fori(0, 4) as i:
                for u in range(2):
                    load_w(i * 2 + (J_Q + 2 + u), i * (2 * P) + (QQ + P * (2 + u)))
                    store_q(i * 2 + (J_Q + u), i * 2 + u, (J_Q + u) % 2)
            kv_dst = []
            for n, which in ((0, "k"), (0, "v")):
                for g in range(NKV):
                    kv_dst.append((a[which + "_prompt"].rearrange("l b (s p) g d -> p (l b s) g d", p=P)[:, :, g, :],
                                   a[which + "_sample"].rearrange("l b t g d -> (l b t) g d")[:, g, :]))
            for m in range(4):
                j = J_K + m
                if m < 2:
                    load_w(j + 2, KK + P * (m + 2))
                    sp.wait_ge(set_read, 3 * j + 3)
                    sp.dma_start(k_s[m], stage[:, j % 2, :]).then_inc(staged[j % 2], 16)
                else:
                    load_w(j + 2, XA if m == 2 else ZA)
                if m >= 1:
                    sp.wait_ge(kv_read, 3 * m)
                    sp.dma_start(kv_dst[m - 1][0], kv_rows[:, (m - 1) % 2, 0:8, :]).then_inc(kv_out[(m - 1) % 2], 16)
                    sp.dma_start(kv_dst[m - 1][1], kv_rows[0:T_SAMPLE, (m - 1) % 2, 8, :]).then_inc(kv_out[(m - 1) % 2], 16)

            def load_gates(i):
                sp.dma_start(gw_raw[:, 0, :], a["w_r"][0, bass.ds(i, 1)].rearrange("h i j -> (h i) j")).then_inc(gw_in, 16)
                sp.dma_start(gw_raw[:, 1, :], a["w_i"][0, bass.ds(i, 1)].rearrange("h i j -> (h i) j")).then_inc(gw_in, 16)

            sp.wait_ge(index_added, DVE_UNITS)
            sp.wait_ge(pool_added, 2 * POOL_UNITS)
            sp.wait_ge(ik_out, 32)
            load_gates(0)
            sp.wait_ge(kv_read, 12)
            sp.dma_start(kv_dst[3][0], kv_rows[:, 1, 0:8, :]).then_inc(kv_out[1], 16)
            sp.dma_start(kv_dst[3][1], kv_rows[0:T_SAMPLE, 1, 8, :]).then_inc(kv_out[1], 16)

            def load_gate_block(i):
                if not isinstance(i, int) or i > 0:
                    sp.wait_ge(gate_ready, i)
                sp.dma_start(wg_raw[:, :, :], w_mod[:, :, bass.ds(i * P + 2 * D, P)]).then_inc(wg_in, 16)

            def store_ya(i):
                sp.wait_ge(lru, i * 7 + 8)
                sp.dma_start(y_s[0, bass.ds(i, 1)].rearrange("h p t -> (h p) t"), y_a[:, :]).then_inc(ya_out, 16)

            load_gate_block(0)
            load_w(J_LRU + 2, XA + P)
            load_w(J_LRU + 3, ZA + P)

            def lru_step(i, col_xa, col_za):
                load_w(i * 2 + (J_LRU + 4), col_xa)
                load_w(i * 2 + (J_LRU + 5), col_za)
                sp.wait_ge(gw_lo_done, i + 1)
                load_gates(i + 1)
                load_gate_block(i + 1)
                store_ya(i)

            with sp.Fori(0, 6) as i:
                lru_step(i, i * P + (XA + 2 * P), i * P + (ZA + 2 * P))
            lru_step(6, ZB, ZB + P)
            load_w(J_ZB + 2, ZB + 2 * P)
            load_w(J_ZB + 3, ZB + 3 * P)

            def store_zb(m):
                slot = (J_ZB + m) % 2
                sp.wait_ge(zb_scaled, m + 1)
                sp.dma_start(zb_s[m], stage[:, slot, :]).then_inc(staged[slot], 16)

            def load_keys():
                sp.wait_ge(v_lo_done, 2)
                for g in range(NKV):
                    sp.dma_start(k_raw[:, g, 0:T_PROMPT], k_s[g, :, 0:T_PROMPT]).then_inc(k_in, 16)
                    sp.dma_start(k_raw[:, g, T_PROMPT + PAST:], k_s[g, :, S0:]).then_inc(k_in, 16)

            def load_values():
                sp.wait_ge(ya_out, 129)
                sp.wait_ge(hsq_step, 17)
                sp.wait_ge(lru, 57)
                sp.wait_ge(gate_ready, KT)
                sp.wait_ge(kv_out[0], 64)
                sp.wait_ge(kv_out[1], 64)
                sp.dma_start(v_raw[:, 0:8, :], a["v_prompt"].rearrange(
                    "l b (s p) g d -> p (l b s) (g d)", p=P)).then_inc(v_in, 16)
                sp.dma_start(v_raw[:, 8:12, :], a["cache_v"].rearrange(
                    "l b (s p) g d -> p (l b s) (g d)", p=P)).then_inc(v_in, 16)
                sp.dma_start(v_raw[0:T_SAMPLE, 12, :], a["v_sample"].rearrange(
                    "l b t g d -> (l b t) (g d)")).then_inc(v_in, 16)
                sp.dma_start(cache_k_rows[:, :, :], a["cache_k"].rearrange(
                    "l b (s p) g d -> p (l b s) (g d)", p=P)).then_inc(ck_in, 16)

            load_w(J_ZB + 4, ZB + 4 * P)
            store_zb(0)
            store_ya(7)
            load_values()
            for m in range(1, 4):
                load_w(J_ZB + 4 + m, ZB + (4 + m) * P)
                store_zb(m)
            load_keys()
            for m in range(4, 6):
                store_zb(m)
            sp.wait_ge(lasts_read, 1)
            sp.dma_start(a["conv_prompt"].rearrange("l b j (r c) -> (l b j r) c", c=P), lasts_t[0:24, :]).then_inc(lasts_out, 16)
            sp.dma_start(a["conv_sample"].rearrange("l b j (r c) -> (l b j r) c", c=P), lasts_t[24:48, :]).then_inc(lasts_out, 16)
            sp.dma_start(a["h_prompt"].rearrange("l b (r c) -> (l b r) c", c=P), lasts_t[48:56, :]).then_inc(lasts_out, 16)
            sp.dma_start(a["h_sample"].rearrange("l b (r c) -> (l b r) c", c=P), lasts_t[56:64, :]).then_inc(lasts_out, 16)

            def load_wo(k):
                if k < 2:
                    sp.wait_ge(w_lo_done, J_END)
                elif k < KT + 2:
                    sp.wait_ge(wo_lo_done, k - 1)
                else:
                    sp.wait_ge(wob_lo_done, k - KT - 1)
                sp.dma_start(wo_raw[:, k % 2, :], w_out[k]).then_inc(wo_in[k % 2], 16)

            def load_q(p_):
                i, g = PASSES[p_]
                t0, rows_ = tile_at(i)
                if p_ == 0:
                    sp.wait_ge(k_lo_done, 1)
                    sp.wait_ge(k_lo_dve, 1)
                    for s in range(2):
                        sp.wait_ge(staged[s], 16 * 4)
                if p_ >= 2:
                    sp.wait_ge(q_lo_done, p_ - 1)
                heads = slice(GROUP * g, GROUP * (g + 1))
                sp.dma_start(q_raw[:, heads, 0:rows_],
                             q_s[heads, :, t0:t0 + rows_].rearrange("h p t -> p h t")).then_inc(q_in[g], 16)

            def load_zb(p_):
                i, g = PASSES[p_]
                t0, rows_ = tile_at(i)
                if p_ == 0:
                    for s in range(2):
                        sp.wait_ge(staged[s], 16 * 9)
                if p_ >= 2:
                    sp.wait_ge(yb_done, p_ - 1)
                heads = slice(GROUP * g, GROUP * (g + 1))
                sp.dma_start(silu_zb[:, heads, 0:rows_],
                             zb_s[heads, :, t0:t0 + rows_].rearrange("h p t -> p h t")).then_inc(zb_in[g], 16)

            def load_y(e):
                t, half = OUT_ORDER[e]
                t0, rows_ = tile_at(t)
                if e >= 2:
                    sp.wait_ge(y_lo_done, e - 1)
                sp.dma_start(y_raw[:, e % 2, :, 0:rows_], y_s[half, :, :, t0:t0 + rows_].rearrange("k p t -> p k t")).then_inc(y_in[e % 2], 16)

            load_q(0)
            load_q(1)
            for m in range(6, KT):
                store_zb(m)
            load_wo(0)
            load_wo(1)
            load_zb(0)
            load_zb(1)
            for p_, (i, g) in enumerate(PASSES):
                t0, rows_ = tile_at(i)
                if p_ + 2 < len(PASSES):
                    load_q(p_ + 2)
                if 0 <= p_ - WO_PASS < KT:
                    load_wo(p_ - WO_PASS + 2)
                sp.wait_ge(yb_done, p_ + 1)
                sp.dma_start(y_s[1, GROUP * g:GROUP * (g + 1), :, t0:t0 + rows_].rearrange("h p t -> p h t"),
                             y_b[:, 0:GROUP * rows_].rearrange("p (h t) -> p h t", h=GROUP)).then_inc(yb_out, 16)
                if p_ + 2 < len(PASSES):
                    load_zb(p_ + 2)
                if p_ == SMALL_PASS - 2:
                    sp.wait_ge(turned, TURNS_UPTO[p_])
                    load_y(0)
                    load_y(1)
                if p_ == SMALL_PASS:
                    load_y(2)
                if p_ == SMALL_PASS + 1:
                    load_y(3)

            def load_x(t):
                rows_ = tile_at(t)[1]
                if t >= 2:
                    sp.wait_ge(out_step, 3 * (t - 1))
                sp.dma_start(x_res[0:rows_, t % 2, :], row_slice(x_rows, t)).then_inc(xres_in[t % 2], 16)

            def store_y(t):
                rows_ = tile_at(t)[1]
                sp.wait_ge(fin_done, t + 1)
                sp.dma_start(row_slice(y_rows, t), y_fin[0:rows_, t % 2, :]).then_inc(y_out[t % 2], 16)

            def load_wob(k):
                sp.dma_start(wob_raw[:, k, :], w_out[KT + k]).then_inc(wob_in[k // 2 - 1], 16)

            sp.wait_ge(mixed, len(TURNS))
            sp.wait_ge(q_lo_done, len(PASSES))
            for k in range(2, 6):
                load_wob(k)
            sp.dma_start(gf_rows[:, :], a["g_final"].rearrange("(b d) -> b d", b=1).broadcast_to([P, D])).then_inc(gf_in, 16)
            load_wob(6)
            load_wob(7)
            sp.wait_ge(yb_out, 16 * len(PASSES))
            load_y(4)
            sp.wait_ge(wob_lo_done, 2)
            load_x(0)
            load_x(1)
            load_y(5)
            e = 6
            for t in range(NT):
                for _ in range(2):
                    if e < 2 * NT:
                        load_y(e)
                        e += 1
                if 2 <= t + 1 < NT:
                    load_x(t + 1)
                store_y(t)
            sp.wait_ge(ik_out, 32)
            sp.wait_ge(kv_out[0], 64)
            sp.wait_ge(kv_out[1], 64)
            sp.wait_ge(lasts_out, 64)
            sp.wait_ge(y_out[0], 16 * 5)
            sp.wait_ge(y_out[1], 16 * 4)

        @block.gpsimd
        def _(pool):
            pool.memset(ident[:, :], 0.0).then_inc(const_zero, 1)
            pool.wait_ge(const_zero, 1)
            pool.affine_select(out=ident[:, :], in_=ident[:, :], compare_op=ALU.not_equal, fill=1.0, base=0,
                               pattern=[[-1, P]], channel_multiplier=1).then_inc(const_done, 1)
            pool.memset(ones[:, :], 1.0).then_inc(const_done, 1)
            pool.memset(x_t[:, :, T_PROMPT:S0], 0.0).then_inc(const_done, 1)
            pool.memset(hsq[:, :], 0.0).then_inc(hsq_step, 1)

            def split_w(j, slot, width=P):
                pool.wait_ge(w_hi_done, j + 1)
                pool.tensor_tensor(w_lo[:, slot, :, 0:width], w_raw[:, slot, :, 0:width],
                                   f32(w_hi[:, slot, :, 0:width]), ALU.subtract).then_inc(w_lo_done, 1)

            split_w(0, 0, 72)
            split_w(1, 1)
            for k in POOL_LOW:
                pool.wait_ge(h_hi_done, k + 1)
                pool.tensor_tensor(h_lo[:, k, :], x_t[:, k, :], f32(h_hi[:, k, :]), ALU.subtract).then_inc(h_lo_pool, 1)
            for j in range(2, J_Q + 2):
                split_w(j, j % 2)
            pool.wait_ge(iw_done, 2)
            for u, (i, h, p_) in enumerate(INDEX_UNITS):
                if u == len(Q_STEPS) + 4:
                    split_w(J_Q + 2, J_Q % 2)
                if i not in POOL_TILES:
                    continue
                rows_ = tile_at(i)[1]
                off, n = pieces_of(i)[p_]
                v = units_before(u)
                out = scores[0:rows_, score_at(i) + off:score_at(i) + off + n]
                r = relu_pool[0:rows_, v % 2, 0:n]
                weights = iw[0:rows_, i, h:h + 1].broadcast_to([rows_, n])
                pool.wait_ge(relu_done, u + 1)
                if h == 0:
                    pool.tensor_tensor(out, r, weights, ALU.mult).then_inc(pool_added, 2)
                else:
                    pool.tensor_tensor(r, r, weights, ALU.mult).then_inc(pool_added, 1)
                    pool.wait_ge(pool_added, 2 * v + 1)
                    pool.tensor_tensor(out, out, r, ALU.add).then_inc(pool_added, 1)
            split_w(J_Q + 3, (J_Q + 1) % 2)
            with pool.Fori(1, 4) as i:
                for u in range(2):
                    split_w(i * 2 + (J_Q + 2 + u), (J_Q + u) % 2)
            for j in range(J_K + 2, J_LRU + 2):
                split_w(j, j % 2)

            def split_gates(i):
                pool.wait_ge(gw_hi_done, i + 1)
                pool.tensor_tensor(gw_lo[:, :, :], gw_raw[:, :, :], f32(gw_hi[:, :, :]), ALU.subtract).then_inc(gw_lo_done, 1)

            def split_conv(i):
                pool.wait_ge(conv_hi_done, i + 1)
                pool.tensor_tensor(conv_lo[:, :], conv[:, :], f32(conv_hi[:, :]), ALU.subtract).then_inc(conv_lo_done, 1)

            def gate_conv(i):
                pool.wait_ge(set_read, i * 12 + (3 * S_LRU + 15))
                pool.tensor_tensor(gate_i[:, :], gate_i[:, :], conv[:, :], ALU.mult).then_inc(gated_u, 1)

            def square_hidden(i):
                pool.wait_ge(lru, i * 7 + 6)
                pool.tensor_tensor(mult[:, :], hidden[:, :], hidden[:, :], ALU.mult).then_inc(hsq_step, 1)
                pool.wait_ge(hsq_step, i * 2 + 2)
                pool.tensor_tensor(hsq[:, :], hsq[:, :], mult[:, :], ALU.add).then_inc(hsq_step, 1)

            split_gates(0)
            split_w(J_LRU + 2, J_LRU % 2)
            split_conv(0)
            split_w(J_LRU + 3, (J_LRU + 1) % 2)
            split_w(J_LRU + 4, J_LRU % 2)
            with pool.Fori(0, 7) as i:
                gate_conv(i)
                split_gates(i + 1)
                split_w(i * 2 + (J_LRU + 5), (J_LRU + 1) % 2)
                split_conv(i + 1)
                square_hidden(i)
                split_w(i * 2 + (J_LRU + 6), J_LRU % 2)

            def scale_zb(m):
                slot = (J_ZB + m) % 2
                pool.wait_ge(set_read, 3 * (S_ZB + m) + 3 if m else 3 * (S_ZB - 2) + 3)
                pool.tensor_tensor(stage[:, slot, :], stage[:, slot, :],
                                   vec[:, V_GB + m:V_GB + m + 1].broadcast_to([P, TP]), ALU.mult).then_inc(zb_scaled, 1)

            def split_q(p_):
                i, g = PASSES[p_]
                rows_ = tile_at(i)[1]
                heads = slice(GROUP * g, GROUP * (g + 1))
                pool.wait_ge(q_hi_done, p_ + 1)
                pool.tensor_tensor(q_lo[:, heads, 0:rows_], q_raw[:, heads, 0:rows_], f32(q_hi[:, heads, 0:rows_]),
                                   ALU.subtract).then_inc(q_lo_done, 1)

            gate_conv(7)
            scale_zb(0)
            split_w(J_ZB + 3, (J_ZB + 3) % 2)
            square_hidden(7)
            for m in range(1, KT):
                scale_zb(m)
                if J_ZB + 3 + m < J_END:
                    split_w(J_ZB + 3 + m, (J_ZB + 3 + m) % 2)
                if m == 3:
                    pool.wait_ge(v_hi_done, 2)
                    pool.tensor_tensor(v_lo[:, 0:12, :], v_raw[:, 0:12, :], f32(v_hi[:, 0:12, :]),
                                       ALU.subtract).then_inc(v_lo_done, 1)
                    pool.tensor_tensor(v_lo[0:T_SAMPLE, 12, :], v_raw[0:T_SAMPLE, 12, :],
                                       f32(v_hi[0:T_SAMPLE, 12, :]), ALU.subtract).then_inc(v_lo_done, 1)
                if m == 5:
                    pool.wait_ge(k_hi_done, 1)
                    pool.tensor_tensor(k_lo[:, 0, :], k_raw[:, 0, :], f32(k_hi[:, 0, :]), ALU.subtract).then_inc(k_lo_done, 1)
                if m == 6:
                    split_q(0)

            def split_y(e):
                rows_ = tile_at(OUT_ORDER[e][0])[1]
                pool.wait_ge(y_hi_done, e + 1)
                pool.tensor_tensor(y_lo[:, e % 2, :, 0:rows_], y_raw[:, e % 2, :, 0:rows_],
                                   f32(y_hi[:, e % 2, :, 0:rows_]), ALU.subtract).then_inc(y_lo_done, 1)

            pool.wait_ge(ssa_ready, 1)
            pool.memset(hsq[:, :], 0.0).then_inc(osum, 1)
            for kind, n in attention_order():
                if kind == "head":
                    p_ = n // GROUP
                    if n % GROUP == GROUP - 1 and p_ + 1 < len(PASSES):
                        split_q(p_ + 1)
                    k = p_ - WO_PASS
                    if n % GROUP == GROUP - 1 and 0 <= k < KT:
                        pool.wait_ge(wo_hi_done, k + 1)
                        pool.tensor_tensor(woa_lo[:, k, :], wo_raw[:, k % 2, :], f32(woa_hi[:, k, :]),
                                           ALU.subtract).then_inc(wo_lo_done, 1)
                elif kind == "prep":
                    split_y(n)
                elif kind == "out":
                    t0, r = tile_at(PASSES[n][0])
                    pool.wait_ge(o_sq_done, n + 1)
                    pool.tensor_tensor(o_sq[:, 0:2 * r], o_sq[:, 0:2 * r], o_sq[:, 2 * r:4 * r], ALU.add).then_inc(osum, 1)
                    pool.wait_ge(osum, 3 * n + 2)
                    pool.tensor_tensor(o_sq[:, 0:r], o_sq[:, 0:r], o_sq[:, r:2 * r], ALU.add).then_inc(osum, 1)
                    pool.wait_ge(osum, 3 * n + 3)
                    pool.tensor_tensor(hsq[:, t0:t0 + r], hsq[:, t0:t0 + r], o_sq[:, 0:r], ALU.add).then_inc(osum, 1)
            for e in range(2 * INSIDE, 2 * NT):
                split_y(e)

        @block.scalar
        def _(act):
            act.wait_ge(c_in, 32)
            nc.scalar.activation(silc[:, :, :], craw[:, :, :].rearrange("p b k -> p k b"), ACT.Silu).then_inc(silc_done, 1)
            act.wait_ge(init_done, 1)

            def square_x(i):
                n = tile_at(i)[1]
                act.wait_ge(x_in_s[i], 16)
                if i >= 2:
                    act.wait_ge(sq_done, i - 1)
                nc.scalar.activation(stage[0:n, i % 2, 0:D], x_in[0:n, i, :], ACT.Square,
                                     accum_out=ssq[0:n, 0, i:i + 1]).then_inc(sq_done, 1)

            def root(n, rows_=P, cols=slice(0, NT)):
                act.wait_ge(rs_step, 6 * n + 1)
                nc.scalar.activation(norm_q[0:rows_, cols], norm_v[0:rows_, cols], ACT.Sqrt).then_inc(rs_sqrt, 1)

            def read_turned(i):
                t0, n = tile_at(i)
                act.wait_ge(xt_ready, i + 1)
                b = 2 * (i % 3)
                nc.scalar.activation(x_t[:, :, t0:t0 + n],
                                     ps[:, b:b + 2, :].rearrange("p b (k t) -> p (b k) t", t=P)[:, :, 0:n],
                                     ACT.Copy).then_inc(xt_read, 1)

            for i in EARLY_TILES:
                square_x(i)
            root(0, P, slice(0, len(EARLY_TILES)))
            square_x(4)
            for i in range(4):
                square_x(5 + i)
                read_turned(i)
            root(1, P, slice(len(EARLY_TILES), NT))
            act.wait_ge(vec_done, 1)
            nc.scalar.activation(soft[:, 0, :], vec[:, V_LAM:V_LAM + 8], ACT.Abs).then_inc(soft_act, 1)
            act.wait_ge(soft_act, 1)
            nc.scalar.activation(soft[:, 0, :], soft[:, 0, :], ACT.Exp, scale=-1.0).then_inc(soft_act, 1)
            for i in LATE_TILES:
                read_turned(i)

            def split_w(slot, loads, s_before=None, width=P):
                act.wait_ge(w_landed[slot], loads * 16)
                if s_before is not None:
                    act.wait_ge(set_ready, s_before)
                nc.scalar.activation(w_hi[:, slot, :, 0:width], w_raw[:, slot, :, 0:width], ACT.Copy).then_inc(w_hi_done, 1)

            split_w(0, 1, None, 72)
            split_w(1, 1)
            for k in range(KT):
                act.wait_ge(h_full, 2 * k + 2)
                nc.scalar.activation(h_hi[:, k, :], x_t[:, k, :], ACT.Copy).then_inc(h_hi_done, 1)

            def read_set(s, dst, func, m=P, bias=None):
                for c in range(NCH):
                    act.wait_ge(set_ready, s * 3 + (c + 1))
                    b = 3 * (read_set.parity) + c
                    d = dst[0:m, CH * c:CH * (c + 1)]
                    if bias is None:
                        x = nc.scalar.activation(d, ps[0:m, b, 0:CH], func)
                    else:
                        x = nc.scalar.activation(d, ps[0:m, b, 0:CH], func, bias=bias)
                    x.then_inc(set_read, 1)
                read_set.parity = 1 - read_set.parity
            read_set.parity = 0

            read_set(0, stage[:, 0, :], ACT.Copy, 72)
            split_w(0, 2, 3)
            act.wait_ge(ik_t, 1)
            nc.scalar.activation(ikw_rows[:, 0:5, :], ps[:, 7, 0:360].rearrange("p (t w) -> p t w", w=72),
                                 ACT.Copy).then_inc(ik_read, 1)
            act.wait_ge(ik_t, 2)
            nc.scalar.activation(ikw_rows[:, 5:8, :], ps[:, 7, 0:216].rearrange("p (t w) -> p t w", w=72), ACT.Copy)
            nc.scalar.activation(ikw_rows[0:T_SAMPLE, 8, :], ps[0:T_SAMPLE, 7, 216:288], ACT.Copy).then_inc(ik_read, 1)
            for m in range(4):
                j = J_IQ + m
                if m == 1:
                    act.wait_ge(ik_parts, 12)
                if m >= 2:
                    act.wait_ge(iq_done, 4 * (m - 1))
                read_set(j, stage[:, j % 2, :], ACT.Copy)
                split_w(j % 2, (j + 2) // 2 + 1, 3 * j + 3)
            for u, (i, h, p_) in enumerate(INDEX_UNITS):
                rows_ = tile_at(i)[1]
                n = pieces_of(i)[p_][1]
                act.wait_ge(index_ready, u + 1)
                v = units_before(u)
                if i in POOL_TILES:
                    dst = relu_pool[0:rows_, v % 2, 0:n]
                    if v >= 2:
                        act.wait_ge(pool_added, 2 * (v - 1))
                else:
                    dst = relu[0:rows_, v % 3, 0:n]
                    if v >= 3:
                        act.wait_ge(index_added, v - 2)
                nc.scalar.activation(dst, ps[0:rows_, 6 + u % 2, 0:n], ACT.Relu).then_inc(relu_done, 1)
                b, c, k = q_step_after(u) or (0, 0, 0)
                if k == KT - 1:
                    j = J_Q + b
                    act.wait_ge(set_ready, 3 * j + c + 1)
                    act.wait_ge(iq_done, 16)
                    nc.scalar.activation(stage[:, j % 2, CH * c:CH * (c + 1)], ps[:, 3 * (j % 2) + c, 0:CH],
                                         ACT.Copy).then_inc(set_read, 1)
                    if c == NCH - 1:
                        split_w(j % 2, (j + 2) // 2 + 1, 3 * j + 3)

            read_set.parity = J_Q % 2
            with act.Fori(1, 4) as i:
                for u in range(2):
                    slot = (J_Q + u) % 2
                    act.wait_ge(staged[slot], i * 16)
                    read_set(i * 2 + (J_Q + u), stage[:, slot, :], ACT.Copy)
                    split_w(slot, i + ((J_Q + 2 + u) // 2 + 1), i * 6 + (3 * (J_Q + u) + 3))

            def read_rows(m):
                slot = m % 2
                if m == 0:
                    act.wait_ge(ik_out, 32)
                    act.wait_ge(index_added, DVE_UNITS)
                    act.wait_ge(pool_added, 2 * POOL_UNITS)
                if m >= 2:
                    act.wait_ge(kv_out[slot], 32)
                act.wait_ge(kv_t, 3 * m + 1)
                nc.scalar.activation(kv_rows[:, slot, 0:4, :], ps[:, 6, :].rearrange("p (t w) -> p t w", w=P),
                                     ACT.Copy).then_inc(kv_read, 1)
                act.wait_ge(kv_t, 3 * m + 2)
                nc.scalar.activation(kv_rows[:, slot, 4:8, :], ps[:, 7, :].rearrange("p (t w) -> p t w", w=P),
                                     ACT.Copy).then_inc(kv_read, 1)
                act.wait_ge(kv_t, 3 * m + 3)
                nc.scalar.activation(kv_rows[0:T_SAMPLE, slot, 8, :], ps[0:T_SAMPLE, 6, 0:P], ACT.Copy).then_inc(kv_read, 1)

            for m in range(4):
                j = J_K + m
                if m < 2:
                    act.wait_ge(staged[j % 2], 64)
                else:
                    act.wait_ge(staged[j % 2], 80)
                    act.wait_ge(kv_t, 3 * (m - 1))
                read_set(j, stage[:, j % 2, :], ACT.Copy)
                split_w(j % 2, (j + 2) // 2 + 1, 3 * j + 3)
                if m >= 1:
                    read_rows(m - 1)
            read_rows(3)

            def take_cols(dst, i):
                return nc.scalar.activation(dst[:, :].unsqueeze(2), vec[:, :].rearrange(
                    "p (v b) -> p v b", b=KT)[:, :, bass.ds(i, 1)], ACT.Copy)

            def ccol(v):
                return conv_cols[:, v // 8:v // 8 + 1]

            def gcol(v):
                return gate_cols_now[:, v // 8:v // 8 + 1]

            def read_xa(i, s):
                take_cols(conv_cols, i).then_inc(conv_cols_done, 1)
                act.wait_ge(taps, i * 3 + 1)
                read_set(s, padded[:, 3:3 + TP], ACT.Copy)
                act.wait_ge(set_read, s * 3 + 3)
                act.wait_ge(conv_cols_done, i + 1)
                nc.scalar.activation(padded[:, S0:S0 + 3], conv_cols[:, V_SC // 8:V_SC // 8 + 3],
                                     ACT.Copy).then_inc(pad_edge, 1)

            def first_tap(i):
                act.wait_ge(gw_in, i * 32 + 32)
                nc.scalar.activation(gw_hi[:, :, :], gw_raw[:, :, :], ACT.Copy).then_inc(gw_hi_done, 1)
                act.wait_ge(pad_edge, i + 1)
                if not isinstance(i, int) or i > 0:
                    act.wait_ge(gated_u, i)
                nc.scalar.activation(conv[:, :], padded[:, 0:TP], ACT.Identity, bias=ccol(V_CB),
                                     scale=ccol(V_CW)).then_inc(tap0, 1)

            def round_conv(i):
                act.wait_ge(taps, i * 3 + 4)
                nc.scalar.activation(conv_hi[:, :], conv[:, :], ACT.Copy).then_inc(conv_hi_done, 1)

            read_set.parity = S_LRU % 2
            split_w(J_LRU % 2, (J_LRU + 2) // 2 + 1, S_LRU * 3 + 3)
            read_xa(0, S_LRU)
            first_tap(0)
            round_conv(0)

            def lru_step(i, last):
                s0 = i * SETS_PER_STEP + (S_LRU + 1)
                read_set.parity = (S_LRU + 1) % 2
                split_w((J_LRU + 1) % 2, i + ((J_LRU + 3) // 2 + 1), s0 * 3 + 3)
                take_cols(gate_cols_now, i).then_inc(gate_cols_done, 1)
                act.wait_ge(lru, i * 7 + 1)
                read_set(s0, silu_z[:, :], ACT.Silu)
                if last:
                    read_zb(0, s0 + 1)
                else:
                    read_xa(i + 1, s0 + 1)
                act.wait_ge(gate_cols_done, i + 1)
                read_set(s0 + 2, gate_r[:, :], ACT.Sigmoid, bias=gcol(V_BR))
                read_set(s0 + 3, gate_i[:, :], ACT.Sigmoid, bias=gcol(V_BI))
                split_w(J_LRU % 2, i + ((J_LRU + 4) // 2 + 1), s0 * 3 + 6)
                act.wait_ge(set_read, s0 * 3 + 9)
                nc.scalar.activation(tanh_t[:, :], gate_r[:, :], ACT.Tanh, scale=gcol(V_DECAY))
                nc.scalar.activation(decay_t[:, :], gate_r[:, :], ACT.Exp, scale=gcol(V_DECAY + 8)).then_inc(decays, 1)
                act.wait_ge(decays, i * 2 + 1)
                act.wait_ge(hsq_step, i * 2 + 1)
                nc.scalar.activation(mult[:, :], decay_t[:, :], ACT.Square).then_inc(decays, 1)
                if not last:
                    first_tap(i + 1)
                act.wait_ge(mult_sq, i + 1)
                nc.scalar.activation(mult[:, :], mult[:, :], ACT.Sqrt).then_inc(mult_done, 1)
                if not last:
                    round_conv(i + 1)

            def read_zb(m, s):
                slot = (J_ZB + m) % 2
                act.wait_ge(staged[slot], 16 * (m // 2) + 80)
                read_set(s, stage[:, slot, :], ACT.Silu)

            with act.Fori(0, 7) as i:
                lru_step(i, False)
            lru_step(7, True)

            def split_q(p_):
                i, g = PASSES[p_]
                rows_ = tile_at(i)[1]
                heads = slice(GROUP * g, GROUP * (g + 1))
                act.wait_ge(q_in[g], 16 * (p_ // 2 + 1))
                if p_ >= 2:
                    act.wait_ge(qk_ready, GROUP * (p_ - 1))
                nc.scalar.activation(q_hi[:, heads, 0:rows_], q_raw[:, heads, 0:rows_], ACT.Copy).then_inc(q_hi_done, 1)

            def probs_of(u):
                if u >= GROUP * SMALL_PASS:
                    return probs_c[:, u % 8, :]
                return probs_a[:, u % 8, :] if u % 8 < 4 else probs_b[:, u % 8 - 4, :]

            def exponentials(n):
                i, g = PASSES[n // GROUP]
                rows_, keys = tile_at(i)[1], keys_of(i)[1]
                w = probs_of(n)[0:rows_, 0:keys]
                act.wait_ge(max_neg, n + 1)
                nc.scalar.activation(w, w, ACT.Exp, bias=small[0:rows_, 1, n % 8:n % 8 + 1], scale=SM_SCALE,
                                     accum_out=small[0:rows_, 2, n % 8:n % 8 + 1]).then_inc(exp_done, 1)
                p_ = n // GROUP
                if n % GROUP == GROUP - 1 and p_ + 1 < len(PASSES):
                    split_q(p_ + 1)
                k = p_ - WO_PASS
                if n % GROUP == GROUP - 1 and 0 <= k < KT:
                    act.wait_ge(wo_in[k % 2], 16 * (k // 2 + 1))
                    nc.scalar.activation(woa_hi[:, k, :], wo_raw[:, k % 2, :], ACT.Copy).then_inc(wo_hi_done, 1)

            read_set.parity = (S_ZB + 1) % 2
            for m in range(1, KT - 1):
                if J_ZB + 2 + m < J_END:
                    split_w((J_ZB + m) % 2, (J_ZB + 2 + m) // 2 + 1, 3 * (S_ZB + m) + 3)
                read_zb(m, S_ZB + m)
                if m == 3:
                    act.wait_ge(v_in, 48)
                    nc.scalar.activation(v_hi[:, 0:12, :], v_raw[:, 0:12, :], ACT.Copy).then_inc(v_hi_done, 1)
                    nc.scalar.activation(v_hi[0:T_SAMPLE, 12, :], v_raw[0:T_SAMPLE, 12, :], ACT.Copy).then_inc(v_hi_done, 1)
                if m == 4:
                    act.wait_ge(ssa_ready, 1)
                    nc.scalar.activation(ssq[:, 1, 0:8], ps[:, 6, 0:16:2], ACT.Copy).then_inc(ssa_read, 1)
                    nc.scalar.activation(ssq[0:T_SAMPLE, 1, 8:9], ps[0:T_SAMPLE, 6, 16:17], ACT.Copy).then_inc(ssa_read, 1)
                    act.wait_ge(lasts_ready, 1)
                    nc.scalar.activation(lasts_t[:, :], ps[0:64, 7, 0:P], ACT.Copy).then_inc(lasts_read, 1)
                if m == 5:
                    act.wait_ge(k_in, 64)
                    for g in range(NKV):
                        act.wait_ge(ck_t, g + 1)
                        nc.scalar.activation(k_raw[:, g, T_PROMPT:T_PROMPT + PAST], ps[:, 6 + g, :], ACT.Copy).then_inc(ck_read, 1)
                    act.wait_ge(ck_read, 2)
                    nc.scalar.activation(k_hi[:, :, :], k_raw[:, :, :], ACT.Copy).then_inc(k_hi_done, 1)
                if m == 6:
                    split_q(0)
                    root(2)

            slot = (J_ZB + 7) % 2
            act.wait_ge(staged[slot], 16 * 3 + 80)
            for c in range(NCH):
                if c == NCH - 1:
                    for n in range(GROUP):
                        exponentials(n)
                act.wait_ge(set_ready, 3 * (S_ZB + 7) + c + 1)
                nc.scalar.activation(stage[:, slot, CH * c:CH * (c + 1)], ps[:, 3 * ((S_ZB + 7) % 2) + c, 0:CH],
                                     ACT.Silu).then_inc(set_read, 1)

            def split_y(e):
                rows_ = tile_at(OUT_ORDER[e][0])[1]
                act.wait_ge(y_in[e % 2], 16 * (e // 2 + 1))
                if e >= 2:
                    act.wait_ge(proj_ready, e - 1)
                else:
                    act.wait_ge(turned, TURNS_UPTO[SMALL_PASS - 1])
                nc.scalar.activation(y_hi[:, e % 2, :, 0:rows_], y_raw[:, e % 2, :, 0:rows_], ACT.Copy).then_inc(y_hi_done, 1)

            due = []
            for kind, n in attention_order():
                if kind == "head" and n >= GROUP:
                    for u in due:
                        exponentials(u)
                    due = [n]
                elif kind == "turn":
                    p_, t = TURNS[n]
                    if due and due[0] // GROUP == p_:
                        exponentials(due.pop())
                    i = PASSES[p_][0]
                    rows_, kr = tile_at(i)[1], key_tiles(i)[t][1]
                    act.wait_ge(turned, n + 1)
                    if n >= 2:
                        act.wait_ge(mixed, n - 1)
                    nc.scalar.activation(pt_hi[0:kr, n % 2, 0:GROUP * rows_], ps[0:kr, 4 + n % 2, 0:GROUP * rows_],
                                         ACT.Copy).then_inc(pt_hi_done, 1)
                    for u in due:
                        exponentials(u)
                    due = []
                elif kind == "prep":
                    split_y(n)
                elif kind == "out":
                    rows_ = tile_at(PASSES[n][0])[1]
                    act.wait_ge(mixed, TURNS_UPTO[n])
                    if n >= 1:
                        act.wait_ge(osum, 3 * n + 1)
                    nc.scalar.activation(o_sq[:, 0:GROUP * rows_], ps[:, 6 + n % 2, 0:GROUP * rows_], ACT.Square).then_inc(o_sq_done, 1)

            def split_wob(k):
                if k < KT + 2:
                    act.wait_ge(wo_in[k % 2], 16 * (k // 2 + 1))
                    src = wo_raw[:, k % 2, :]
                else:
                    act.wait_ge(wob_in[(k - KT) // 2 - 1], 32)
                    src = wob_raw[:, k - KT, :]
                nc.scalar.activation(wob_hi[:, k - KT, :], src, ACT.Copy).then_inc(wo_hi_done, 1)

            def read_gate_rows(b):
                act.wait_ge(grow_ready, b + 1)
                nc.scalar.activation(gate_rows[:, b, :].rearrange("p (c n) -> p c n", c=2), ps[:, 4 + 2 * b:6 + 2 * b, :],
                                     ACT.Copy).then_inc(grow_read, 1)

            act.wait_ge(pt_lo_done, len(TURNS))
            act.wait_ge(q_lo_done, len(PASSES))
            for k in range(KT, KT + 4):
                split_wob(k)
            root(3)
            read_gate_rows(0)
            for k in range(KT + 4, 2 * KT):
                split_wob(k)
                if k == KT + 5:
                    split_y(4)
            read_gate_rows(1)
            split_y(5)
            e = 6
            for t in range(NT):
                rows_ = tile_at(t)[1]
                act.wait_ge(out_step, 3 * t + 3)
                nc.scalar.activation(acc[t % 3][0:rows_, :], y_fin[0:rows_, t % 2, :], ACT.Square,
                                     accum_out=ssq[0:rows_, 0, t:t + 1]).then_inc(fin_sq, 1)
                root(4 + t, rows_, slice(t, t + 1))
                for _ in range(2):
                    if e < 2 * NT:
                        split_y(e)
                        e += 1

        @block.tensor
        def _(pe):
            pe.wait_ge(silc_done, 1)

            def mod_part(m):
                pe.wait_ge(wmod_in[m], 16)
                n = PE_CHUNKS.index(m)
                if n >= 2:
                    pe.wait_ge(mod_rows_done, n - 1)
                for k in range(KT):
                    x = nc.tensor.matmul(ps[0:2, 6 + n % 2, 0:MOD_CH], silc[:, k, :],
                                         w_mod_raw[:, k, MOD_CH * m:MOD_CH * (m + 1)],
                                         start=(k == 0), stop=(k == KT - 1))
                x.then_inc(mod_chunk, 1)

            def turn_x(i):
                n = tile_at(i)[1]
                pe.wait_ge(x_diag, i + 1)
                if i == 2:
                    pe.wait_ge(vec_done, 1)
                if i >= 3:
                    pe.wait_ge(xt_read, i - 2)
                for k in range(KT):
                    b = 2 * (i % 3) + k // 4
                    x = nc.tensor.matmul(ps[:, b, P * (k % 4):P * (k % 4) + n], x_in[0:n, i, P * k:P * (k + 1)],
                                         x_diags[0:n, i, 0:n], start=True, stop=True)
                x.then_inc(xt_ready, 1)

            mod_part(0)
            pe.wait_ge(const_done, 3)
            pe.wait_ge(vec_in, 16 * 11)
            nc.tensor.transpose(ps[:, 5, 0:120], vrows[0:120, 0, :], ident[0:120, 0:120])
            nc.tensor.transpose(ps[:, 5, 120:144], vrows[0:24, 1, :], ident[0:24, 0:24]).then_inc(vec_t, 1)
            mod_part(1)
            for i in EARLY_TILES:
                turn_x(i)
            mod_part(2)
            for i in LATE_TILES:
                turn_x(i)
            for m in PE_CHUNKS[3:]:
                mod_part(m)
            pe.wait_ge(xt_read, NT)
            pe.wait_ge(mod_acc_step, 2 * KT)
            dve_blocks = range(DVE_COLS.start // P, DVE_COLS.stop // P)
            for m in dve_blocks:
                for b in range(2):
                    cols = slice(P * m - DVE_COLS.start, P * (m + 1) - DVE_COLS.start)
                    nc.tensor.matmul(ps[:, 0, 2 * m + b:2 * m + b + 1], mod_acc[:, b, cols], ones[:, 0:1],
                                     start=True, stop=True)
            pe.wait_ge(mod_rows_done, len(PE_CHUNKS))
            for m in (m for m in range(16) if m not in dve_blocks):
                x = nc.tensor.transpose(ps[:, 0, 2 * m:2 * m + 2], mod_rows[0:2, P * m:P * (m + 1)], ident[0:2, 0:2])
            x.then_inc(mod_ready, 1)

            def project(j, s, slot, width=P, first=False):
                pe.wait_ge(w_lo_done, j + 1)
                for c in range(NCH):
                    if not first:
                        pe.wait_ge(set_read, s * 3 + (c + 1 - 6))
                    out = ps[0:width, 3 * project.parity + c, 0:CH]
                    for k in range(KT):
                        cols = slice(CH * c, CH * (c + 1))
                        x = split3(k, w_hi[:, slot, k, 0:width], w_lo[:, slot, k, 0:width],
                                   h_hi[:, k, cols], h_lo[:, k, cols], out, k == 0, k == KT - 1)
                    x.then_inc(set_ready, 1)
                project.parity = 1 - project.parity
            project.parity = 0

            pe.wait_ge(mod_step, 1)
            pe.wait_ge(w_lo_done, 2)
            for k in range(KT):
                if k in POOL_LOW:
                    pe.wait_ge(h_lo_pool, POOL_LOW.index(k) + 1)
                else:
                    pe.wait_ge(h_lo_done, k + 1 - sum(q < k for q in POOL_LOW))
                for j in range(2):
                    width = (72, P)[j]
                    for c in range(NCH):
                        cols = slice(CH * c, CH * (c + 1))
                        x = split3(k, w_hi[:, j, k, 0:width], w_lo[:, j, k, 0:width], h_hi[:, k, cols], h_lo[:, k, cols],
                                   ps[0:width, 3 * j + c, 0:CH], k == 0, k == KT - 1)
                        if k == KT - 1:
                            x.then_inc(set_ready, 1)
            pe.wait_ge(cik_in, 16)
            pe.wait_ge(mod_step, 1)
            for t in range(4):
                x = nc.tensor.transpose(ps[0:IDX, 6, P * t:P * (t + 1)], cache_ik[:, t, :], ident[:, :])
            x.then_inc(cik_t, 1)
            pe.wait_ge(set_read, 3)
            pe.wait_ge(vec_done, 1)
            for i in range(NT):
                t0, n = tile_at(i)
                if i == 5:
                    pe.wait_ge(ik_read, 1)
                c = 72 * (i if i < 5 else i - 5)
                x = nc.tensor.transpose(ps[0:n, 7, c:c + 72], stage[0:72, 0, t0:t0 + n], ident[0:72, 0:72])
                if i in (4, NT - 1):
                    x.then_inc(ik_t, 1)
            for m in range(1, 4):
                j = J_IQ + m
                project(j, j, j % 2)
            pe.wait_ge(ik_parts, 12)
            pe.wait_ge(ik_read, 2)
            for u, (i, h, p_) in enumerate(INDEX_UNITS):
                t0, rows_ = tile_at(i)
                off, n = pieces_of(i)[p_]
                k0 = keys_of(i)[0] + off
                pe.wait_ge(iq_done, 4 * (h // 2 + 1))
                if u >= 2:
                    pe.wait_ge(relu_done, u - 1)
                out = ps[0:rows_, 6 + u % 2, 0:n]
                nc.tensor.matmul(out, iq_parts[:, h, t0:t0 + rows_], ik_hi[:, k0:k0 + n], start=True, stop=False)
                nc.tensor.matmul(out, iq_parts[:, h, t0:t0 + rows_], ik_lo[:, k0:k0 + n], start=False,
                                 stop=True).then_inc(index_ready, 1)
                if q_step_after(u):
                    b, c, k = q_step_after(u)
                    j, cols = J_Q + b, slice(CH * c, CH * (c + 1))
                    if k == 0:
                        pe.wait_ge(w_lo_done, j + 1)
                        pe.wait_ge(set_read, 3 * j + c + 1 - 6)
                    x = split3(k, w_hi[:, j % 2, k, :], w_lo[:, j % 2, k, :], h_hi[:, k, cols], h_lo[:, k, cols],
                               ps[:, 3 * (j % 2) + c, 0:CH], k == 0, k == KT - 1)
                    if k == KT - 1:
                        x.then_inc(set_ready, 1)
            project.parity = J_Q % 2
            with pe.Fori(1, 4) as i:
                for u in range(2):
                    project(i * 2 + (J_Q + u), i * 2 + (J_Q + u), (J_Q + u) % 2)

            def turn_rows(m):
                slot = (J_K + m) % 2
                pe.wait_ge(set_read, 3 * (J_K + m) + 3)
                for part, tiles in enumerate((range(0, 4), range(4, 8), (8,))):
                    bank = (6, 7, 6)[part]
                    if part < 2:
                        if m >= 1:
                            pe.wait_ge(kv_read, 3 * m)
                        else:
                            pe.wait_ge(relu_done, len(INDEX_UNITS))
                    else:
                        pe.wait_ge(kv_read, 3 * m + 1)
                    for q, i in enumerate(tiles):
                        t0, n = tile_at(i)
                        x = nc.tensor.transpose(ps[0:n, bank, P * q:P * (q + 1)], stage[:, slot, t0:t0 + n], ident[:, :])
                    x.then_inc(kv_t, 1)

            for m in range(4):
                project(J_K + m, J_K + m, (J_K + m) % 2)
                if m >= 1:
                    turn_rows(m - 1)
            turn_rows(3)

            project.parity = S_LRU % 2
            project(J_LRU, S_LRU, J_LRU % 2)
            pe.wait_ge(kv_read, 12)

            def lru_step(i):
                s0 = i * SETS_PER_STEP + (S_LRU + 1)
                project.parity = (S_LRU + 1) % 2
                project(i * 2 + (J_LRU + 1), s0, (J_LRU + 1) % 2)
                project(i * 2 + (J_LRU + 2), s0 + 1, J_LRU % 2)
                pe.wait_ge(conv_lo_done, i + 1)
                pe.wait_ge(gw_lo_done, i + 1)
                for q in range(2):
                    for c in range(NCH):
                        pe.wait_ge(set_read, s0 * 3 + (3 * q + c + 1))
                        cols = slice(CH * c, CH * (c + 1))
                        split3(0, gw_hi[:, q, :], gw_lo[:, q, :], conv_hi[:, cols], conv_lo[:, cols],
                               ps[:, 3 * project.parity + c, 0:CH], True, True).then_inc(set_ready, 1)
                    project.parity = 1 - project.parity
                pe.wait_ge(wg_in, i * 16 + 16)
                for k in range(KT):
                    x = nc.tensor.matmul(ps[:, 7, bass.ds(i * 2, 2)], wg_raw[:, k, :], silc[:, k, :],
                                         start=(k == 0), stop=(k == KT - 1))
                x.then_inc(gate_ready, 1)

            with pe.Fori(0, 8) as i:
                lru_step(i)
            project.parity = (S_ZB + 1) % 2
            with pe.Fori(0, 2) as i:
                for u in range(2):
                    m = 1 + u
                    project(i * 2 + (J_ZB + m), i * 2 + (S_ZB + m), (J_ZB + m) % 2)

            pe.wait_ge(hsq_step, 17)
            for i in range(NT):
                t0, n = tile_at(i)
                x = nc.tensor.matmul(ps[0:n, 6, 2 * i:2 * i + 2], hsq[:, t0:t0 + n], ones[:, 0:2], start=True, stop=True)
            x.then_inc(ssa_ready, 1)
            pe.wait_ge(lru, 57)
            pe.wait_ge(gate_read, 1)
            nc.tensor.transpose(ps[0:64, 7, 0:P], lasts[:, :, :].rearrange("p v b -> p (v b)"), ident[:, :]).then_inc(lasts_ready, 1)
            project(J_ZB + 5, S_ZB + 5, (J_ZB + 5) % 2)
            pe.wait_ge(ck_in, 16)
            for g in range(NKV):
                pe.wait_ge(ssa_read if g == 0 else lasts_read, 2 if g == 0 else 1)
                for t in range(4):
                    x = nc.tensor.transpose(ps[:, 6 + g, P * t:P * (t + 1)], cache_k_rows[:, t, P * g:P * (g + 1)], ident[:, :])
                x.then_inc(ck_t, 1)
            project(J_ZB + 6, S_ZB + 6, (J_ZB + 6) % 2)
            def out_step_of(e, k):
                t, half = OUT_ORDER[e]
                rows_ = tile_at(t)[1]
                wh, wl = (woa_hi, woa_lo) if half == 0 else (wob_hi, wob_lo)
                b = 2 if e < INSIDE else 2 * ((e - INSIDE) % 4)
                for q in range(2):
                    cols = slice(512 * q, 512 * (q + 1))
                    x = split3(k, y_hi[:, e % 2, k, 0:rows_], y_lo[:, e % 2, k, 0:rows_], wh[:, k, cols], wl[:, k, cols],
                               ps[0:rows_, b + q, :], k == 0, k == KT - 1)
                return x

            def probs_of(u):
                if u >= GROUP * SMALL_PASS:
                    return probs_c[:, u % 8, :]
                return probs_a[:, u % 8, :] if u % 8 < 4 else probs_b[:, u % 8 - 4, :]

            def diag_of(u):
                return diag_a[:, u % 8, :] if u % 8 < 4 else diag_b[:, u % 8 - 4, :]

            def logits_of(n):
                p_ = n // GROUP
                i, g = PASSES[p_]
                rows_ = tile_at(i)[1]
                k0, keys = keys_of(i)
                h = n % 8
                if n % GROUP == 0:
                    pe.wait_ge(q_lo_done, p_ + 1)
                if n >= 2:
                    pe.wait_ge(logits, n - 1)
                for q in range((keys + 511) // 512):
                    off, w = 512 * q, min(512, keys - 512 * q)
                    cols = slice(k0 + off, k0 + off + w)
                    x = split3(0, q_hi[:, h, 0:rows_], q_lo[:, h, 0:rows_], k_hi[:, g, cols], k_lo[:, g, cols],
                               ps[0:rows_, logits_bank(n) + q, 0:w], True, True)
                x.then_inc(qk_ready, 1)

            pe.wait_ge(w_lo_done, J_ZB + 8)
            for c in range(NCH):
                pe.wait_ge(set_read, 3 * (S_ZB + 7) + c + 1 - 6)
                cols = slice(CH * c, CH * (c + 1))
                slot = (J_ZB + 7) % 2
                for k in range(KT):
                    x = split3(k, w_hi[:, slot, k, :], w_lo[:, slot, k, :], h_hi[:, k, cols], h_lo[:, k, cols],
                               ps[:, 3 * ((S_ZB + 7) % 2) + c, 0:CH], k == 0, k == KT - 1)
                x.then_inc(set_ready, 1)
                if c == 1:
                    pe.wait_ge(ck_read, 2)
                    pe.wait_ge(k_lo_done, 1)
                    pe.wait_ge(k_lo_dve, 1)
                    for n in range(GROUP):
                        logits_of(n)
            pe.wait_ge(set_read, 3 * (S_ZB + 7) + 3)
            for kind, n in attention_order():
                if kind == "head":
                    if n >= GROUP:
                        logits_of(n)
                elif kind == "turn":
                    p_, t = TURNS[n]
                    i = PASSES[p_][0]
                    rows_, kr = tile_at(i)[1], key_tiles(i)[t][1]
                    pe.wait_ge(diag_ready, GROUP * (p_ + 1))
                    if n >= 2:
                        pe.wait_ge(pt_lo_done, n - 1)
                    for h in range(GROUP):
                        u = GROUP * p_ + h
                        x = nc.tensor.matmul(ps[0:kr, 4 + n % 2, rows_ * h:rows_ * (h + 1)],
                                             probs_of(u)[0:rows_, P * t:P * t + kr], diag_of(u)[0:rows_, 0:rows_],
                                             start=True, stop=True)
                    x.then_inc(turned, 1)
                elif kind == "mix":
                    p_, t = TURNS[n]
                    i, g = PASSES[p_]
                    rows_ = tile_at(i)[1]
                    key, kr = key_tiles(i)[t]
                    if n == 0:
                        pe.wait_ge(v_lo_done, 2)
                        pe.wait_ge(logits, GROUP)
                    if t == 0 and p_ >= 2:
                        pe.wait_ge(yb_done, p_ - 1)
                    pe.wait_ge(pt_lo_done, n + 1)
                    kt, cols = key // P, slice(P * g, P * (g + 1))
                    split3(0, v_hi[0:kr, kt, cols], v_lo[0:kr, kt, cols], pt_hi[0:kr, n % 2, 0:GROUP * rows_],
                           pt_lo[0:kr, n % 2, 0:GROUP * rows_], ps[:, 6 + p_ % 2, 0:GROUP * rows_],
                           t == 0, t == len(key_tiles(i)) - 1).then_inc(mixed, 1)
                elif kind == "fill":
                    e, k = n // KT, n % KT
                    if k == 0:
                        pe.wait_ge(y_lo_done, e + 1)
                        if e == 0:
                            pe.wait_ge(logits, GROUP * SMALL_PASS)
                            pe.wait_ge(wo_lo_done, KT)
                        else:
                            pe.wait_ge(a_scaled, e)
                    x = out_step_of(e, k)
                    if k == KT - 1:
                        x.then_inc(proj_ready, 1)

            def project_out(e):
                for k in range(KT):
                    x = out_step_of(e, k)
                x.then_inc(proj_ready, 1)

            pe.wait_ge(y_lo_done, 3)
            pe.wait_ge(logits, GROUP * len(PASSES))
            project_out(2)
            pe.wait_ge(osum, 3 * len(PASSES) + 1)
            pe.wait_ge(yb_done, len(PASSES))
            for i in range(NT):
                t0, n = tile_at(i)
                x = nc.tensor.matmul(ps[0:n, 6, 2 * i:2 * i + 2], hsq[:, t0:t0 + n], ones[:, 0:2], start=True, stop=True)
            x.then_inc(ssb_ready, 1)

            def gate_as_rows(b):
                pe.wait_ge(diag_done, 8 * (b + 1))
                for k in range(KT):
                    x = nc.tensor.matmul(ps[:, 4 + 2 * b + k // 4, P * (k % 4):P * (k % 4 + 1)], ones[:, :],
                                         y_fin[:, b, P * k:P * (k + 1)], start=True, stop=True)
                x.then_inc(grow_ready, 1)

            gate_as_rows(0)
            pe.wait_ge(y_lo_done, 4)
            pe.wait_ge(a_scaled, 2)
            project_out(3)
            pe.wait_ge(ssb_read, 2)
            gate_as_rows(1)
            pe.wait_ge(wob_lo_done, KT)
            for e in range(4, 2 * NT):
                pe.wait_ge(y_lo_done, e + 1)
                if e < 6:
                    pe.wait_ge(grow_read, e - 3)
                else:
                    t, half = OUT_ORDER[e - 4]
                    if half == 0:
                        pe.wait_ge(a_scaled, t + 1)
                    else:
                        pe.wait_ge(out_step, 3 * t + 1)
                project_out(e)

        @block.vector
        def _(dve):
            V = nc.vector
            V.memset(ssq[:, :, :], 1.0).then_inc(init_done, 1)
            dve.wait_ge(vec_t, 1)
            V.tensor_copy(vec[:, 0:V_DECAY], ps[:, 5, 0:V_DECAY]).then_inc(vec_done, 1)
            dve.wait_ge(vec_done, 1)

            def inv_rms(n, src, dst, rows_=P, cols=slice(0, NT)):
                v, q, t = norm_v[0:rows_, cols], norm_q[0:rows_, cols], norm_t[0:rows_, cols]
                src, dst = src[0:rows_, cols], dst[0:rows_, cols]
                V.tensor_scalar(v, src, 1.0 / D, EPS, ALU.mult, ALU.add).then_inc(rs_step, 1)
                dve.wait_ge(rs_sqrt, n + 1)
                V.reciprocal(dst, q).then_inc(rs_step, 1)
                dve.wait_ge(rs_step, 6 * n + 2)
                V.tensor_tensor(t, dst, dst, ALU.mult).then_inc(rs_step, 1)
                dve.wait_ge(rs_step, 6 * n + 3)
                V.tensor_tensor(t, t, v, ALU.mult).then_inc(rs_step, 1)
                dve.wait_ge(rs_step, 6 * n + 4)
                V.tensor_scalar(t, t, -0.5, 1.5, ALU.mult, ALU.add).then_inc(rs_step, 1)
                dve.wait_ge(rs_step, 6 * n + 5)
                V.tensor_tensor(dst, dst, t, ALU.mult).then_inc(rs_step, 1)
                dve.wait_ge(rs_step, 6 * n + 6)


            def read_mod(m):
                n = PE_CHUNKS.index(m)
                dve.wait_ge(mod_chunk, n + 1)
                V.tensor_copy(mod_rows[0:2, MOD_CH * m:MOD_CH * (m + 1)], ps[0:2, 6 + n % 2, 0:MOD_CH]).then_inc(mod_rows_done, 1)

            def diag_x(i):
                V.tensor_scalar(x_diags[:, i, :], ident[:, :], rstd[:, 0, i:i + 1], None, ALU.mult).then_inc(x_diag, 1)

            dve.wait_ge(const_done, 3)
            read_mod(0)
            read_mod(1)
            dve.wait_ge(sq_done, len(EARLY_TILES))
            inv_rms(0, ssq[:, 0, :], rstd[:, 0, :], P, slice(0, len(EARLY_TILES)))
            for i in EARLY_TILES:
                diag_x(i)
            dve.wait_ge(sq_done, NT)
            inv_rms(1, ssq[:, 0, :], rstd[:, 0, :], P, slice(len(EARLY_TILES), NT))
            for i in LATE_TILES:
                diag_x(i)
            read_mod(2)
            dve.wait_ge(soft_act, 2)
            steps = [0]

            def soft_next(ins):
                steps[0] += 1
                ins.then_inc(soft_step, 1)
                dve.wait_ge(soft_step, steps[0])

            e_, s_, q_, p_ = (soft[:, n, :] for n in range(4))
            soft_next(V.tensor_scalar(s_, e_, 2.0, None, ALU.add))
            soft_next(V.reciprocal(s_, s_))
            soft_next(V.tensor_tensor(s_, s_, e_, ALU.mult))
            soft_next(V.tensor_tensor(q_, s_, s_, ALU.mult))
            soft_next(V.tensor_scalar(p_, q_, 1.0 / 15, None, ALU.mult))
            for d in (13, 11, 9, 7, 5, 3):
                soft_next(V.scalar_tensor_tensor(p_, p_, 1.0 / d, q_, ALU.add, ALU.mult))
            soft_next(V.scalar_tensor_tensor(p_, p_, 1.0, s_, ALU.add, ALU.mult))
            soft_next(V.tensor_scalar(q_, vec[:, V_LAM:V_LAM + 8], -1.0, 0.0, ALU.mult, ALU.max))
            soft_next(V.scalar_tensor_tensor(p_, p_, 2.0, q_, ALU.mult, ALU.add))
            soft_next(V.tensor_scalar(vec[:, V_DECAY:V_DECAY + 8], p_, 8.0, None, ALU.mult))
            soft_next(V.tensor_scalar(vec[:, V_DECAY + 8:V_DECAY + 16], p_, -8.0, None, ALU.mult))

            for m in DVE_CHUNKS:
                dve.wait_ge(wmod_in[m], 16)
            for k in range(KT):
                for b in range(2):
                    if k == 0:
                        x = V.tensor_scalar(mod_acc[:, b, :], w_mod_raw[:, k, DVE_COLS], silc[:, k, b:b + 1], None, ALU.mult)
                    else:
                        dve.wait_ge(mod_acc_step, 2 * k + b - 1)
                        x = V.scalar_tensor_tensor(mod_acc[:, b, :], w_mod_raw[:, k, DVE_COLS], silc[:, k, b:b + 1],
                                                   mod_acc[:, b, :], ALU.mult, ALU.add)
                    x.then_inc(mod_acc_step, 1)
            for m in PE_CHUNKS[3:]:
                read_mod(m)
            dve.wait_ge(mod_ready, 1)
            V.tensor_tensor(mod[:, :, :], ps[:, 0, 0:32].rearrange("p (m b) -> p m b", b=2),
                            vec[:, 0:16].unsqueeze(2).broadcast_to([P, 16, 2]), ALU.add).then_inc(mod_step, 1)
            dve.wait_ge(mod_step, 1)
            V.scalar_tensor_tensor(shiftscale[:, :, :], mod[:, 8:16, :], 1.0,
                                   vec[:, V_GN:V_GN + 8].unsqueeze(2).broadcast_to([P, 8, 2]),
                                   ALU.add, ALU.mult).then_inc(mod_step, 1)
            dve.wait_ge(mod_step, 2)
            dve.wait_ge(xt_read, NT)
            dve.wait_ge(const_done, 3)

            def h_low(k):
                dve.wait_ge(h_hi_done, k + 1)
                V.tensor_tensor(h_lo[:, k, :], x_t[:, k, :], f32(h_hi[:, k, :]), ALU.subtract).then_inc(h_lo_done, 1)

            for k in range(KT):
                for b, cols in ((0, slice(0, S0)), (1, slice(S0, TP))):
                    V.tensor_scalar(x_t[:, k, cols], x_t[:, k, cols], shiftscale[:, k, b:b + 1], mod[:, k, b:b + 1],
                                    ALU.mult, ALU.add).then_inc(h_full, 1)
                if k >= 1 and k - 1 not in POOL_LOW:
                    h_low(k - 1)
            h_low(KT - 1)

            dve.wait_ge(cik_t, 1)
            dve.wait_ge(set_read, 3)
            n_ik = 0
            for src, k0, n in ((stage[0:IDX, 0, 0:T_PROMPT], 0, T_PROMPT), (ps[0:IDX, 6, :], T_PROMPT, PAST),
                               (stage[0:IDX, 0, S0:TP], T_PROMPT + PAST, T_SAMPLE)):
                cols = slice(k0, k0 + n)
                V.tensor_copy(ik_hi[0:IDX, cols], src).then_inc(ik_parts, 1)
                V.tensor_copy(ik_hi[IDX:P, cols], src).then_inc(ik_parts, 1)
                dve.wait_ge(ik_parts, n_ik + 1)
                V.tensor_tensor(ik_lo[0:IDX, cols], src, f32(ik_hi[0:IDX, cols]), ALU.subtract).then_inc(ik_parts, 1)
                V.tensor_tensor(ik_lo[IDX:P, cols], src, f32(ik_hi[0:IDX, cols]), ALU.subtract).then_inc(ik_parts, 1)
                n_ik += 4
            dve.wait_ge(ik_read, 2)
            V.tensor_scalar(iw[:, 0:8, :], ikw_rows[:, 0:8, IDX:72], IW_SCALE, None, ALU.mult).then_inc(iw_done, 1)
            V.tensor_scalar(iw[0:T_SAMPLE, 8, :], ikw_rows[0:T_SAMPLE, 8, IDX:72], IW_SCALE, None, ALU.mult).then_inc(iw_done, 1)

            lower, upper = slice(0, IDX), slice(IDX, P)
            for m in range(4):
                j = J_IQ + m
                src = stage[:, j % 2, :]
                dve.wait_ge(set_read, 3 * j + 3)
                V.tensor_copy(iq_parts[lower, 2 * m, :], src[lower]).then_inc(iq_done, 1)
                V.tensor_copy(iq_parts[upper, 2 * m + 1, :], src[upper]).then_inc(iq_done, 1)
                dve.wait_ge(iq_done, 4 * m + 2)
                V.tensor_tensor(iq_parts[upper, 2 * m, :], src[lower], f32(iq_parts[lower, 2 * m, :]),
                                ALU.subtract).then_inc(iq_done, 1)
                V.tensor_tensor(iq_parts[lower, 2 * m + 1, :], src[upper], f32(iq_parts[upper, 2 * m + 1, :]),
                                ALU.subtract).then_inc(iq_done, 1)

            def mask(i):
                end = score_at(i) + P * (i + 1)
                V.memset(scores[0:CHUNK, end - CHUNK:end], NEG).then_inc(masked, 1)

            V.memset(soft[:, 3, 0:1], 0.0).then_inc(select, 1)
            dve.wait_ge(iw_done, 2)
            for u, (i, h, p_) in enumerate(INDEX_UNITS):
                rows_ = tile_at(i)[1]
                off, n = pieces_of(i)[p_]
                out = scores[0:rows_, score_at(i) + off:score_at(i) + off + n]
                if i in POOL_TILES:
                    continue
                v = units_before(u)
                dve.wait_ge(relu_done, u + 1)
                if h == 0:
                    x = V.tensor_scalar(out, relu[0:rows_, v % 3, 0:n], iw[0:rows_, i, h:h + 1], None, ALU.mult)
                else:
                    dve.wait_ge(index_added, v - len(pieces_of(i)) + 1)
                    x = V.scalar_tensor_tensor(out, relu[0:rows_, v % 3, 0:n], iw[0:rows_, i, h:h + 1], out,
                                               ALU.mult, ALU.add)
                x.then_inc(index_added, 1)
                v += 1 - FIRST_SELECTION
                if v == 0:
                    dve.wait_ge(index_added, FIRST_SELECTION)
                    for tile in FIRST_TILES:
                        mask(tile)
                    dve.wait_ge(masked, len(FIRST_TILES))
                if v > 0 and v % 3 == 0 and v // 3 <= 2 * len(FIRST_ROUNDS):
                    step = v // 3 - 1
                    tile = FIRST_ROUNDS[step // 2]
                    w = scores[:, score_at(tile):score_at(tile) + keys_of(tile)[1]]
                    b = best[:, tile - 2, :]
                    dve.wait_ge(select, step + 1)
                    if step % 2 == 0:
                        V.max(b, w).then_inc(select, 1)
                    else:
                        V.match_replace(w, b, w, TAKEN).then_inc(select, 1)
            dve.wait_ge(index_added, DVE_UNITS)
            dve.wait_ge(pool_added, 2 * POOL_UNITS)
            for i in ROUND_ONE_TILES:
                if i not in FIRST_TILES:
                    mask(i)
            dve.wait_ge(masked, len(ROUND_ONE_TILES))

            def select_round(tiles, before):
                w = {i: (scores[0:tile_at(i)[1], score_at(i):score_at(i) + keys_of(i)[1]],
                         best[0:tile_at(i)[1], min(i, 8) - 2, :]) for i in tiles}
                dve.wait_ge(select, before)
                V.memset(held, 0.0)
                for i in tiles:
                    V.max(w[i][1], w[i][0]).then_inc(select, 1)
                dve.wait_ge(select, before + len(tiles))
                V.memset(held, 0.0)
                for i in tiles:
                    V.match_replace(w[i][0], w[i][1], w[i][0], TAKEN).then_inc(select, 1)

            n_select = 1 + 2 * len(FIRST_ROUNDS)
            with dve.Fori(0, Q_ROUNDS) as i:
                select_round(INDEX_TILES, i * 14 + n_select)
            n_select += 14 * Q_ROUNDS

            V.memset(padded[:, 0:3], 0.0).then_inc(taps, 1)
            V.memset(soft[:, 1, 0:1], 0.0).then_inc(lru, 1)
            V.memset(soft[:, 2, 0:1], 0.0).then_inc(ya_out, 1)

            def col(v, i):
                return vec[:, bass.ds(i + v, 1)]

            def other_taps(i):
                dve.wait_ge(tap0, i + 1)
                V.tensor_copy(lasts[:, 0:3, bass.ds(i, 1)], padded[:, T_PROMPT:T_PROMPT + 3].unsqueeze(2))
                V.tensor_copy(lasts[:, 3:6, bass.ds(i, 1)], padded[:, TP:TP + 3].unsqueeze(2))
                for j in range(1, 4):
                    V.scalar_tensor_tensor(conv[:, :], padded[:, j:j + TP], col(V_CW + 8 * j, i), conv[:, :],
                                           ALU.mult, ALU.add).then_inc(taps, 1)
                    dve.wait_ge(taps, i * 3 + (j + 1))

            def lru_step(i, last):
                select_round(EARLY, i * PER_STEP + n_select)
                dve.wait_ge(decays, i * 2 + 2)
                V.scalar_tensor_tensor(mult[:, :], mult[:, :], 1.0, tanh_t[:, :], ALU.add, ALU.mult).then_inc(mult_sq, 1)
                if not last:
                    other_taps(i + 1)
                dve.wait_ge(mult_done, i + 1)
                V.memset(mult[:, 0:1], 1.0).then_inc(lru, 1)
                V.memset(decay_t[:, S0 - 1:S0], 0.0).then_inc(lru, 1)
                dve.wait_ge(gated_u, i + 1)
                dve.wait_ge(lru, i * 7 + 3)
                V.tensor_tensor(mult[:, :], mult[:, :], gate_i[:, :], ALU.mult).then_inc(lru, 1)
                dve.wait_ge(lru, i * 7 + 4)
                V.tensor_copy(mult[:, S0 - 1:S0], col(V_H0, i)).then_inc(lru, 1)
                dve.wait_ge(lru, i * 7 + 5)
                dve.wait_ge(hsq_step, i * 2 + 1)
                V.tensor_tensor_scan(hidden[:, :], decay_t[:, :], mult[:, :], 0.0, ALU.mult, ALU.add).then_inc(lru, 1)
                dve.wait_ge(lru, i * 7 + 6)
                V.tensor_copy(lasts[:, 6:8, bass.ds(i, 1)],
                              hidden[:, T_PROMPT - 1:TP:TP - T_PROMPT].unsqueeze(2)).then_inc(lru, 1)
                dve.wait_ge(ya_out, i * 16 + 1)
                V.scalar_tensor_tensor(y_a[:, :], hidden[:, :], col(V_GA, i), silu_z[:, :], ALU.mult, ALU.mult).then_inc(lru, 1)
                done = 2 * len(EARLY)
                for tiles in LATE:
                    select_round(tiles, i * PER_STEP + (n_select + done))
                    done += 2 * len(tiles)

            other_taps(0)
            for tiles in BEFORE_LRU:
                select_round(tiles, n_select)
                n_select += 2 * len(tiles)
            with dve.Fori(0, 7) as i:
                lru_step(i, False)
            lru_step(7, True)
            n_select += PER_STEP * KT
            dve.wait_ge(gate_ready, KT)
            V.tensor_tensor(gate_cols[:, :, :], ps[:, 7, 0:16].rearrange("p (m b) -> p m b", b=2),
                            vec[:, V_GATE:V_GATE + 8].unsqueeze(2).broadcast_to([P, 8, 2]), ALU.add).then_inc(gate_read, 1)
            with dve.Fori(0, SHARED_ROUNDS - Q_ROUNDS) as i:
                select_round((8,), i * 2 + n_select)
            n_select += 2 * (SHARED_ROUNDS - Q_ROUNDS)
            left = {i: TOPK_ROUNDS - Q_ROUNDS - FIRST_ROUNDS.count(i) - sum(i in tiles for tiles in BEFORE_LRU)
                    - KT * sum(i in tiles for tiles in (EARLY, *LATE)) for i in ROUND_ONE_TILES}
            def rounds_left(keep):
                n = n_select
                while max(left.values()) > keep:
                    tiles = tuple(i for i in ROUND_ONE_TILES if left[i])
                    rounds = min(min(left[i] for i in tiles), max(left.values()) - keep)
                    with dve.Fori(0, rounds) as i:
                        select_round(tiles, i * (2 * len(tiles)) + n)
                    n += 2 * len(tiles) * rounds
                    for i in tiles:
                        left[i] -= rounds
                return n

            n_select = rounds_left(LAST_ROUNDS)
            dve.wait_ge(k_hi_done, 1)
            V.tensor_tensor(k_lo[:, 1, :], k_raw[:, 1, :], f32(k_hi[:, 1, :]), ALU.subtract).then_inc(k_lo_dve, 1)
            n_select = rounds_left(0)

            dve.wait_ge(ssa_read, 2)
            inv_rms(2, ssq[:, 1, :], rstd[:, 1, :])

            dve.wait_ge(kv_out[0], 64)
            dve.wait_ge(kv_out[1], 64)
            dve.wait_ge(ya_out, 129)
            dve.wait_ge(select, n_select)
            n0 = bias_at(2)
            V.memset(bias[:, 0:n0], 0.0).then_inc(bias_done, 1)
            dve.wait_ge(bias_done, 1)
            for i in (0, 1):
                end = bias_at(i) + P * (i + 1)
                V.memset(bias[0:CHUNK, end - CHUNK:end], BIAS).then_inc(bias_done, 1)
            V.tensor_scalar(bias[:, n0:bias_at(8)], scores[:, 0:score_at(8)], TAKEN, BIAS,
                            ALU.not_equal, ALU.mult).then_inc(bias_done, 1)
            V.tensor_scalar(bias[0:T_SAMPLE, bias_at(8):], scores[0:T_SAMPLE, score_at(8):], TAKEN, BIAS,
                            ALU.not_equal, ALU.mult).then_inc(bias_done, 1)
            dve.wait_ge(bias_done, 5)
            def probs_of(u):
                if u >= GROUP * SMALL_PASS:
                    return probs_c[:, u % 8, :]
                return probs_a[:, u % 8, :] if u % 8 < 4 else probs_b[:, u % 8 - 4, :]

            def diag_of(u):
                return diag_a[:, u % 8, :] if u % 8 < 4 else diag_b[:, u % 8 - 4, :]

            def invert(u):
                r = tile_at(PASSES[u // GROUP][0])[1]
                dve.wait_ge(exp_done, u + 1)
                V.reciprocal(small[0:r, 3, u % 8:u % 8 + 1], small[0:r, 2, u % 8:u % 8 + 1]).then_inc(inv_done, 1)
                dve.wait_ge(inv_done, u + 1)
                V.tensor_scalar(diag_of(u)[0:r, 0:r], ident[0:r, 0:r], small[0:r, 3, u % 8:u % 8 + 1], None,
                                ALU.mult).then_inc(diag_ready, 1)

            def scale_first(t):
                e = OUT_ORDER.index((t, 0))
                r = slice(0, tile_at(t)[1])
                dve.wait_ge(proj_ready, e + 1)
                if t >= 3:
                    dve.wait_ge(fin_sq, t - 2)
                V.tensor_scalar(acc[t % 3][r, :], banks(e, r), rstd[r, 1, t:t + 1], None, ALU.mult).then_inc(a_scaled, 1)

            def banks(e, r):
                b = 2 if e < INSIDE else 2 * ((e - INSIDE) % 4)
                return ps[r, b:b + 2, :].rearrange("p b n -> p (b n)")

            waiting = []
            for kind, n in attention_order():
                if kind == "head":
                    p_ = n // GROUP
                    i, g = PASSES[p_]
                    rows_, keys = tile_at(i)[1], keys_of(i)[1]
                    dve.wait_ge(qk_ready, n + 1)
                    if n >= 8:
                        dve.wait_ge(turned, TURNS_UPTO[p_ - 2])
                    b = logits_bank(n)
                    src = ps[0:rows_, b:b + (keys + 511) // 512, :].rearrange("p b n -> p (b n)")[:, 0:keys]
                    c = n % 8
                    V.tensor_tensor_reduce(probs_of(n)[0:rows_, 0:keys], src, bias[0:rows_, bias_at(i):bias_at(i) + keys],
                                           1.0, NEG, ALU.add, ALU.max, small[0:rows_, 0, c:c + 1]).then_inc(logits, 1)
                    dve.wait_ge(logits, n + 1)
                    V.tensor_scalar(small[0:rows_, 1, c:c + 1], small[0:rows_, 0, c:c + 1], -SM_SCALE, None,
                                    ALU.mult).then_inc(max_neg, 1)
                    late = False
                    for u in waiting:
                        invert(u)
                    waiting = [n]
                elif kind == "turn":
                    p_, t = TURNS[n]
                    i = PASSES[p_][0]
                    rows_, kr = tile_at(i)[1], key_tiles(i)[t][1]
                    if n == 0 or waiting and (waiting[0] // GROUP == p_ or late):
                        for u in waiting:
                            invert(u)
                        waiting = []
                    late = True
                    dve.wait_ge(pt_hi_done, n + 1)
                    V.tensor_tensor(pt_lo[0:kr, n % 2, 0:GROUP * rows_], ps[0:kr, 4 + n % 2, 0:GROUP * rows_],
                                    f32(pt_hi[0:kr, n % 2, 0:GROUP * rows_]), ALU.subtract).then_inc(pt_lo_done, 1)
                elif kind == "out":
                    i, g = PASSES[n]
                    rows_ = tile_at(i)[1]
                    dve.wait_ge(o_sq_done, n + 1)
                    dve.wait_ge(zb_in[g], 16 * (n // 2 + 1))
                    if n >= 1:
                        dve.wait_ge(yb_out, 16 * n)
                    V.tensor_tensor(y_b[:, 0:GROUP * rows_].rearrange("p (h t) -> p h t", h=GROUP),
                                    ps[:, 6 + n % 2, 0:GROUP * rows_].rearrange("p (h t) -> p h t", h=GROUP),
                                    silu_zb[:, GROUP * g:GROUP * (g + 1), 0:rows_], ALU.mult).then_inc(yb_done, 1)
                elif kind == "take":
                    scale_first(OUT_ORDER[n][0])

            dve.wait_ge(yb_out, 16 * len(PASSES))
            dve.wait_ge(osum, 3 * len(PASSES) + 1)
            for b in range(2):
                for k in range(KT):
                    V.tensor_scalar(y_fin[:, b, P * k:P * (k + 1)], ident[:, :], gate_cols[:, k, b:b + 1], None,
                                    ALU.mult).then_inc(diag_done, 1)

            def split_wob(k):
                dve.wait_ge(wo_hi_done, KT + k + 1)
                src = wo_raw[:, k % 2, :] if k < 2 else wob_raw[:, k, :]
                V.tensor_tensor(wob_lo[:, k, :], src, f32(wob_hi[:, k, :]), ALU.subtract).then_inc(wob_lo_done, 1)

            for k in range(4):
                split_wob(k)
            scale_first(2)
            dve.wait_ge(ssb_ready, 1)
            V.tensor_copy(ssq[:, 2, 0:8], ps[:, 6, 0:16:2]).then_inc(ssb_read, 1)
            V.tensor_copy(ssq[0:T_SAMPLE, 2, 8:9], ps[0:T_SAMPLE, 6, 16:17]).then_inc(ssb_read, 1)
            dve.wait_ge(ssb_read, 2)
            inv_rms(3, ssq[:, 2, :], rstd[:, 2, :])
            for k in range(4, KT):
                split_wob(k)
            dve.wait_ge(gf_in, 16)
            dve.wait_ge(grow_read, 2)
            for t in range(NT):
                rows_ = tile_at(t)[1]
                r = slice(0, rows_)
                e = OUT_ORDER.index((t, 1))
                y, w = y_fin[r, t % 2, :], acc[t % 3][r, :]
                dve.wait_ge(proj_ready, e + 1)
                dve.wait_ge(a_scaled, t + 1)
                V.scalar_tensor_tensor(w, banks(e, r), rstd[r, 2, t:t + 1], w, ALU.mult, ALU.add).then_inc(out_step, 1)
                dve.wait_ge(out_step, 3 * t + 1)
                V.tensor_tensor(w, w, gate_rows[r, 0 if t < NT - 1 else 1, :], ALU.mult).then_inc(out_step, 1)
                dve.wait_ge(out_step, 3 * t + 2)
                dve.wait_ge(xres_in[t % 2], 16 * (t // 2 + 1))
                if t >= 2:
                    dve.wait_ge(y_out[t % 2], 16 * (t // 2))
                V.tensor_tensor(y, w, x_res[r, t % 2, :], ALU.add).then_inc(out_step, 1)
                dve.wait_ge(fin_sq, t + 1)
                inv_rms(4 + t, ssq[:, 0, :], rstd[:, 0, :], rows_, slice(t, t + 1))
                V.scalar_tensor_tensor(y, y, rstd[r, 0, t:t + 1], gf_rows[r, :], ALU.mult, ALU.mult).then_inc(fin_done, 1)
                if t + 3 < NT:
                    scale_first(t + 3)


def logits_bank(u):
    if u < GROUP:
        return 6 + u % 2
    return u % 2 if u >= GROUP * SMALL_PASS else 2 * (u % 2)


TURNS_UPTO = [sum(len(key_tiles(i)) for i, _ in PASSES[:p + 1]) for p in range(len(PASSES))]

_INS = ["x_prompt", "x_sample", "c_prompt", "c_sample", "cache_k", "cache_v", "cache_idx_k", "state_lru_h",
        "state_conv", "w_mod", "b_mod", "g_norm", "w_in", "conv_w", "conv_b", "w_r", "b_r", "w_i", "b_i",
        "lru_lambda", "g_a", "g_b", "w_out", "g_final"]
_OUTS = [("y_prompt", (1, T_PROMPT, D)), ("y_sample", (1, T_SAMPLE, D)),
         ("k_prompt", (1, 1, T_PROMPT, NKV, P)), ("v_prompt", (1, 1, T_PROMPT, NKV, P)),
         ("ik_prompt", (1, 1, T_PROMPT, IDX)), ("h_prompt", (1, 1, D)), ("conv_prompt", (1, 1, 3, D)),
         ("k_sample", (1, 1, T_SAMPLE, NKV, P)), ("v_sample", (1, 1, T_SAMPLE, NKV, P)),
         ("ik_sample", (1, 1, T_SAMPLE, IDX)), ("h_sample", (1, 1, D)), ("conv_sample", (1, 1, 3, D))]


def kernel(**inputs):
    import concourse.bacc as bacc
    from concourse.bass_utils import run_bass_kernel_spmd

    nc = bacc.Bacc("TRN2", target_bir_lowering=False, num_devices=1)
    arrays, aps = {}, {}
    for name in _INS:
        x = np.ascontiguousarray(inputs[name])
        arrays[f"in_{name}"] = x
        aps[name] = nc.dram_tensor(f"in_{name}", x.shape, mybir.dt.from_np(x.dtype), kind="ExternalInput").ap()
    for name, shape in _OUTS:
        aps[name] = nc.dram_tensor(f"out_{name}", shape, F32, kind="ExternalOutput").ap()
    build(nc, aps)
    r = run_bass_kernel_spmd(nc, [arrays], core_ids=[0])
    return tuple(r.results[0][f"out_{name}"] for name, _ in _OUTS)
```
